# Optimizing a Trainium2 kernel written in Bass

```python
import math
import jax, jax.numpy as jnp
from jax import lax
import numpy as np

D_MODEL = 1024
BATCH = 1
SEQ = 2048
DEPTH = 1

PLE_DIM = 256
RWKV_HEADS = 8
RWKV_HEAD_DIM = 64
RWKV_WIDTH = RWKV_HEADS * RWKV_HEAD_DIM
DECAY_LORA = 64
AAA_LORA = 64
MV_LORA = 32
GATE_LORA = 128
LNX_EPS = 64e-5
SWA_Q_HEADS = 8
SWA_KV_HEADS = 2
SWA_HEAD_DIM = 64
SWA_GROUP = SWA_Q_HEADS // SWA_KV_HEADS
SWA_WIDTH = SWA_Q_HEADS * SWA_HEAD_DIM
SWA_KV_WIDTH = SWA_KV_HEADS * SWA_HEAD_DIM
WINDOW = 128
BLOCK = 128
ATTN_SCALE = 1.0 / math.sqrt(SWA_HEAD_DIM)
REL_BUCKETS = 32
REL_MAX_DIST = 128
MIX_WIDTH = RWKV_WIDTH + SWA_WIDTH
D_FF = 4 * D_MODEL
NORM_EPS = 1e-6
RWKV_COLS = 3 * RWKV_WIDTH + DECAY_LORA + AAA_LORA + GATE_LORA
SWA_COLS = SWA_WIDTH + 2 * SWA_KV_WIDTH
IN_COLS = RWKV_COLS + SWA_COLS

kernel_name = "hymba_rwkv7_swa_sink_hybrid"

def rms_norm(x, g):
    xf = x.astype(jnp.float32)
    y = xf * lax.rsqrt(jnp.mean(xf * xf, axis=-1, keepdims=True) + NORM_EPS)
    return (y * g.astype(jnp.float32)).astype(x.dtype)

def token_shift(z, mu):
    prev = jnp.concatenate([jnp.zeros_like(z[:, :1]), z[:, :-1]], axis=1)
    return z + (prev - z) * mu

def t5_causal_bucket(dist):
    max_exact = REL_BUCKETS // 2
    n = jnp.maximum(dist, 0)
    nf = jnp.maximum(n, 1).astype(jnp.float32)
    large = max_exact + (jnp.log(nf / max_exact) / math.log(REL_MAX_DIST / max_exact)
                         * (REL_BUCKETS - max_exact)).astype(jnp.int32)
    large = jnp.minimum(large, REL_BUCKETS - 1)
    return jnp.where(n < max_exact, n, large)

def rwkv7_scan(r, decay, k, v, kk, a):
    def step(state, inp):
        r_t, w_t, k_t, v_t, kk_t, a_t = inp
        sa = jnp.einsum('bhvk,bhk->bhv', state, -kk_t)
        state = (state * w_t[:, :, None, :]
                 + sa[..., None] * (kk_t * a_t)[:, :, None, :]
                 + v_t[..., None] * k_t[:, :, None, :])
        y = jnp.einsum('bhvk,bhk->bhv', state, r_t)
        return state, y
    B, S, H, N = r.shape
    xs = tuple(jnp.swapaxes(t, 0, 1) for t in (r, decay, k, v, kk, a))
    s0 = jnp.zeros((B, H, N, N), jnp.float32)
    _, y = lax.scan(step, s0, xs)
    return jnp.swapaxes(y, 0, 1)

def swa_sink_attention(q, k, v, sinks, rel_bias):
    B, S = q.shape[0], q.shape[1]
    nb = S // BLOCK
    f32 = jnp.float32
    qb = q.astype(f32).reshape(B, nb, BLOCK, SWA_KV_HEADS, SWA_GROUP, SWA_HEAD_DIM)
    kb = k.astype(f32).reshape(B, nb, BLOCK, SWA_KV_HEADS, SWA_HEAD_DIM)
    vb = v.astype(f32).reshape(B, nb, BLOCK, SWA_KV_HEADS, SWA_HEAD_DIM)

    def with_prev(t):
        prev = jnp.concatenate([jnp.zeros_like(t[:, :1]), t[:, :-1]], axis=1)
        return jnp.concatenate([prev, t], axis=2)

    kw, vw = with_prev(kb), with_prev(vb)
    qi = jnp.arange(BLOCK)[:, None] + BLOCK
    ki = jnp.arange(2 * BLOCK)[None, :]
    dist = qi - ki
    blk = jnp.arange(nb)[:, None, None]
    valid = (dist >= 0) & (dist < WINDOW) & (blk * BLOCK + ki[None] - BLOCK >= 0)
    bias = rel_bias.astype(f32)[t5_causal_bucket(dist)]
    bias = jnp.transpose(bias, (2, 0, 1)).reshape(SWA_KV_HEADS, SWA_GROUP, BLOCK, 2 * BLOCK)
    logits = jnp.einsum('bnqhgd,bnkhd->bnhgqk', qb, kw) * ATTN_SCALE + bias
    logits = jnp.where(valid[None, :, None, None], logits, -jnp.inf)
    sink = sinks.astype(f32).reshape(SWA_KV_HEADS, SWA_GROUP)[None, None, :, :, None, None]
    m = jnp.maximum(jnp.max(logits, axis=-1, keepdims=True), sink)
    e = jnp.exp(logits - m)
    probs = e / (jnp.sum(e, axis=-1, keepdims=True) + jnp.exp(sink - m))
    out = jnp.einsum('bnhgqk,bnkhd->bnqhgd', probs, vw)
    return out.reshape(B, S, SWA_WIDTH).astype(q.dtype)

def setup_inputs(seed: int = 0) -> dict:
    key = jax.random.key(seed)
    ks = iter(jax.random.split(key, 40))
    f32 = jnp.float32

    def nrm(shape, scale):
        return jax.random.normal(next(ks), shape, f32) * scale

    def gain(shape):
        return 1.0 + nrm(shape, 0.05)

    L, Lm1 = DEPTH, DEPTH - 1
    return {
        "x": nrm((BATCH, SEQ, D_MODEL), 1.0),
        "p": nrm((DEPTH, BATCH, SEQ, PLE_DIM), 1.0),
        "norm_mix_g": gain((L, D_MODEL)),
        "w_in": nrm((L, D_MODEL, IN_COLS), D_MODEL ** -0.5),
        "mu_shift": jax.random.uniform(next(ks), (L, RWKV_COLS), f32),
        "w0": jax.random.uniform(next(ks), (L, RWKV_WIDTH), f32, -5.0, 0.0),
        "w_up": nrm((L, DECAY_LORA, RWKV_WIDTH), 0.1),
        "a0": nrm((L, RWKV_WIDTH), 0.1),
        "a_up": nrm((L, AAA_LORA, RWKV_WIDTH), 0.5 * AAA_LORA ** -0.5),
        "g_up": nrm((L, GATE_LORA, RWKV_WIDTH), GATE_LORA ** -0.5),
        "vres_down": nrm((Lm1, D_MODEL, MV_LORA), D_MODEL ** -0.5),
        "mu_vres": jax.random.uniform(next(ks), (Lm1, MV_LORA), f32),
        "v0": 1.0 + nrm((Lm1, RWKV_WIDTH), 0.1),
        "vres_up": nrm((Lm1, MV_LORA, RWKV_WIDTH), 0.5 * MV_LORA ** -0.5),
        "k_k": 0.85 + nrm((L, RWKV_WIDTH), 0.05),
        "k_a": 1.0 + nrm((L, RWKV_WIDTH), 0.05),
        "r_k": nrm((L, RWKV_HEADS, RWKV_HEAD_DIM), 0.1),
        "lnx_g": gain((L, RWKV_WIDTH)),
        "lnx_b": nrm((L, RWKV_WIDTH), 0.01),
        "sinks": nrm((L, SWA_Q_HEADS), 1.0),
        "rel_bias": nrm((REL_BUCKETS, SWA_Q_HEADS), 0.5),
        "w_out": nrm((L, MIX_WIDTH, D_MODEL), MIX_WIDTH ** -0.5),
        "norm_mlp_g": gain((L, D_MODEL)),
        "w_ff_up": nrm((L, D_MODEL, D_FF), D_MODEL ** -0.5),
        "w_ff_down": nrm((L, D_FF, D_MODEL), D_FF ** -0.5),
        "ple_proj": nrm((L, PLE_DIM, D_MODEL), PLE_DIM ** -0.5),
        "ple_norm_g": gain((L, D_MODEL)),
        "ple_gate": nrm((L, D_MODEL, D_MODEL), D_MODEL ** -0.5),
        "final_norm_g": gain((D_MODEL,)),
    }

def reference(x, p, norm_mix_g, w_in, mu_shift, w0, w_up, a0, a_up, g_up,
              vres_down, mu_vres, v0, vres_up, k_k, k_a, r_k, lnx_g, lnx_b,
              sinks, rel_bias, w_out, norm_mlp_g, w_ff_up, w_ff_down,
              ple_proj, ple_norm_g, ple_gate, final_norm_g):
    f32 = jnp.float32
    B, S = x.shape[0], x.shape[1]
    H, N = RWKV_HEADS, RWKV_HEAD_DIM
    v_first = None
    for i in range(DEPTH):
        h = rms_norm(x, norm_mix_g[i])
        w_cols = w_in[i]
        if i > 0:
            w_cols = jnp.concatenate([w_cols, vres_down[i - 1]], axis=1)
        z = h @ w_cols

        zs = token_shift(z[..., :RWKV_COLS].astype(f32), mu_shift[i].astype(f32))
        o = np.cumsum([RWKV_WIDTH, RWKV_WIDTH, RWKV_WIDTH, DECAY_LORA, AAA_LORA])
        r, k, v = zs[..., :o[0]], zs[..., o[0]:o[1]], zs[..., o[1]:o[2]]
        xw, xa, xg = zs[..., o[2]:o[3]], zs[..., o[3]:o[4]], zs[..., o[4]:]
        w = -jax.nn.softplus(-(w0[i].astype(f32) + jnp.tanh(xw) @ w_up[i].astype(f32))) - 0.5
        decay = jnp.exp(-jnp.exp(w))
        if i == 0:
            v_first = v
        else:
            zv = token_shift(z[..., IN_COLS:].astype(f32), mu_vres[i - 1].astype(f32))
            v = v + (v_first - v) * jax.nn.sigmoid(v0[i - 1].astype(f32) + zv @ vres_up[i - 1].astype(f32))
        a = jax.nn.sigmoid(a0[i].astype(f32) + xa @ a_up[i].astype(f32))
        g = jax.nn.sigmoid(xg) @ g_up[i].astype(f32)
        kk = (k * k_k[i].astype(f32)).reshape(B, S, H, N)
        kk = kk / jnp.maximum(jnp.linalg.norm(kk, axis=-1, keepdims=True), 1e-12)
        k = k * (1.0 + (a - 1.0) * k_a[i].astype(f32))
        rh, kh, vh = r.reshape(B, S, H, N), k.reshape(B, S, H, N), v.reshape(B, S, H, N)
        y = rwkv7_scan(rh, decay.reshape(B, S, H, N), kh, vh, kk, a.reshape(B, S, H, N))
        ym = jnp.mean(y, axis=-1, keepdims=True)
        yv = jnp.mean(jnp.square(y - ym), axis=-1, keepdims=True)
        y = ((y - ym) * lax.rsqrt(yv + LNX_EPS)).reshape(B, S, RWKV_WIDTH)
        y = (y * lnx_g[i].astype(f32) + lnx_b[i].astype(f32)).reshape(B, S, H, N)
        y = y + jnp.sum(rh * kh * r_k[i].astype(f32), axis=-1, keepdims=True) * vh
        rwkv_out = (y.reshape(B, S, RWKV_WIDTH) * g).astype(x.dtype)

        zq = z[..., RWKV_COLS:RWKV_COLS + SWA_WIDTH].reshape(B, S, SWA_Q_HEADS, SWA_HEAD_DIM)
        zk = z[..., RWKV_COLS + SWA_WIDTH:RWKV_COLS + SWA_WIDTH + SWA_KV_WIDTH].reshape(B, S, SWA_KV_HEADS, SWA_HEAD_DIM)
        zvv = z[..., RWKV_COLS + SWA_WIDTH + SWA_KV_WIDTH:IN_COLS].reshape(B, S, SWA_KV_HEADS, SWA_HEAD_DIM)
        swa_out = swa_sink_attention(zq, zk, zvv, sinks[i], rel_bias)

        x = x + jnp.concatenate([rwkv_out, swa_out], axis=-1) @ w_out[i]

        u = rms_norm(x, norm_mlp_g[i])
        x = x + jnp.square(jax.nn.relu(u @ w_ff_up[i])) @ w_ff_down[i]

        e = rms_norm(p[i] @ ple_proj[i], ple_norm_g[i])
        x = x + e * jax.nn.sigmoid(x @ ple_gate[i])
    return rms_norm(x, final_norm_g)


_drawn_inputs = setup_inputs


def setup_inputs(seed=0):
    import zlib

    import numpy as np

    out = dict(_drawn_inputs(seed))
    spreads = {}
    factors = {'w_up': 3.183,
     'a0': 3.799,
     'k_k': 14.715,
     'k_a': 2.73,
     'lnx_g': 3.455,
     'lnx_b': 30.276,
     'sinks': 8.0,
     'ple_norm_g': 3.36,
     'rel_bias': 3.228}
    for name, (base, spread) in spreads.items():
        noise = np.random.default_rng([zlib.crc32(name.encode()), seed]).standard_normal(out[name].shape)
        drawn = base * np.exp(spread * noise) if base else spread * noise
        out[name] = __import__('jax').numpy.asarray(drawn.astype(out[name].dtype))
    for name, factor in factors.items():
        out[name] = (out[name] * factor).astype(out[name].dtype)
    return out
```

```python
from contextlib import ExitStack

import numpy as np

import concourse.bass as bass
from concourse import mybir

F32 = mybir.dt.float32
F32R = mybir.dt.float32r
ALU = mybir.AluOpType
ACT = mybir.ActivationFunctionType
AX = mybir.AxisListType

P = 128
SEQ, D, PLE, FF = 2048, 1024, 256, 4096
DK = D // P
TILES = SEQ // P
HEADS, HD = 8, 64
RW = HEADS * HD
PAIRS = RW // P
RWT = 14
ZT = 20
CH = 64
BUCKETS = 32
PADC = P
DECAY = float(np.exp(-0.5))
NEG = -1e30
NORM_EPS, LNX_EPS = 1e-6, 64e-5
EXT = 3 * P

PV = {}
_at = 0
for _n, _w in (("norm_mix_g", DK), ("norm_mlp_g", DK), ("mu", RWT), ("w0", PAIRS), ("a0", PAIRS),
               ("k_k", PAIRS), ("k_a", PAIRS), ("r_k", PAIRS)):
    PV[_n] = (_at, _at + _w)
    _at += _w
NPV = _at

LEVELS = 6
CC = {}
_at = 0
for _n, _w in (("ident", P), ("score_mask", 4 * P), ("level_mask", LEVELS * P), ("first_mask_t", P),
               ("chunk_start", PAIRS * P), ("head_of", PAIRS * HEADS), ("pair_sel", 2)):
    CC[_n] = (_at, _at + _w)
    _at += _w
NCC = _at


def shape_constants():
    c = np.zeros((P, NCC), np.float32)
    r, t = np.arange(P)[:, None], np.arange(P)[None, :]
    c[:, CC["ident"][0]:CC["ident"][1]] = r == t
    same = r // CH == t // CH
    strict, incl = same & (r < t), same & (r <= t)
    c[:, CC["score_mask"][0]:CC["score_mask"][1]] = np.concatenate([strict, incl, strict, incl], 1)
    lv = []
    for l in range(LEVELS):
        b = 1 << l
        lv.append((r // (2 * b) == t // (2 * b)) & ((r // b) % 2 == 1) & ((t // b) % 2 == 0))
    c[:, CC["level_mask"][0]:CC["level_mask"][1]] = np.concatenate(lv, 1)
    c[:, CC["first_mask_t"][0]:CC["first_mask_t"][1]] = lv[0].T
    c[:, CC["chunk_start"][0]:CC["chunk_start"][1]] = np.tile(np.arange(P) % CH != 0, PAIRS)[None]
    ho = np.zeros((P, PAIRS, HEADS), np.float32)
    for f in range(PAIRS):
        for h in range(2):
            ho[h * HD:(h + 1) * HD, f, 2 * f + h] = 1
    c[:, CC["head_of"][0]:CC["head_of"][1]] = ho.reshape(P, -1)
    c[:, CC["pair_sel"][0]:CC["pair_sel"][1]] = ho[:, 0, 0:2]
    return c


def head_rows():
    return np.repeat(np.eye(HEADS, dtype=np.float32), HD, axis=1)


def bucket_onehot():
    o = np.zeros((BUCKETS + 1, EXT), np.float32)
    for m in range(EXT):
        d = 2 * P - 1 - m
        if not 0 <= d < P:
            o[BUCKETS, m] = NEG
            continue
        half = BUCKETS // 2
        if d < half:
            b = d
        else:
            b = half + int(np.float32(np.log(np.float32(d) / np.float32(half))) / np.float32(np.log(P / half))
                           * np.float32(BUCKETS - half))
        o[min(b, BUCKETS - 1), m] = 1
    return o


def norm_and_project(nc, x, w_in, params, consts, zT):
    FC = 2
    CHUNKS = ZT // FC
    TB = 512
    NTB = SEQ // TB
    with ExitStack() as ctx:
        sb = lambda n, s, d=F32: ctx.enter_context(nc.sbuf_tensor(n, s, d))
        sem = lambda n: ctx.enter_context(nc.semaphore(n))
        hT_hi = sb("hT_hi", [P, DK, SEQ], F32R)
        hT_lo = sb("hT_lo", [P, DK, SEQ], F32R)
        par = sb("par_a", [P, NPV])
        ident = sb("ident_a", [P, P])
        ps = ctx.enter_context(nc.psum_tensor("ps_a", [P, 8, 512], F32))
        g = par[:, PV["norm_mix_g"][0]:PV["norm_mix_g"][1]]

        with ExitStack() as inner:
            sbi = lambda n, s, d=F32: inner.enter_context(nc.sbuf_tensor(n, s, d))
            xt = sbi("xt_a", [P, 2, D])
            junk = sbi("junk_a", [P, D])
            xn = sbi("xn_a", [P, 2, D])
            xg = sbi("xg_a", [P, 2, DK, P])
            ss = sbi("ss_a", [P, 2, 1])
            rs = sbi("rs_a", [P, 2, 1])
            eps = sbi("eps_a", [P, 1])
            const_in, x_in0, x_in1 = sem("const_in_a"), sem("x_in0_a"), sem("x_in1_a")
            x_in = [x_in0, x_in1]
            sumsq_done, rms_done, rstd_done = sem("sumsq_a"), sem("rms_a"), sem("rstd_a")
            xn_done, transposed, scaled, hi_done, lo_done = (
                sem("xn_a"), sem("tr_a"), sem("scaled_a"), sem("hi_a"), sem("lo_a"))
            eps_done = sem("eps_done_a")
            with nc.Block() as block:
                @block.sync
                def _(sp):
                    sp.dma_start(par[:, :], params).then_inc(const_in, 16)
                    sp.dma_start(ident[:, :], consts[:, CC["ident"][0]:CC["ident"][1]]).then_inc(const_in, 16)
                    with sp.Fori(0, TILES // 2) as it:
                        for s in range(2):
                            sp.wait_ge(xn_done, 2 * it + s + 1)
                            sp.dma_start(xt[:, s, :], x[bass.ds(it * (2 * P) + s * P, P), :]).then_inc(x_in[s], 16)

                @block.scalar
                def _(act):
                    act.wait_ge(eps_done, 1)
                    with act.Fori(0, TILES // 2) as it:
                        for s in range(2):
                            act.wait_ge(x_in[s], 16 * (it + 1))
                            act.wait_ge(rstd_done, 2 * it + s + 1)
                            nc.scalar.activation(junk[:, :], xt[:, s, :], ACT.Square,
                                                 accum_out=ss[:, s, :]).then_inc(sumsq_done, 1)
                            act.wait_ge(sumsq_done, 2 * it + s + 1)
                            nc.scalar.activation(rs[:, s, :], ss[:, s, :], ACT.Sqrt, scale=1.0 / D,
                                                 bias=eps[:, 0:1]).then_inc(rms_done, 1)
                            act.wait_ge(scaled, 2 * it + s + 3)
                            nc.scalar.activation(hT_hi[:, :, bass.ds(it * (2 * P) + s * P, P)], xg[:, s, :, :],
                                                 ACT.Copy).then_inc(hi_done, 1)

                @block.vector
                def _(dve):
                    nc.vector.memset(eps[:, :], NORM_EPS).then_inc(eps_done, 1)
                    for free in (xn_done, scaled, rstd_done):
                        dve.sem_inc(free, 2)
                    dve.wait_ge(const_in, 32)
                    with dve.Fori(0, TILES // 2) as it:
                        for s in range(2):
                            n = 2 * it + s
                            dve.wait_ge(rms_done, n + 1)
                            nc.vector.reciprocal(rs[:, s, :], rs[:, s, :]).then_inc(rstd_done, 1)
                            dve.wait_ge(rstd_done, n + 3)
                            dve.wait_ge(transposed, n + 1)
                            nc.vector.tensor_scalar(xn[:, s, :], xt[:, s, :], rs[:, s, :], None,
                                                    ALU.mult).then_inc(xn_done, 1)
                            dve.wait_ge(transposed, n + 3)
                            nc.vector.tensor_tensor(
                                xg[:, s, :, :], ps[:, 2 * s:2 * s + 2, :].rearrange("p b (k t) -> p (b k) t", t=P),
                                g.unsqueeze(2).broadcast_to([P, DK, P]), ALU.mult).then_inc(scaled, 1)
                            dve.wait_ge(hi_done, n + 1)
                            cols = bass.ds(it * (2 * P) + s * P, P)
                            nc.vector.tensor_tensor(hT_lo[:, :, cols], xg[:, s, :, :],
                                                    hT_hi[:, :, cols].bitcast(F32), ALU.subtract).then_inc(lo_done, 1)

                @block.tensor
                def _(pe):
                    pe.sem_inc(transposed, 2)
                    pe.wait_ge(const_in, 32)
                    with pe.Fori(0, TILES // 2) as it:
                        for s in range(2):
                            n = 2 * it + s
                            pe.wait_ge(xn_done, n + 3)
                            pe.wait_ge(scaled, n + 1)
                            for k in range(DK):
                                last = nc.tensor.transpose(ps[:, 2 * s + k // 4, (k % 4) * P:(k % 4 + 1) * P],
                                                           xn[:, s, k * P:(k + 1) * P], ident[:, :])
                            last.then_inc(transposed, 1)

        with ExitStack() as inner:
            sbi = lambda n, s, d=F32: inner.enter_context(nc.sbuf_tensor(n, s, d))
            raw = sbi("wraw_a", [P, 2, DK, FC * P])
            w_hi = sbi("whi_a", [P, 2, DK, FC * P], F32R)
            w_lo = sbi("wlo_a", [P, 2, DK, FC * P], F32R)
            zo = sbi("zo_a", [P, 2, SEQ])
            zero = sbi("zero_a", [P, PADC])
            raw_in = [sem("raw_in0_a"), sem("raw_in1_a")]
            passed = sem("passed_a")
            w_hi_done, w_lo_done, w_used = sem("w_hi_a"), sem("w_lo_a"), sem("w_used_a")
            z_full, z_out, stored, pad_done, zero_done = (
                sem("z_full_a"), sem("z_out_a"), [sem("zst0_a"), sem("zst1_a")], sem("pad_a"), sem("zero_done_a"))
            with nc.Block() as block:
                @block.sync
                def _(sp):
                    sp.wait_ge(zero_done, 1)
                    sp.dma_start(zT[:, :, 0:PADC].rearrange("f p t -> p f t"),
                                 zero[:, :].unsqueeze(1).broadcast_to([P, ZT, PADC])).then_inc(pad_done, 16)
                    with sp.Fori(0, CHUNKS // 2) as it:
                        for s in range(2):
                            sp.wait_ge(w_lo_done, 2 * it + s + 1)
                            sp.sem_inc(passed, 1)
                            sp.dma_start(raw[:, s, :, :], w_in[bass.ds(2 * it + s, 1)].rearrange(
                                "n p k f -> p (n k) f")).then_inc(raw_in[s], 16)
                    sp.wait_ge(pad_done, 16)

                @block.gpsimd
                def _(pool):
                    nc.gpsimd.memset(zero[:, :], 0.0).then_inc(zero_done, 1)
                    pool.sem_inc(w_lo_done, 2)
                    with pool.Fori(0, CHUNKS // 2) as it:
                        for s in range(2):
                            n = 2 * it + s
                            pool.wait_ge(raw_in[s], 16 * (it + 1))
                            pool.wait_ge(w_used, n + 1)
                            pool.sem_inc(passed, 1)
                            nc.gpsimd.tensor_scalar(w_hi[:, s, :, :], raw[:, s, :, :], 1.0, None,
                                                    ALU.mult).then_inc(w_hi_done, 1)
                            pool.wait_ge(w_hi_done, n + 1)
                            nc.gpsimd.tensor_tensor(w_lo[:, s, :, :], raw[:, s, :, :],
                                                    w_hi[:, s, :, :].bitcast(F32), ALU.subtract).then_inc(w_lo_done, 1)

                @block.tensor
                def _(pe):
                    pe.sem_inc(w_used, 1)
                    with pe.Fori(0, CHUNKS // 2) as it:
                        for s in range(2):
                            n = 2 * it + s
                            pe.wait_ge(w_lo_done, n + 3)
                            for f in range(FC):
                                for tb in range(NTB):
                                    bank = f * NTB + tb
                                    pe.wait_ge(z_out, 8 * n + bank + 1)
                                    tok = slice(tb * TB, (tb + 1) * TB)
                                    feat = slice(f * P, (f + 1) * P)
                                    for k in range(DK):
                                        mm = nc.tensor.matmul(ps[:, bank, :], w_hi[:, s, k, feat], hT_hi[:, k, tok],
                                                              start=(k == 0), stop=False)
                                        if bank == 0 and k == 0:
                                            mm.then_inc(w_used, 1)
                                        nc.tensor.matmul(ps[:, bank, :], w_hi[:, s, k, feat], hT_lo[:, k, tok],
                                                         start=False, stop=False)
                                        mm = nc.tensor.matmul(ps[:, bank, :], w_lo[:, s, k, feat], hT_hi[:, k, tok],
                                                              start=False, stop=(k == DK - 1))
                                    mm.then_inc(z_full, 1)

                @block.scalar
                def _(act):
                    act.sem_inc(z_out, 8)
                    for f in range(FC):
                        act.sem_inc(stored[f], 16)
                    with act.Fori(0, CHUNKS // 2) as it:
                        for s in range(2):
                            n = 2 * it + s
                            for f in range(FC):
                                act.wait_ge(stored[f], 32 * it + (16 * s + 16))
                                for tb in range(NTB):
                                    bank = f * NTB + tb
                                    act.wait_ge(z_full, 8 * n + bank + 1)
                                    nc.scalar.activation(zo[:, f, tb * TB:(tb + 1) * TB], ps[:, bank, :],
                                                         ACT.Copy).then_inc(z_out, 1)
                                act.wait_ge(z_out, 8 * n + f * NTB + NTB + 8)
                                act.dma_start(zT[bass.ds(it * (2 * FC) + s * FC + f, 1), :, PADC:].rearrange(
                                    "n p t -> p (n t)"), zo[:, f, :]).then_inc(stored[f], 16)
                    for f in range(FC):
                        act.wait_ge(stored[f], 16 * CHUNKS + 16)


PE_STEPS = (["lora_w", "lora_a", "gate", "kk_norm", "v_keys", "score_a", "score_b", "norm_rows", "bonus",
             "probs_t_a", "probs_t_b", "pv", "t_beta", "t_kappa", "t_alpha", "t_v"]
            + [f"rw_score{h}" for h in range(HEADS)]
            + [f"first_t{q}" for q in range(2)]
            + [f"{s}{l}_{q}" for l in range(1, LEVELS) for s in ("ax", "xax") for q in range(2)]
            + ["av", "u", "w_t", "sa0", "grow0", "sa1", "grow1", "y", "out_t"])
DVE_STEPS = (["diff", "diff_mu", "zs", "kk_raw", "cum", "cum_before", "norm_floor", "norm_inv", "a_scale", "kmod",
              "kk", "alpha", "kk_a", "beta", "kappa", "rho", "rk", "rk_rk"]
             + [f"{s}_{g}" for g in "ab" for s in ("logit", "first_mask", "rowmax", "max", "negmax", "sink_gap")]
             + [f"{s}_{g}" for g in "ab" for s in ("denom", "inv", "probs")]
             + [f"masked{h}" for h in range(HEADS)]
             + [f"{s}{q}" for q in range(2) for s in ("a_first", "x_first", "xt_mask", "xt_first")]
             + [f"{s}{l}_{q}" for l in range(1, LEVELS) for s in ("ax_masked", "x_next") for q in range(2)]
             + ["sa_add0", "grow_add0", "state0", "sa_add1", "grow_add1", "state1",
                "y_sum", "y_mean", "y_center", "y_sq", "y_sqsum", "y_inv", "y_norm", "y_gain", "y_bias",
                "bonus_v", "y_bonus", "y_gate"])
ACT_STEPS = (["tanh_w", "sig_g", "kk_sq", "sig_w", "sig_a", "gate_copy", "norm_sqrt", "v_copy", "p_inc", "p_exc",
              "p_inv", "bonus_copy", "exp_a", "exp_sink_a", "exp_b", "exp_sink_b", "pt_copy_a", "pt_copy_b", "att_copy",
              "beta_t", "kappa_t", "alpha_t", "v_t", "av_copy", "u_copy", "w_copy", "y_rms", "out_copy"])


def progress(steps, sem):
    seen = []

    def mark(label):
        assert steps[len(seen)] == label, (steps[len(seen)], label)
        seen.append(label)
        return sem

    def done(i, label):
        return sem, i * len(steps) + (steps.index(label) + 2)

    return mark, done


def mix_tokens(nc, zT, mixT, params, consts, hrows, onehot, rel_bias, sinks, w_up, a_up, g_up, lnx_g, lnx_b, skew):
    with ExitStack() as ctx:
        sb = lambda n, s, d=F32: ctx.enter_context(nc.sbuf_tensor(n, s, d))
        sem = lambda n: ctx.enter_context(nc.semaphore(n))
        ps = ctx.enter_context(nc.psum_tensor("ps_m", [P, 8, 512], F32))
        par, con = sb("par_m", [P, NPV]), sb("con_m", [P, NCC])
        hsel = sb("hsel_m", [HEADS, RW])
        oneh, relb = sb("oneh_m", [BUCKETS + 1, EXT]), sb("relb_m", [BUCKETS + 1, HEADS])
        ext = sb("ext_m", [P, 2, EXT])
        bias = sb("bias_m", [P, HEADS, 2 * P])
        sink = sb("sink_m", [P, HEADS])
        lora = sb("lora_m", [P, RW])
        gup = sb("gup_m", [P, RW])
        lng, lnb = sb("lng_m", [P, RW]), sb("lnb_m", [P, RW])
        one_minus_ka = sb("omka_m", [P, PAIRS])
        first_mask = sb("firstmask_m", [P, 1])
        lnx_eps = sb("lnxeps_m", [P, 1])

        zr = sb("zr_m", [P, RWT, P + 1])
        zd, zs = sb("zd_m", [P, RWT, P]), sb("zs_m", [P, RWT, P])
        qT, kvT = sb("qT_m", [P, PAIRS, P]), sb("kvT_m", [P, 2, 2 * P])
        f4 = lambda n: sb(n, [P, PAIRS, P])
        kk_raw, kk_sq, sw, av, cum, cumx = f4("kkraw_m"), f4("kksq_m"), f4("sw_m"), f4("av_m"), f4("cum_m"), f4("cumx_m")
        p_inc, p_exc, p_inv = f4("pinc_m"), f4("pexc_m"), f4("pinv_m")
        ascale, kmod, kk, kka, betaT, kappaT, rk = (
            f4("ascale_m"), f4("kmod_m"), f4("kk_m"), f4("kka_m"), f4("betaT_m"), f4("kappaT_m"), f4("rk_m"))
        ar = sb("ar_m", [P, PAIRS, 2, P])
        th = sb("th_m", [HD, P])
        sg = sb("sg_m", [P, P])
        gate = sb("gate_m", [P, RW])
        nrm = sb("nrm_m", [HEADS, P])
        vk = sb("vk_m", [P, 2, P])
        bon = sb("bon_m", [P, HEADS])
        logit, pt = sb("logit_m", [P, HEADS, 2 * P]), sb("pt_m", [P, 2, 2, PAIRS, P])
        small = lambda n: sb(n, [P, HEADS])
        rowmax, negmax, gap, den, esink = small("rowmax_m"), small("negmax_m"), small("gap_m"), small("den_m"), small("esink_m")
        attT = sb("attT_m", [P, PAIRS, P])
        t4 = lambda n: sb(n, [P, RW])
        beta_t, kappa_t, alpha_t, v_t = t4("betat_m"), t4("kappat_m"), t4("alphat_m"), t4("vt_m")
        bm = sb("bm_m", [P, HEADS, 4, P])
        x_m, xt_m, ax = sb("x_m", [P, HEADS, P]), sb("xt_m", [P, HEADS, P]), sb("ax_m", [P, HEADS, P])
        avt, u_t, wT, sa = t4("avt_m"), t4("ut_m"), f4("wT_m"), t4("sa_m")
        state = sb("state_m", [P, 2, PAIRS, HD])
        grow = sb("grow_m", [P, PAIRS, HD])
        y, ysq, yb = t4("y_m"), t4("ysq_m"), t4("yb_m")
        ysum, yss = small("ysum_m"), small("yss_m")
        rwT = f4("rwT_m")

        col = lambda n: par[:, PV[n][0]:PV[n][1]]
        cst = lambda n: con[:, CC[n][0]:CC[n][1]]
        ident = cst("ident")
        score_mask = cst("score_mask").rearrange("p (a t) -> p a t", a=4)
        level_mask = cst("level_mask").rearrange("p (l t) -> p l t", l=LEVELS)
        head_of = cst("head_of").rearrange("p (f h) -> p f h", f=PAIRS)
        bank = lambda b: ps[:, b, :]
        over = lambda a, n: a.unsqueeze(2).broadcast_to([a.shape[0], a.shape[1], n])
        by_parity = lambda a: a.rearrange("p (f a v) -> p a f v", a=2, v=HD)
        four = lambda m: m.unsqueeze(1).broadcast_to([P, 4, P])

        c_in, b_ps, b_sb, b_st, b_rd, ready = sem("c_in_m"), sem("b_ps_m"), sem("b_sb_m"), sem("b_st_m"), sem("b_rd_m"), sem("ready_m")
        CIN = 13
        with nc.Block() as block:
            @block.sync
            def _(sp):
                for dst, src in ((par[:, :], params), (con[:, :], consts), (hsel[:, :], hrows), (oneh[:, :], onehot),
                                 (relb[0:BUCKETS, :], rel_bias), (sink[:, :], sinks.broadcast_to([P, HEADS])),
                                 (lora[0:HD, :], w_up), (lora[HD:P, :], a_up), (gup[:, :], g_up),
                                 (lng[:, :], lnx_g.broadcast_to([P, RW])), (lnb[:, :], lnx_b.broadcast_to([P, RW]))):
                    sp.dma_start(dst, src).then_inc(c_in, 16)
                for h in range(HEADS):
                    sp.wait_ge(b_sb, h + 1)
                    sp.dma_start(bass.AP(skew, h * P * EXT, [[EXT, P], [1, EXT]]), ext[:, h % 2, :]).then_inc(b_st, 16)
                sp.wait_ge(b_st, 16 * HEADS)
                sp.dma_start(bias[:, :, :], bass.AP(skew, P - 1, [[EXT - 1, P], [P * EXT, HEADS], [1, 2 * P]])).then_inc(b_rd, 16)
                sp.wait_ge(b_rd, 16)

            @block.vector
            def _(dve):
                nc.vector.memset(relb[BUCKETS:BUCKETS + 1, :], 1.0).then_inc(ready, 1)
                nc.vector.memset(first_mask[:, :], NEG)
                nc.vector.memset(lnx_eps[:, :], LNX_EPS)
                nc.vector.memset(state[:, :, :, :], 0.0)
                dve.wait_ge(c_in, 16 * 11)
                nc.vector.tensor_scalar(one_minus_ka[:, :], col("k_a"), -1.0, 1.0, ALU.mult, ALU.add)
                for h in range(HEADS):
                    dve.wait_ge(b_ps, h + 1)
                    if h >= 2:
                        dve.wait_ge(b_st, 16 * h)
                    nc.vector.tensor_copy(ext[:, h % 2, :], ps[:, h, 0:EXT]).then_inc(b_sb, 1)

            @block.tensor
            def _(pe):
                pe.wait_ge(c_in, 16 * 11)
                pe.wait_ge(ready, 1)
                for h in range(HEADS):
                    nc.tensor.matmul(ps[:, h, 0:EXT], relb[:, h:h + 1].broadcast_to([BUCKETS + 1, P]), oneh[:, :],
                                     start=True, stop=True).then_inc(b_ps, 1)

        pe_done, dve_done, act_done = sem("pe_done_m"), sem("dve_done_m"), sem("act_done_m")
        rw_in, qkv_in, rw_stored, att_stored = sem("rw_in_m"), sem("qkv_in_m"), sem("rwst_m"), sem("attst_m")
        pmark, pdone = progress(PE_STEPS, pe_done)
        vmark, vdone = progress(DVE_STEPS, dve_done)
        amark, adone = progress(ACT_STEPS, act_done)
        groups = {"a": 0, "b": 1}
        passed = sem("passed_m")

        with nc.Block() as block:
            @block.sync
            def _(sp):
                def load_rw(i):
                    sp.dma_start(zr[:, :, :], zT[0:RWT, :, bass.ds(i * P + (PADC - 1), P + 1)].rearrange(
                        "f p t -> p f t")).then_inc(rw_in, 16)

                def load_qkv(i):
                    sp.dma_start(qT[:, :, :], zT[RWT:RWT + PAIRS, :, bass.ds(i * P + PADC, P)].rearrange(
                        "f p t -> p f t")).then_inc(qkv_in, 16)
                    sp.dma_start(kvT[:, :, :], zT[RWT + PAIRS:ZT, :, bass.ds(i * P, 2 * P)].rearrange(
                        "f p t -> p f t")).then_inc(qkv_in, 16)

                def store(i):
                    sp.wait_ge(*adone(i, "att_copy"))
                    sp.sem_inc(passed, 1)
                    sp.dma_start(mixT[PAIRS:, :, bass.ds(i * P, P)].rearrange("f p t -> p f t"),
                                 attT[:, :, :]).then_inc(att_stored, 16)
                    sp.wait_ge(*adone(i, "out_copy"))
                    sp.sem_inc(passed, 1)
                    sp.dma_start(mixT[0:PAIRS, :, bass.ds(i * P, P)].rearrange("f p t -> p f t"),
                                 rwT[:, :, :]).then_inc(rw_stored, 16)

                load_rw(0)
                load_qkv(0)
                with sp.Fori(0, TILES - 1) as i:
                    sp.wait_ge(*vdone(i, "zs"))
                    sp.sem_inc(passed, 1)
                    load_rw(i + 1)
                    sp.wait_ge(*pdone(i, "score_b"))
                    sp.sem_inc(passed, 1)
                    load_qkv(i + 1)
                    store(i)
                store(TILES - 1)
                sp.wait_ge(rw_stored, 16 * TILES + 16)
                sp.wait_ge(att_stored, 16 * TILES + 16)

            def tile_start(eng, i):
                for sem_, steps in ((pe_done, PE_STEPS), (dve_done, DVE_STEPS), (act_done, ACT_STEPS)):
                    eng.wait_ge(sem_, i * len(steps) + 1)

            @block.tensor
            def _(pe):
                pe.sem_inc(pe_done, 1)
                with pe.Fori(0, TILES) as i:
                    tile_start(pe, i)
                    pe.wait_ge(*adone(i, "tanh_w"))
                    for f in range(PAIRS):
                        mm = nc.tensor.matmul(ps[:, 0, f * P:(f + 1) * P], lora[0:HD, f * P:(f + 1) * P], th[:, :],
                                              start=True, stop=True)
                    mm.then_inc(pmark("lora_w"), 1)
                    for f in range(PAIRS):
                        mm = nc.tensor.matmul(ps[:, 1, f * P:(f + 1) * P], lora[HD:P, f * P:(f + 1) * P], zs[HD:P, 12, :],
                                              start=True, stop=True)
                    mm.then_inc(pmark("lora_a"), 1)
                    pe.wait_ge(*adone(i, "sig_g"))
                    nc.tensor.matmul(bank(2), sg[:, :], gup[:, :], start=True, stop=True).then_inc(pmark("gate"), 1)
                    pe.wait_ge(*adone(i, "kk_sq"))
                    for f in range(PAIRS):
                        mm = nc.tensor.matmul(ps[0:HEADS, 3, 0:P], head_of[:, f, :], kk_sq[:, f, :],
                                              start=(f == 0), stop=(f == PAIRS - 1))
                    mm.then_inc(pmark("kk_norm"), 1)
                    pe.wait_ge(qkv_in, 32 * (i + 1))
                    pe.wait_ge(*adone(i, "norm_sqrt"))
                    for b in range(2):
                        mm = nc.tensor.transpose(ps[:, 3, b * P:(b + 1) * P], kvT[:, 1, b * P:(b + 1) * P], ident)
                    mm.then_inc(pmark("v_keys"), 1)
                    for g, kv in groups.items():
                        rows = slice(kv * HD, (kv + 1) * HD)
                        for j in range(PAIRS):
                            mm = nc.tensor.matmul(ps[:, 4 + 2 * kv + j // 2, (j % 2) * 2 * P:(j % 2 + 1) * 2 * P],
                                                  qT[rows, j, :], kvT[rows, 0, :], start=True, stop=True)
                        mm.then_inc(pmark("score_" + g), 1)
                    pe.wait_ge(*vdone(i, "norm_inv"))
                    pe.wait_ge(*adone(i, "sig_a"))
                    for f in range(PAIRS):
                        mm = nc.tensor.matmul(ps[:, 1, f * P:(f + 1) * P], hsel[:, f * P:(f + 1) * P], nrm[:, :],
                                              start=True, stop=True)
                    mm.then_inc(pmark("norm_rows"), 1)
                    pe.wait_ge(*vdone(i, "rk_rk"))
                    pe.wait_ge(*adone(i, "gate_copy"))
                    for f in range(PAIRS):
                        mm = nc.tensor.matmul(ps[:, 2, 2 * f:2 * f + 2], rk[:, f, :], cst("pair_sel"), start=True, stop=True)
                    mm.then_inc(pmark("bonus"), 1)
                    for g, kv in groups.items():
                        pe.wait_ge(*vdone(i, "probs_" + g))
                        for b in range(2):
                            for j in range(PAIRS):
                                mm = nc.tensor.transpose(ps[:, 4 + 2 * kv + b, j * P:(j + 1) * P],
                                                         logit[:, 4 * kv + j, b * P:(b + 1) * P], ident)
                        mm.then_inc(pmark("probs_t_" + g), 1)
                    pe.wait_ge(*adone(i, "sig_w"))
                    for g, kv in groups.items():
                        pe.wait_ge(*adone(i, "pt_copy_" + g))
                        for b in range(2):
                            mm = nc.tensor.matmul(ps[kv * HD:(kv + 1) * HD, 0, :], vk[:, b, kv * HD:(kv + 1) * HD],
                                                  pt[:, kv, b, :, :], start=(b == 0), stop=(b == 1))
                    mm.then_inc(pmark("pv"), 1)
                    for n, (name, src, ready_) in enumerate((("beta", betaT[:, :, :], "beta"), ("kappa", kappaT[:, :, :], "kappa"),
                                                             ("alpha", ar[:, :, 0, :], "alpha"), ("v", zs[:, 8:12, :], "zs"))):
                        pe.wait_ge(*vdone(i, ready_))
                        if name == "beta":
                            pe.wait_ge(*adone(i, "v_copy"))
                        for f in range(PAIRS):
                            mm = nc.tensor.transpose(ps[:, 3 + n, f * P:(f + 1) * P], src[:, f, :], ident)
                        mm.then_inc(pmark("t_" + name), 1)
                    pe.wait_ge(*vdone(i, "rho"))
                    pe.wait_ge(*adone(i, "att_copy"))
                    pe.wait_ge(*adone(i, "bonus_copy"))
                    for h in range(HEADS):
                        rows, f, b = slice((h % 2) * HD, (h % 2 + 1) * HD), h // 2, (7, 0, 1, 2)[h % 4]
                        if h >= 4:
                            pe.wait_ge(*vdone(i, f"masked{h - 4}"))
                        rhs = ar[rows, f, :, :]
                        nc.tensor.matmul(ps[:, b, 0:2 * P], betaT[rows, f, :], rhs, start=True, stop=True)
                        nc.tensor.matmul(ps[:, b, 2 * P:], kappaT[rows, f, :], rhs, start=True, stop=True).then_inc(
                            pmark(f"rw_score{h}"), 1)
                    pe.wait_ge(*adone(i, "v_t"))
                    for q in range(2):
                        pe.wait_ge(*vdone(i, f"masked{4 * q + 3}"))
                        for j in range(4):
                            mm = nc.tensor.transpose(ps[:, 3 + 3 * q, j * P:(j + 1) * P], bm[:, 4 * q + j, 0, :], ident)
                        mm.then_inc(pmark(f"first_t{q}"), 1)
                    for l in range(1, LEVELS):
                        for q in range(2):
                            pe.wait_ge(*vdone(i, f"xt_first{q}" if l == 1 else f"x_next{l - 1}_{q}"))
                            for j in range(4):
                                h = 4 * q + j
                                mm = nc.tensor.matmul(ps[:, 3 + 3 * q, j * P:(j + 1) * P], bm[:, h, 0, :], x_m[:, h, :],
                                                      start=True, stop=True)
                            mm.then_inc(pmark(f"ax{l}_{q}"), 1)
                        for q in range(2):
                            pe.wait_ge(*vdone(i, f"ax_masked{l}_{q}"))
                            bx, bt = ((4, 5), (7, 0))[q]
                            for j in range(4):
                                h = 4 * q + j
                                if l < LEVELS - 1:
                                    nc.tensor.matmul(ps[:, bx, j * P:(j + 1) * P], xt_m[:, h, :], ax[:, h, :],
                                                     start=True, stop=True)
                                mm = nc.tensor.matmul(ps[:, bt, j * P:(j + 1) * P], ax[:, h, :], xt_m[:, h, :],
                                                      start=True, stop=True)
                            mm.then_inc(pmark(f"xax{l}_{q}"), 1)
                    head = lambda a, h: a[:, h * HD:(h + 1) * HD]
                    for h in range(HEADS):
                        mm = nc.tensor.matmul(head(bank(1), h), bm[:, h, 2, :], head(v_t, h), start=True, stop=True)
                    mm.then_inc(pmark("av"), 1)
                    pe.wait_ge(*adone(i, "av_copy"))
                    pe.wait_ge(*vdone(i, f"x_next{LEVELS - 1}_1"))
                    for h in range(HEADS):
                        mm = nc.tensor.matmul(head(bank(2), h), xt_m[:, h, :], head(avt, h), start=True, stop=True)
                    mm.then_inc(pmark("u"), 1)
                    for h in range(HEADS):
                        rows, f = slice((h % 2) * HD, (h % 2 + 1) * HD), h // 2
                        mm = nc.tensor.matmul(ps[rows, 3, f * P:(f + 1) * P], head(alpha_t, h), xt_m[:, h, :],
                                              start=True, stop=True)
                    mm.then_inc(pmark("w_t"), 1)
                    for c in range(2):
                        tok = slice(c * CH, (c + 1) * CH)
                        pe.wait_ge(*(adone(i, "w_copy") if c == 0 else vdone(i, "state0")))
                        pe.sem_inc(passed, 1)
                        for h in range(HEADS):
                            rows, f = slice((h % 2) * HD, (h % 2 + 1) * HD), h // 2
                            mm = nc.tensor.matmul(ps[tok, 4 + h % 2, f * HD:(f + 1) * HD], wT[rows, f, tok], state[rows, c, f, :],
                                                  start=True, stop=True)
                        mm.then_inc(pmark(f"sa{c}"), 1)
                        pe.wait_ge(*vdone(i, f"sa_add{c}"))
                        pe.sem_inc(passed, 1)
                        for h in range(HEADS):
                            rows, f = slice((h % 2) * HD, (h % 2 + 1) * HD), h // 2
                            dst = ps[rows, 6 + c, f * HD:(f + 1) * HD]
                            nc.tensor.matmul(dst, head(kappa_t[tok, :], h), head(v_t[tok, :], h), start=True, stop=False)
                            mm = nc.tensor.matmul(dst, head(beta_t[tok, :], h), head(sa[tok, :], h), start=False, stop=True)
                        mm.then_inc(pmark(f"grow{c}"), 1)
                    for h in range(HEADS):
                        rows, f = slice((h % 2) * HD, (h % 2 + 1) * HD), h // 2
                        dst = ps[:, h % 2, f * HD:(f + 1) * HD]
                        nc.tensor.matmul(dst, bm[:, h, 3, :], head(v_t, h), start=True, stop=False)
                        nc.tensor.matmul(dst, bm[:, h, 1, :], head(sa, h), start=False, stop=False)
                        for c in range(2):
                            tok = slice(c * CH, (c + 1) * CH)
                            mm = nc.tensor.matmul(ps[tok, h % 2, f * HD:(f + 1) * HD], ar[rows, f, 1, tok], state[rows, c, f, :],
                                                  start=False, stop=True)
                    mm.then_inc(pmark("y"), 1)
                    pe.wait_ge(*vdone(i, "y_gate"))
                    for f in range(PAIRS):
                        mm = nc.tensor.transpose(ps[:, 1, f * P:(f + 1) * P], y[:, f * P:(f + 1) * P], ident)
                    mm.then_inc(pmark("out_t"), 1)

            @block.vector
            def _(dve):
                V = nc.vector
                w = lambda *labels: [dve.wait_ge(*vdone(i, n)) for n in labels]
                dve.sem_inc(dve_done, 1)
                with dve.Fori(0, TILES) as i:
                    tile_start(dve, i)
                    r, k, v = zs[:, 0:4, :], zs[:, 4:8, :], zs[:, 8:12, :]
                    dve.wait_ge(rw_in, 16 * (i + 1))
                    V.tensor_tensor(zd[:, :, :], zr[:, :, 0:P], zr[:, :, 1:P + 1], ALU.subtract).then_inc(vmark("diff"), 1)
                    w("diff")
                    V.tensor_tensor(zd[:, :, :], zd[:, :, :], over(col("mu"), P), ALU.mult).then_inc(vmark("diff_mu"), 1)
                    w("diff_mu")
                    V.tensor_tensor(zs[:, :, :], zd[:, :, :], zr[:, :, 1:P + 1], ALU.add).then_inc(vmark("zs"), 1)
                    w("zs")
                    V.tensor_tensor(kk_raw[:, :, :], k, over(col("k_k"), P), ALU.mult).then_inc(vmark("kk_raw"), 1)
                    dve.wait_ge(*adone(i, "sig_w"))
                    V.tensor_tensor_scan(cum[:, :, :].rearrange("p f t -> p (f t)"), cst("chunk_start"),
                                         sw[:, :, :].rearrange("p f t -> p (f t)"), 0.0, ALU.mult, ALU.add).then_inc(vmark("cum"), 1)
                    w("cum")
                    V.tensor_tensor(cumx[:, :, :], cum[:, :, :], sw[:, :, :], ALU.subtract).then_inc(vmark("cum_before"), 1)
                    dve.wait_ge(*adone(i, "norm_sqrt"))
                    V.tensor_scalar(nrm[:, :], nrm[:, :], 1e-12, None, ALU.max).then_inc(vmark("norm_floor"), 1)
                    w("norm_floor")
                    V.reciprocal(nrm[:, :], nrm[:, :]).then_inc(vmark("norm_inv"), 1)
                    dve.wait_ge(*adone(i, "sig_a"))
                    for f in range(PAIRS):
                        o = V.tensor_scalar(ascale[:, f, :], av[:, f, :], col("k_a")[:, f:f + 1], one_minus_ka[:, f:f + 1],
                                            ALU.mult, ALU.add)
                    o.then_inc(vmark("a_scale"), 1)
                    w("a_scale")
                    V.tensor_tensor(kmod[:, :, :], k, ascale[:, :, :], ALU.mult).then_inc(vmark("kmod"), 1)
                    dve.wait_ge(*pdone(i, "norm_rows"))
                    V.tensor_tensor(kk[:, :, :], bank(1).rearrange("p (f t) -> p f t", t=P), kk_raw[:, :, :],
                                    ALU.mult).then_inc(vmark("kk"), 1)
                    w("kk")
                    dve.wait_ge(*adone(i, "p_inv"))
                    V.scalar_tensor_tensor(ar[:, :, 0, :], kk[:, :, :], -1.0, p_exc[:, :, :], ALU.mult, ALU.mult).then_inc(vmark("alpha"), 1)
                    V.tensor_tensor(kka[:, :, :], kk[:, :, :], av[:, :, :], ALU.mult).then_inc(vmark("kk_a"), 1)
                    w("kk_a")
                    V.tensor_tensor(betaT[:, :, :], kka[:, :, :], p_inv[:, :, :], ALU.mult).then_inc(vmark("beta"), 1)
                    V.tensor_tensor(kappaT[:, :, :], kmod[:, :, :], p_inv[:, :, :], ALU.mult).then_inc(vmark("kappa"), 1)
                    V.tensor_tensor(ar[:, :, 1, :], r, p_inc[:, :, :], ALU.mult).then_inc(vmark("rho"), 1)
                    V.tensor_tensor(rk[:, :, :], r, kmod[:, :, :], ALU.mult).then_inc(vmark("rk"), 1)
                    w("rk")
                    V.tensor_tensor(rk[:, :, :], rk[:, :, :], over(col("r_k"), P), ALU.mult).then_inc(vmark("rk_rk"), 1)
                    for g, kv in groups.items():
                        hs = slice(4 * kv, 4 * kv + 4)
                        dve.wait_ge(*pdone(i, "score_" + g))
                        V.scalar_tensor_tensor(logit[:, hs, :].rearrange("p h t -> p (h t)"),
                                               ps[:, 4 + 2 * kv:6 + 2 * kv, :].rearrange("p b t -> p (b t)"), HD ** -0.5,
                                               bias[:, hs, :].rearrange("p h t -> p (h t)"), ALU.mult, ALU.add).then_inc(vmark("logit_" + g), 1)
                        w("logit_" + g)
                        V.tensor_scalar(logit[:, hs, 0:P], logit[:, hs, 0:P], first_mask[:, 0:1], None,
                                        ALU.add).then_inc(vmark("first_mask_" + g), 1)
                        w("first_mask_" + g)
                        V.tensor_reduce(rowmax[:, hs], logit[:, hs, :], AX.X, ALU.max).then_inc(vmark("rowmax_" + g), 1)
                        w("rowmax_" + g)
                        V.tensor_tensor(rowmax[:, hs], rowmax[:, hs], sink[:, hs], ALU.max).then_inc(vmark("max_" + g), 1)
                        w("max_" + g)
                        V.tensor_scalar(negmax[:, hs], rowmax[:, hs], -1.0, None, ALU.mult).then_inc(vmark("negmax_" + g), 1)
                        V.tensor_tensor(gap[:, hs], sink[:, hs], rowmax[:, hs], ALU.subtract).then_inc(vmark("sink_gap_" + g), 1)
                    for g, kv in groups.items():
                        hs = slice(4 * kv, 4 * kv + 4)
                        dve.wait_ge(*adone(i, "exp_sink_" + g))
                        V.tensor_tensor(den[:, hs], den[:, hs], esink[:, hs], ALU.add).then_inc(vmark("denom_" + g), 1)
                        w("denom_" + g)
                        V.reciprocal(den[:, hs], den[:, hs]).then_inc(vmark("inv_" + g), 1)
                        w("inv_" + g)
                        V.tensor_tensor(logit[:, hs, :], logit[:, hs, :], over(den[:, hs], 2 * P), ALU.mult).then_inc(vmark("probs_" + g), 1)
                    for h in range(HEADS):
                        dve.wait_ge(*pdone(i, f"rw_score{h}"))
                        V.tensor_tensor(bm[:, h, :, :], ps[:, (7, 0, 1, 2)[h % 4], :].rearrange("p (a t) -> p a t", a=4),
                                        score_mask, ALU.mult).then_inc(vmark(f"masked{h}"), 1)
                    for q in range(2):
                        hs = slice(4 * q, 4 * q + 4)
                        dve.wait_ge(*pdone(i, f"first_t{q}"))
                        V.tensor_tensor(x_m[:, hs, :], bank(3 + 3 * q).rearrange("p (h t) -> p h t", h=4), four(level_mask[:, 0, :]),
                                        ALU.mult).then_inc(vmark(f"a_first{q}"), 1)
                        w(f"a_first{q}")
                        V.tensor_tensor(x_m[:, hs, :], x_m[:, hs, :], four(ident), ALU.add).then_inc(vmark(f"x_first{q}"), 1)
                        V.tensor_tensor(xt_m[:, hs, :], bm[:, hs, 0, :], four(cst("first_mask_t")), ALU.mult).then_inc(vmark(f"xt_mask{q}"), 1)
                        w(f"xt_mask{q}")
                        V.tensor_tensor(xt_m[:, hs, :], xt_m[:, hs, :], four(ident), ALU.add).then_inc(vmark(f"xt_first{q}"), 1)
                    for l in range(1, LEVELS):
                        for q in range(2):
                            hs = slice(4 * q, 4 * q + 4)
                            dve.wait_ge(*pdone(i, f"ax{l}_{q}"))
                            V.tensor_tensor(ax[:, hs, :], bank(3 + 3 * q).rearrange("p (h t) -> p h t", h=4), four(level_mask[:, l, :]),
                                            ALU.mult).then_inc(vmark(f"ax_masked{l}_{q}"), 1)
                        for q in range(2):
                            hs = slice(4 * q, 4 * q + 4)
                            bx, bt = ((4, 5), (7, 0))[q]
                            dve.wait_ge(*pdone(i, f"xax{l}_{q}"))
                            if l < LEVELS - 1:
                                V.tensor_tensor(x_m[:, hs, :], bank(bx).rearrange("p (h t) -> p h t", h=4), x_m[:, hs, :], ALU.add)
                            V.tensor_tensor(xt_m[:, hs, :], bank(bt).rearrange("p (h t) -> p h t", h=4), xt_m[:, hs, :],
                                            ALU.add).then_inc(vmark(f"x_next{l}_{q}"), 1)
                    for c in range(2):
                        tok = slice(c * CH, (c + 1) * CH)
                        dve.wait_ge(*pdone(i, f"sa{c}"))
                        V.tensor_tensor(by_parity(sa[tok, :]), ps[tok, 4:6, 0:PAIRS * HD].rearrange("p a (f v) -> p a f v", f=PAIRS),
                                        by_parity(u_t[tok, :]), ALU.add).then_inc(vmark(f"sa_add{c}"), 1)
                        dve.wait_ge(*pdone(i, f"grow{c}"))
                        V.tensor_tensor(grow[:, :, :], ps[:, 6 + c, 0:PAIRS * HD].rearrange("p (f v) -> p f v", f=PAIRS),
                                        state[:, c, :, :], ALU.add).then_inc(vmark(f"grow_add{c}"), 1)
                        w(f"grow_add{c}")
                        if c == 1:
                            dve.wait_ge(*pdone(i, "y"))
                        V.tensor_tensor(state[:, 1 - c, :, :], grow[:, :, :],
                                        p_inc[:, :, c * CH + CH - 1:(c + 1) * CH].broadcast_to([P, PAIRS, HD]),
                                        ALU.mult).then_inc(vmark(f"state{c}"), 1)
                    y3 = lambda a: a[:, :].rearrange("p (h v) -> p h v", h=HEADS)
                    y_ps = ps[:, 0:2, 0:PAIRS * HD].rearrange("p a (f v) -> p f a v", f=PAIRS)
                    V.tensor_reduce(ysum[:, :].rearrange("p (f a) -> p f a", a=2), y_ps, AX.X, ALU.add).then_inc(vmark("y_sum"), 1)
                    w("y_sum")
                    V.tensor_scalar(ysum[:, :], ysum[:, :], 1.0 / HD, None, ALU.mult).then_inc(vmark("y_mean"), 1)
                    w("y_mean")
                    V.tensor_tensor(y[:, :].rearrange("p (f a v) -> p f a v", a=2, v=HD), y_ps,
                                    ysum[:, :].rearrange("p (f a) -> p f a", a=2).unsqueeze(3).broadcast_to([P, PAIRS, 2, HD]),
                                    ALU.subtract).then_inc(vmark("y_center"), 1)
                    w("y_center")
                    V.tensor_tensor(ysq[:, :], y[:, :], y[:, :], ALU.mult).then_inc(vmark("y_sq"), 1)
                    w("y_sq")
                    V.tensor_reduce(yss[:, :], y3(ysq), AX.X, ALU.add).then_inc(vmark("y_sqsum"), 1)
                    dve.wait_ge(*adone(i, "y_rms"))
                    V.reciprocal(yss[:, :], yss[:, :]).then_inc(vmark("y_inv"), 1)
                    w("y_inv")
                    V.tensor_tensor(y3(y), y3(y), over(yss[:, :], HD), ALU.mult).then_inc(vmark("y_norm"), 1)
                    w("y_norm")
                    V.tensor_tensor(y[:, :], y[:, :], lng[:, :], ALU.mult).then_inc(vmark("y_gain"), 1)
                    w("y_gain")
                    V.tensor_tensor(y[:, :], y[:, :], lnb[:, :], ALU.add).then_inc(vmark("y_bias"), 1)
                    V.tensor_tensor(y3(yb), y3(v_t), over(bon[:, :], HD), ALU.mult).then_inc(vmark("bonus_v"), 1)
                    w("bonus_v")
                    V.tensor_tensor(y[:, :], y[:, :], yb[:, :], ALU.add).then_inc(vmark("y_bonus"), 1)
                    w("y_bonus")
                    V.memset(first_mask[:, :], 0.0)
                    V.tensor_tensor(y[:, :], y[:, :], gate[:, :], ALU.mult).then_inc(vmark("y_gate"), 1)

            @block.scalar
            def _(act):
                A = nc.scalar
                for count, start in ((act_done, 1), (att_stored, 16), (rw_stored, 16)):
                    act.sem_inc(count, start)
                with act.Fori(0, TILES) as i:
                    tile_start(act, i)
                    act.wait_ge(att_stored, 16 * i + 16)
                    act.wait_ge(rw_stored, 16 * i + 16)
                    act.wait_ge(*vdone(i, "zs"))
                    A.activation(th[:, :], zs[0:HD, 12, :], ACT.Tanh).then_inc(amark("tanh_w"), 1)
                    A.activation(sg[:, :], zs[:, 13, :], ACT.Sigmoid).then_inc(amark("sig_g"), 1)
                    act.wait_ge(*vdone(i, "kk_raw"))
                    A.activation(kk_sq[:, :, :], kk_raw[:, :, :], ACT.Square).then_inc(amark("kk_sq"), 1)
                    act.wait_ge(*pdone(i, "lora_w"))
                    for f in range(PAIRS):
                        o = A.activation(sw[:, f, :], ps[:, 0, f * P:(f + 1) * P], ACT.Sigmoid, bias=col("w0")[:, f:f + 1])
                    o.then_inc(amark("sig_w"), 1)
                    act.wait_ge(*pdone(i, "lora_a"))
                    for f in range(PAIRS):
                        o = A.activation(av[:, f, :], ps[:, 1, f * P:(f + 1) * P], ACT.Sigmoid, bias=col("a0")[:, f:f + 1])
                    o.then_inc(amark("sig_a"), 1)
                    act.wait_ge(*pdone(i, "gate"))
                    A.activation(gate[:, :], bank(2), ACT.Copy).then_inc(amark("gate_copy"), 1)
                    act.wait_ge(*pdone(i, "kk_norm"))
                    A.activation(nrm[:, :], ps[0:HEADS, 3, 0:P], ACT.Sqrt).then_inc(amark("norm_sqrt"), 1)
                    act.wait_ge(*pdone(i, "v_keys"))
                    A.activation(vk[:, :, :], ps[:, 3, 0:2 * P].rearrange("p (b t) -> p b t", b=2), ACT.Copy).then_inc(amark("v_copy"), 1)
                    act.wait_ge(*vdone(i, "cum"))
                    A.activation(p_inc[:, :, :], cum[:, :, :], ACT.Exp, scale=-DECAY).then_inc(amark("p_inc"), 1)
                    act.wait_ge(*vdone(i, "cum_before"))
                    A.activation(p_exc[:, :, :], cumx[:, :, :], ACT.Exp, scale=-DECAY).then_inc(amark("p_exc"), 1)
                    A.activation(p_inv[:, :, :], cum[:, :, :], ACT.Exp, scale=DECAY).then_inc(amark("p_inv"), 1)
                    act.wait_ge(*pdone(i, "bonus"))
                    A.activation(bon[:, :], ps[:, 2, 0:HEADS], ACT.Copy).then_inc(amark("bonus_copy"), 1)
                    for g, kv in groups.items():
                        hs = slice(4 * kv, 4 * kv + 4)
                        act.wait_ge(*vdone(i, "sink_gap_" + g))
                        for h in range(4 * kv, 4 * kv + 4):
                            o = A.activation(logit[:, h, :], logit[:, h, :], ACT.Exp, bias=negmax[:, h:h + 1],
                                             accum_out=den[:, h:h + 1])
                        o.then_inc(amark("exp_" + g), 1)
                        A.activation(esink[:, hs], gap[:, hs], ACT.Exp).then_inc(amark("exp_sink_" + g), 1)
                    for g, kv in groups.items():
                        act.wait_ge(*pdone(i, "probs_t_" + g))
                        A.activation(pt[:, kv, :, :, :].rearrange("p b j t -> p (b j t)"),
                                     ps[:, 4 + 2 * kv:6 + 2 * kv, :].rearrange("p b t -> p (b t)"), ACT.Copy).then_inc(amark("pt_copy_" + g), 1)
                    act.wait_ge(*pdone(i, "pv"))
                    A.activation(attT[:, :, :], bank(0).rearrange("p (j t) -> p j t", j=PAIRS), ACT.Copy).then_inc(amark("att_copy"), 1)
                    for n, (name, dst) in enumerate((("beta", beta_t), ("kappa", kappa_t), ("alpha", alpha_t), ("v", v_t))):
                        act.wait_ge(*pdone(i, "t_" + name))
                        A.activation(dst[:, :], bank(3 + n), ACT.Copy).then_inc(amark(name + "_t"), 1)
                    act.wait_ge(*pdone(i, "av"))
                    A.activation(avt[:, :], bank(1), ACT.Copy).then_inc(amark("av_copy"), 1)
                    act.wait_ge(*pdone(i, "u"))
                    A.activation(u_t[:, :], bank(2), ACT.Copy).then_inc(amark("u_copy"), 1)
                    act.wait_ge(*pdone(i, "w_t"))
                    A.activation(wT[:, :, :], bank(3).rearrange("p (f t) -> p f t", f=PAIRS), ACT.Copy).then_inc(amark("w_copy"), 1)
                    act.wait_ge(*vdone(i, "y_sqsum"))
                    A.activation(yss[:, :], yss[:, :], ACT.Sqrt, scale=1.0 / HD, bias=lnx_eps[:, 0:1]).then_inc(amark("y_rms"), 1)
                    act.wait_ge(*pdone(i, "out_t"))
                    A.activation(rwT[:, :, :], bank(1).rearrange("p (f t) -> p f t", f=PAIRS), ACT.Copy).then_inc(amark("out_copy"), 1)


HG, HGD = 4, FF // 4
TBK = 512
BLOCKS = SEQ // TBK
NJ = [(n, j) for n in range(2) for j in range(4)]
each = lambda s: [f"{s}{n}_{j}" for n, j in NJ]
PE_L = ([*each("out")] + [f"ut{k}" for k in range(DK)], each("up") + each("down"),
        [f"xt{k}" for k in range(DK)] + ["pt0", "pt1"] + each("ple") + each("gate"))
ACT_L = (["mix_hi"] + [f"{s}{j}" for j in range(4) for s in ("ss", "rms")] + [f"u_hi{k}" for k in range(DK)],
         [f"{s}{n}_{j}" for n, j in NJ for s in ("relu", "h_hi")],
         [f"x2_hi{k}" for k in range(DK)] + ["p_hi0", "p_hi1"] + each("e_copy")
         + [f"{s}{j}" for s in ("ess", "erms") for j in range(4)] + each("sig") + [f"{s}{j}" for s in ("fss", "frms") for j in range(4)])
DVE_L = (["mix_lo"] + each("out_add") + [f"{s}{j}" for j in range(4) for s in ("inv", "xn")]
         + [f"{s}{k}" for k in range(DK) for s in ("ug", "u_lo")],
         [f"{s}{n}_{j}" for n, j in NJ for s in ("square", "h_lo")] + each("down_add"),
         [f"x2_lo{k}" for k in range(DK)] + ["p_lo0", "p_lo1"] + [f"{s}{j}" for j in range(4) for s in ("einv", "e_norm")]
         + [f"{s}{n}_{j}" for n, j in NJ for s in ("gmul", "x_add")] + [f"{s}{j}" for j in range(4) for s in ("finv", "fout")])


def nested_progress(parts, sem):
    pre, mid, post = parts
    total, seen = len(pre) + HG * len(mid) + len(post), []

    def mark(label):
        assert (pre + mid + post)[len(seen)] == label, ((pre + mid + post)[len(seen)], label)
        seen.append(label)
        return sem

    def done(b, g, label):
        if label in pre:
            return sem, b * total + (pre.index(label) + 2)
        if label in mid:
            return sem, b * total + g * len(mid) + (len(pre) + mid.index(label) + 2)
        return sem, b * total + (len(pre) + HG * len(mid) + post.index(label) + 2)

    return mark, done, total


def finish_layer(nc, x, p, mixT, out, params, consts, ple_g, final_g, w_out, w_up, w_down, w_ple, w_gate):
    PRE, MID, POST = 4, 8, 6
    PER = PRE + HG * MID + POST
    with ExitStack() as ctx:
        sb = lambda n, s, d=F32: ctx.enter_context(nc.sbuf_tensor(n, s, d))
        sem = lambda n: ctx.enter_context(nc.semaphore(n))
        ps = ctx.enter_context(nc.psum_tensor("ps_f", [P, 8, 512], F32))
        par, ident = sb("par_f", [P, NPV]), sb("ident_f", [P, P])
        pleg, fing = sb("pleg_f", [P, D]), sb("fing_f", [P, D])
        eps = sb("eps_f", [P, 1])
        raw = sb("wraw_f", [P, 2, 4, 512])
        w_hi, w_lo = sb("whi_f", [P, 2, 4, 512], F32R), sb("wlo_f", [P, 2, 4, 512], F32R)
        xr = sb("x_f", [P, 4, D])
        stage = sb("stage_f", [P, 4, D])
        act_hi, act_lo = sb("acthi_f", [P, DK, TBK], F32R), sb("actlo_f", [P, DK, TBK], F32R)
        h_hi, h_lo = sb("hhi_f", [P, 8, TBK], F32R), sb("hlo_f", [P, 8, TBK], F32R)
        tmp, sq = sb("tmp_f", [P, 2, 512]), sb("sq_f", [P, 2, 512])
        pin = sb("p_f", [P, 4, PLE])
        pT_hi, pT_lo = sb("pthi_f", [P, 2, TBK], F32R), sb("ptlo_f", [P, 2, TBK], F32R)
        e = sb("e_f", [P, 4, D])
        stat = sb("stat_f", [P, 3, 4])
        junk = sb("junk_f", [P, D])
        gain = par[:, PV["norm_mlp_g"][0]:PV["norm_mlp_g"][1]]

        const_in, eps_done = sem("const_in_f"), sem("eps_f_done")
        raw_in = [sem("raw_in0_f"), sem("raw_in1_f")]
        w_hi_done, w_lo_done, w_used = sem("w_hi_f_done"), sem("w_lo_f_done"), sem("w_used_f")
        x_in, mix_in, p_in, stored = sem("x_in_f"), sem("mix_in_f"), sem("p_in_f"), sem("stored_f")
        pe_done, dve_done, act_done = sem("pe_done_f"), sem("dve_done_f"), sem("act_done_f")
        passed = sem("passed_f")
        pmark, pdone, PT = nested_progress(PE_L, pe_done)
        vmark, vdone, VT = nested_progress(DVE_L, dve_done)
        amark, adone, AT = nested_progress(ACT_L, act_done)

        def block_start(eng, b):
            for s_, t_ in ((pe_done, PT), (dve_done, VT), (act_done, AT)):
                eng.wait_ge(s_, b * t_ + 1)

        with nc.Block() as block:
            @block.sync
            def _(sp):
                for dst, src in ((par[:, :], params), (ident[:, :], consts[:, CC["ident"][0]:CC["ident"][1]]),
                                 (pleg[:, :], ple_g.broadcast_to([P, D])), (fing[:, :], final_g.broadcast_to([P, D]))):
                    sp.dma_start(dst, src).then_inc(const_in, 16)

                def load(n, s, src, k=4):
                    sp.wait_ge(w_lo_done, n + 1)
                    sp.sem_inc(passed, 1)
                    sp.dma_start(raw[:, s, 0:k, :], src).then_inc(raw_in[s], 16)

                with sp.Fori(0, BLOCKS) as b:
                    for c in range(PRE):
                        load(b * PER + c, c % 2, w_out[c])
                    with sp.Fori(0, HG) as g:
                        for c in range(MID):
                            src = w_up if c < 4 else w_down
                            load(b * PER + g * MID + (PRE + c), c % 2,
                                 src[bass.ds(g * 4 + c % 4, 1)].rearrange("n p k f -> p (n k) f"))
                    for c in range(POST):
                        src = w_ple[c] if c < 2 else w_gate[c - 2]
                        load(b * PER + (PRE + HG * MID + c), c % 2, src, 2 if c < 2 else 4)

            @block.gpsimd
            def _(pool):
                pool.sem_inc(w_lo_done, 2)

                def split(n, s, uses, k=4):
                    pool.wait_ge(raw_in[s], 16 * uses)
                    pool.wait_ge(w_used, n + 1)
                    pool.sem_inc(passed, 1)
                    nc.gpsimd.tensor_scalar(w_hi[:, s, 0:k, :], raw[:, s, 0:k, :], 1.0, None, ALU.mult).then_inc(w_hi_done, 1)
                    pool.wait_ge(w_hi_done, n + 1)
                    nc.gpsimd.tensor_tensor(w_lo[:, s, 0:k, :], raw[:, s, 0:k, :], w_hi[:, s, 0:k, :].bitcast(F32),
                                            ALU.subtract).then_inc(w_lo_done, 1)

                with pool.Fori(0, BLOCKS) as b:
                    for c in range(PRE):
                        split(b * PER + c, c % 2, b * (PER // 2) + (c // 2 + 1))
                    with pool.Fori(0, HG) as g:
                        for c in range(MID):
                            split(b * PER + g * MID + (PRE + c), c % 2, b * (PER // 2) + g * (MID // 2) + ((PRE + c) // 2 + 1))
                    for c in range(POST):
                        m = PRE + HG * MID + c
                        split(b * PER + m, c % 2, b * (PER // 2) + (m // 2 + 1), 2 if c < 2 else 4)

            @block.tensor
            def _(pe):
                T = nc.tensor
                pe.sem_inc(w_used, 1)
                pe.sem_inc(pe_done, 1)
                pe.wait_ge(const_in, 64)

                def products(bank, s, k0, ks, weights_still, j, hi, lo, first, final, label):
                    for k in range(ks):
                        if weights_still:
                            wh, wl = (w[:, s, k, j * P:(j + 1) * P] for w in (w_hi, w_lo))
                            pairs = ((wh, hi[:, k0 + k, :]), (wh, lo[:, k0 + k, :]), (wl, hi[:, k0 + k, :]))
                        else:
                            ah, al = (a[:, k0 + k, j * P:(j + 1) * P] for a in (hi, lo))
                            pairs = ((ah, w_hi[:, s, k, :]), (ah, w_lo[:, s, k, :]), (al, w_hi[:, s, k, :]))
                        for t, (still, moving) in enumerate(pairs):
                            mm = T.matmul(ps[:, bank, :], still, moving, start=(first and k == 0 and t == 0),
                                          stop=(final and k == ks - 1 and t == 2))
                            if j == 0 and k == 0 and t == 0:
                                mm.then_inc(w_used, 1)
                    if final:
                        mm.then_inc(pmark(label), 1)

                def project(name, n, n_chunk, banks, weights_still, hi, lo, free, ready=None, chunks=2, ks=4):
                    for c in range(chunks):
                        pe.wait_ge(w_lo_done, n_chunk + (c + 3))
                        for j in range(4):
                            if c == 0:
                                pe.wait_ge(*free(j))
                            if ready is not None and j == 0:
                                pe.wait_ge(*ready((c + 1) * ks - 1))
                            products(banks + j, (c if chunks == 2 else n) % 2, c * ks, ks, weights_still, j, hi, lo,
                                     c == 0, c == chunks - 1, f"{name}{n}_{j}")

                with pe.Fori(0, BLOCKS) as b:
                    block_start(pe, b)
                    pe.wait_ge(*vdone(b, 0, "mix_lo"))
                    for n in range(2):
                        project("out", n, b * PER + 2 * n, 4 * n, False, act_hi, act_lo,
                                free=lambda j: vdone(b, 0, "mix_lo"))
                    for j in range(4):
                        pe.wait_ge(*vdone(b, 0, f"xn{j}"))
                    for k in range(DK):
                        for j in range(4):
                            mm = T.transpose(ps[:, k, j * P:(j + 1) * P], stage[:, j, k * P:(k + 1) * P], ident[:, :])
                        mm.then_inc(pmark(f"ut{k}"), 1)
                    pe.wait_ge(*vdone(b, 0, f"u_lo{DK - 1}"))
                    pe.sem_inc(passed, 1)
                    with pe.Fori(0, HG) as g:
                        for n in range(2):
                            ahead = b * VT + g * len(DVE_L[1]) + (len(DVE_L[0]) + 1)
                            project("up", n, b * PER + g * MID + (PRE + 2 * n), 4 * n, True, act_hi, act_lo,
                                    free=lambda j: (dve_done, ahead - (3 - j) - (0 if n else 4)))
                        for n in range(2):
                            project("down", n, b * PER + g * MID + (PRE + 4 + 2 * n), 4 * n, False, h_hi, h_lo,
                                    free=lambda j: adone(b, g, f"relu{n}_{j}"),
                                    ready=lambda k: vdone(b, g, f"h_lo{k // 4}_{k % 4}"))
                    for k in range(DK):
                        pe.wait_ge(*vdone(b, HG - 1, f"down_add1_3"))
                        for j in range(4):
                            mm = T.transpose(ps[:, k, j * P:(j + 1) * P], xr[:, j, k * P:(k + 1) * P], ident[:, :])
                        mm.then_inc(pmark(f"xt{k}"), 1)
                    pe.wait_ge(p_in, 16 * (b + 1))
                    for k in range(2):
                        pe.wait_ge(*vdone(b, 0, f"x2_lo{k}"))
                        for j in range(4):
                            mm = T.transpose(ps[:, k, j * P:(j + 1) * P], pin[:, j, k * P:(k + 1) * P], ident[:, :])
                        mm.then_inc(pmark(f"pt{k}"), 1)
                    base = b * PER + (PRE + HG * MID)
                    pe.wait_ge(*vdone(b, 0, "p_lo1"))
                    for n in range(2):
                        project("ple", n, base + n, 4 * (1 - n), False, pT_hi, pT_lo,
                                free=lambda j: vdone(b, 0, "p_lo1"), chunks=1, ks=2)
                    for n in range(2):
                        project("gate", n, base + (2 + 2 * n), 4 * (1 - n), False, act_hi, act_lo,
                                free=lambda j: adone(b, 0, f"e_copy{n}_{j}"))

            @block.scalar
            def _(act):
                A = nc.scalar
                act.sem_inc(act_done, 1)
                act.sem_inc(stored, 16)
                act.wait_ge(eps_done, 1)
                tok = lambda a, b: a[bass.ds(b * TBK, TBK), :].rearrange("(j p) d -> p j d", p=P)
                with act.Fori(0, BLOCKS) as b:
                    block_start(act, b)
                    act.dma_start(stage[:, :, :].rearrange("p j d -> p (j d)").rearrange("p (k t) -> p k t", k=DK),
                                  mixT[:, :, bass.ds(b * TBK, TBK)].rearrange("k p t -> p k t")).then_inc(mix_in, 16)
                    act.dma_start(xr[:, :, :], tok(x, b)).then_inc(x_in, 16)
                    act.dma_start(pin[:, :, :], tok(p, b)).then_inc(p_in, 16)
                    act.wait_ge(mix_in, 16 * (b + 1))
                    A.activation(act_hi[:, :, :].rearrange("p k t -> p (k t)"), stage[:, :, :].rearrange("p j d -> p (j d)"),
                                 ACT.Copy).then_inc(amark("mix_hi"), 1)
                    for j in range(4):
                        act.wait_ge(*vdone(b, 0, f"out_add1_{j}"))
                        A.activation(junk[:, :], xr[:, j, :], ACT.Square, accum_out=stat[:, 0, j:j + 1]).then_inc(amark(f"ss{j}"), 1)
                        act.wait_ge(*adone(b, 0, f"ss{j}"))
                        A.activation(stat[:, 0, j:j + 1], stat[:, 0, j:j + 1], ACT.Sqrt, scale=1.0 / D,
                                     bias=eps[:, 0:1]).then_inc(amark(f"rms{j}"), 1)
                    for k in range(DK):
                        act.wait_ge(*vdone(b, 0, f"ug{k}"))
                        A.activation(act_hi[:, k, :], sq[:, k % 2, :], ACT.Copy).then_inc(amark(f"u_hi{k}"), 1)
                    with act.Fori(0, HG) as g:
                        for n, j in NJ:
                            act.wait_ge(*pdone(b, g, f"up{n}_{j}"))
                            A.activation(tmp[:, j % 2, :], ps[:, 4 * n + j, :], ACT.Relu).then_inc(amark(f"relu{n}_{j}"), 1)
                            act.wait_ge(*vdone(b, g, f"square{n}_{j}"))
                            A.activation(h_hi[:, 4 * n + j, :], sq[:, j % 2, :], ACT.Copy).then_inc(amark(f"h_hi{n}_{j}"), 1)
                    for k in range(DK):
                        act.wait_ge(*pdone(b, 0, f"xt{k}"))
                        A.activation(act_hi[:, k, :], ps[:, k, :], ACT.Copy).then_inc(amark(f"x2_hi{k}"), 1)
                    for k in range(2):
                        act.wait_ge(*pdone(b, 0, f"pt{k}"))
                        A.activation(pT_hi[:, k, :], ps[:, k, :], ACT.Copy).then_inc(amark(f"p_hi{k}"), 1)
                    act.wait_ge(stored, 64 * b + 16)
                    for n, j in NJ:
                        act.wait_ge(*pdone(b, 0, f"ple{n}_{j}"))
                        A.activation(e[:, j, n * 512:(n + 1) * 512], ps[:, 4 * (1 - n) + j, :], ACT.Copy).then_inc(amark(f"e_copy{n}_{j}"), 1)
                    for j in range(4):
                        act.wait_ge(*adone(b, 0, f"ess{j - 1}" if j else "e_copy1_3"))
                        A.activation(junk[:, :], e[:, j, :], ACT.Square, accum_out=stat[:, 1, j:j + 1]).then_inc(amark(f"ess{j}"), 1)
                    for j in range(4):
                        act.wait_ge(*adone(b, 0, f"ess{j}"))
                        A.activation(stat[:, 1, j:j + 1], stat[:, 1, j:j + 1], ACT.Sqrt, scale=1.0 / D,
                                     bias=eps[:, 0:1]).then_inc(amark(f"erms{j}"), 1)
                    for n, j in NJ:
                        act.wait_ge(*pdone(b, 0, f"gate{n}_{j}"))
                        if n or j >= 2:
                            act.wait_ge(*vdone(b, 0, f"gmul{n if j >= 2 else n - 1}_{(j + 2) % 4}"))
                        A.activation(tmp[:, j % 2, :], ps[:, 4 * (1 - n) + j, :], ACT.Sigmoid).then_inc(amark(f"sig{n}_{j}"), 1)
                    for j in range(4):
                        act.wait_ge(*vdone(b, 0, f"x_add1_{j}"))
                        act.wait_ge(*adone(b, 0, f"fss{j - 1}" if j else "erms3"))
                        A.activation(junk[:, :], xr[:, j, :], ACT.Square, accum_out=stat[:, 2, j:j + 1]).then_inc(amark(f"fss{j}"), 1)
                    for j in range(4):
                        act.wait_ge(*adone(b, 0, f"fss{j}"))
                        A.activation(stat[:, 2, j:j + 1], stat[:, 2, j:j + 1], ACT.Sqrt, scale=1.0 / D,
                                     bias=eps[:, 0:1]).then_inc(amark(f"frms{j}"), 1)
                    for j in range(4):
                        act.wait_ge(*vdone(b, 0, f"fout{j}"))
                        act.dma_start(out[bass.ds(b * TBK + j * P, P), :], e[:, j, :]).then_inc(stored, 16)
                act.wait_ge(stored, 64 * BLOCKS + 16)

            @block.vector
            def _(dve):
                V = nc.vector
                dve.sem_inc(dve_done, 1)
                V.memset(eps[:, :], NORM_EPS).then_inc(eps_done, 1)
                dve.wait_ge(const_in, 64)
                with dve.Fori(0, BLOCKS) as b:
                    block_start(dve, b)
                    dve.wait_ge(*adone(b, 0, "mix_hi"))
                    V.tensor_tensor(act_lo[:, :, :].rearrange("p k t -> p (k t)"), stage[:, :, :].rearrange("p j d -> p (j d)"),
                                    act_hi[:, :, :].rearrange("p k t -> p (k t)").bitcast(F32), ALU.subtract).then_inc(vmark("mix_lo"), 1)
                    dve.wait_ge(x_in, 16 * (b + 1))
                    for n, j in NJ:
                        dve.wait_ge(*pdone(b, 0, f"out{n}_{j}"))
                        V.tensor_tensor(xr[:, j, n * 512:(n + 1) * 512], ps[:, 4 * n + j, :], xr[:, j, n * 512:(n + 1) * 512],
                                        ALU.add).then_inc(vmark(f"out_add{n}_{j}"), 1)
                    for j in range(4):
                        dve.wait_ge(*adone(b, 0, f"rms{j}"))
                        V.reciprocal(stat[:, 0, j:j + 1], stat[:, 0, j:j + 1]).then_inc(vmark(f"inv{j}"), 1)
                        dve.wait_ge(*vdone(b, 0, f"inv{j}"))
                        V.tensor_scalar(stage[:, j, :], xr[:, j, :], stat[:, 0, j:j + 1], None, ALU.mult).then_inc(vmark(f"xn{j}"), 1)
                    for k in range(DK):
                        dve.wait_ge(*pdone(b, 0, f"ut{k}"))
                        V.tensor_scalar(sq[:, k % 2, :], ps[:, k, :], gain[:, k:k + 1], None, ALU.mult).then_inc(vmark(f"ug{k}"), 1)
                        dve.wait_ge(*adone(b, 0, f"u_hi{k}"))
                        V.tensor_tensor(act_lo[:, k, :], sq[:, k % 2, :], act_hi[:, k, :].bitcast(F32),
                                        ALU.subtract).then_inc(vmark(f"u_lo{k}"), 1)
                    with dve.Fori(0, HG) as g:
                        for n, j in NJ:
                            dve.wait_ge(*adone(b, g, f"relu{n}_{j}"))
                            V.tensor_tensor(sq[:, j % 2, :], tmp[:, j % 2, :], tmp[:, j % 2, :], ALU.mult).then_inc(vmark(f"square{n}_{j}"), 1)
                            dve.wait_ge(*adone(b, g, f"h_hi{n}_{j}"))
                            V.tensor_tensor(h_lo[:, 4 * n + j, :], sq[:, j % 2, :], h_hi[:, 4 * n + j, :].bitcast(F32),
                                            ALU.subtract).then_inc(vmark(f"h_lo{n}_{j}"), 1)
                        for n, j in NJ:
                            dve.wait_ge(*pdone(b, g, f"down{n}_{j}"))
                            V.tensor_tensor(xr[:, j, n * 512:(n + 1) * 512], ps[:, 4 * n + j, :], xr[:, j, n * 512:(n + 1) * 512],
                                            ALU.add).then_inc(vmark(f"down_add{n}_{j}"), 1)
                    for k in range(DK):
                        dve.wait_ge(*adone(b, 0, f"x2_hi{k}"))
                        V.tensor_tensor(act_lo[:, k, :], ps[:, k, :], act_hi[:, k, :].bitcast(F32), ALU.subtract).then_inc(vmark(f"x2_lo{k}"), 1)
                    for k in range(2):
                        dve.wait_ge(*adone(b, 0, f"p_hi{k}"))
                        V.tensor_tensor(pT_lo[:, k, :], ps[:, k, :], pT_hi[:, k, :].bitcast(F32), ALU.subtract).then_inc(vmark(f"p_lo{k}"), 1)
                    for j in range(4):
                        dve.wait_ge(*adone(b, 0, f"erms{j}"))
                        V.reciprocal(stat[:, 1, j:j + 1], stat[:, 1, j:j + 1]).then_inc(vmark(f"einv{j}"), 1)
                        dve.wait_ge(*vdone(b, 0, f"einv{j}"))
                        V.scalar_tensor_tensor(e[:, j, :], e[:, j, :], stat[:, 1, j:j + 1], pleg[:, :], ALU.mult,
                                               ALU.mult).then_inc(vmark(f"e_norm{j}"), 1)
                    for n, j in NJ:
                        cols = slice(n * 512, (n + 1) * 512)
                        dve.wait_ge(*adone(b, 0, f"sig{n}_{j}"))
                        dve.wait_ge(*vdone(b, 0, f"e_norm{j}"))
                        V.tensor_tensor(e[:, j, cols], tmp[:, j % 2, :], e[:, j, cols], ALU.mult).then_inc(vmark(f"gmul{n}_{j}"), 1)
                        dve.wait_ge(*vdone(b, 0, f"gmul{n}_{j}"))
                        V.tensor_tensor(xr[:, j, cols], e[:, j, cols], xr[:, j, cols], ALU.add).then_inc(vmark(f"x_add{n}_{j}"), 1)
                    for j in range(4):
                        dve.wait_ge(*adone(b, 0, f"frms{j}"))
                        V.reciprocal(stat[:, 2, j:j + 1], stat[:, 2, j:j + 1]).then_inc(vmark(f"finv{j}"), 1)
                        dve.wait_ge(*vdone(b, 0, f"finv{j}"))
                        V.scalar_tensor_tensor(e[:, j, :], xr[:, j, :], stat[:, 2, j:j + 1], fing[:, :], ALU.mult,
                                               ALU.mult).then_inc(vmark(f"fout{j}"), 1)


def pack(inputs):
    f = lambda n: np.ascontiguousarray(inputs[n])
    per_feature = lambda a: np.asarray(a).reshape(-1, P).T
    q = np.arange(RW).reshape(2, PAIRS, HD).transpose(1, 0, 2).reshape(-1)
    cols = np.concatenate([np.arange(RWT * P), RWT * P + q, np.arange((RWT + PAIRS) * P, ZT * P)])
    rows = np.concatenate([np.arange(RW), RW + q])
    chunks = lambda w, n, c, k: np.asarray(w).reshape(c, k, P, n, -1).transpose(3, 0, 2, 1, 4).reshape(n * c, P, k, -1)
    up = f("w_ff_up")[0]
    down = f("w_ff_down")[0]
    a = {
        "x": f("x")[0], "p": f("p")[0, 0],
        "params": np.concatenate([per_feature(inputs[n]) for n in
                                  ("norm_mix_g", "norm_mlp_g", "mu_shift", "w0", "a0", "k_k", "k_a", "r_k")], 1),
        "consts": shape_constants(), "hrows": head_rows(), "onehot": bucket_onehot(),
        "rel_bias": f("rel_bias"), "sinks": f("sinks"),
        "w_lora": f("w_up")[0], "a_lora": f("a_up")[0], "g_lora": f("g_up")[0],
        "lnx_g": f("lnx_g"), "lnx_b": f("lnx_b"),
        "ple_g": f("ple_norm_g"), "final_g": f("final_norm_g").reshape(1, D),
        "w_in": chunks(f("w_in")[0][:, cols], ZT // 2, 1, DK),
        "w_out": chunks(f("w_out")[0][rows], 2, 2, 4),
        "w_ff_up": chunks(up, 2 * HG, 2, 4),
        "w_ff_down": np.concatenate([chunks(down[g * HGD:(g + 1) * HGD], 2, 2, 4) for g in range(HG)], 0),
        "w_ple": chunks(f("ple_proj")[0], 2, 1, 2),
        "w_gate": chunks(f("ple_gate")[0], 2, 2, 4),
    }
    return {k: np.ascontiguousarray(v) for k, v in a.items()}


def build(nc, t, out):
    zT = nc.dram_tensor("zT", [ZT, P, PADC + SEQ], F32, kind="Internal")
    mixT = nc.dram_tensor("mixT", [2 * PAIRS, P, SEQ], F32, kind="Internal")
    skew = nc.dram_tensor("skew", [HEADS * P * EXT + P], F32, kind="Internal")
    norm_and_project(nc, t["x"], t["w_in"], t["params"], t["consts"], zT)
    mix_tokens(nc, zT, mixT, t["params"], t["consts"], t["hrows"], t["onehot"], t["rel_bias"], t["sinks"],
               t["w_lora"], t["a_lora"], t["g_lora"], t["lnx_g"], t["lnx_b"], skew)
    finish_layer(nc, t["x"], t["p"], mixT, out, t["params"], t["consts"], t["ple_g"], t["final_g"],
                 t["w_out"], t["w_ff_up"], t["w_ff_down"], t["w_ple"], t["w_gate"])


def kernel(**inputs):
    import concourse.bacc as bacc
    from concourse.bass_utils import run_bass_kernel_spmd

    nc = bacc.Bacc("TRN2", target_bir_lowering=False, num_devices=1)
    arrays = {f"in_{k}": v for k, v in pack(inputs).items()}
    t = {k[3:]: nc.dram_tensor(k, v.shape, mybir.dt.from_np(v.dtype), kind="ExternalInput").ap() for k, v in arrays.items()}
    out = nc.dram_tensor("out_y", (SEQ, D), F32, kind="ExternalOutput").ap()
    build(nc, t, out)
    r = run_bass_kernel_spmd(nc, [arrays], core_ids=[0])
    return np.asarray(r.results[0]["out_y"]).reshape(1, SEQ, D)
```

```python
from contextlib import ExitStack

import numpy as np

import concourse.bass as bass
from concourse import mybir

F32 = mybir.dt.float32
F32R = mybir.dt.float32r
ALU = mybir.AluOpType
ACT = mybir.ActivationFunctionType
AX = mybir.AxisListType

P = 128
SEQ, D, PLE, FF = 2048, 1024, 256, 4096
DK = D // P
TILES = SEQ // P
HEADS, HD = 8, 64
RW = HEADS * HD
PAIRS = RW // P
RWT = 14
ZT = 20
CH = 64
BUCKETS = 32
PADC = P
DECAY = float(np.exp(-0.5))
NEG = -1e30
NORM_EPS, LNX_EPS = 1e-6, 64e-5
EXT = 3 * P

PV = {}
_at = 0
for _n, _w in (("norm_mix_g", DK), ("norm_mlp_g", DK), ("mu", RWT), ("w0", PAIRS), ("a0", PAIRS),
               ("k_k", PAIRS), ("k_a", PAIRS), ("r_k", PAIRS)):
    PV[_n] = (_at, _at + _w)
    _at += _w
NPV = _at

LEVELS = 6
CC = {}
_at = 0
for _n, _w in (("ident", P), ("score_mask", 4 * P), ("level_mask", LEVELS * P), ("first_mask_t", P),
               ("chunk_start", PAIRS * P), ("head_of", PAIRS * HEADS), ("pair_sel", 2)):
    CC[_n] = (_at, _at + _w)
    _at += _w
NCC = _at


def shape_constants():
    c = np.zeros((P, NCC), np.float32)
    r, t = np.arange(P)[:, None], np.arange(P)[None, :]
    c[:, CC["ident"][0]:CC["ident"][1]] = r == t
    same = r // CH == t // CH
    strict, incl = same & (r < t), same & (r <= t)
    c[:, CC["score_mask"][0]:CC["score_mask"][1]] = np.concatenate([strict, incl, strict, incl], 1)
    lv = []
    for l in range(LEVELS):
        b = 1 << l
        lv.append((r // (2 * b) == t // (2 * b)) & ((r // b) % 2 == 1) & ((t // b) % 2 == 0))
    c[:, CC["level_mask"][0]:CC["level_mask"][1]] = np.concatenate(lv, 1)
    c[:, CC["first_mask_t"][0]:CC["first_mask_t"][1]] = lv[0].T
    c[:, CC["chunk_start"][0]:CC["chunk_start"][1]] = np.tile(np.arange(P) % CH != 0, PAIRS)[None]
    ho = np.zeros((P, PAIRS, HEADS), np.float32)
    for f in range(PAIRS):
        for h in range(2):
            ho[h * HD:(h + 1) * HD, f, 2 * f + h] = 1
    c[:, CC["head_of"][0]:CC["head_of"][1]] = ho.reshape(P, -1)
    c[:, CC["pair_sel"][0]:CC["pair_sel"][1]] = ho[:, 0, 0:2]
    return c


def head_rows():
    return np.repeat(np.eye(HEADS, dtype=np.float32), HD, axis=1)


def bucket_onehot():
    o = np.zeros((BUCKETS + 1, EXT), np.float32)
    for m in range(EXT):
        d = 2 * P - 1 - m
        if not 0 <= d < P:
            o[BUCKETS, m] = NEG
            continue
        half = BUCKETS // 2
        if d < half:
            b = d
        else:
            b = half + int(np.float32(np.log(np.float32(d) / np.float32(half))) / np.float32(np.log(P / half))
                           * np.float32(BUCKETS - half))
        o[min(b, BUCKETS - 1), m] = 1
    return o


def norm_and_project(nc, x, w_in, params, consts, zT):
    FC = 2
    CHUNKS = ZT // FC
    TB = 512
    NTB = SEQ // TB
    with ExitStack() as ctx:
        sb = lambda n, s, d=F32: ctx.enter_context(nc.sbuf_tensor(n, s, d))
        sem = lambda n: ctx.enter_context(nc.semaphore(n))
        hT_hi = sb("hT_hi", [P, DK, SEQ], F32R)
        hT_lo = sb("hT_lo", [P, DK, SEQ], F32R)
        par = sb("par_a", [P, NPV])
        ident = sb("ident_a", [P, P])
        ps = ctx.enter_context(nc.psum_tensor("ps_a", [P, 8, 512], F32))
        g = par[:, PV["norm_mix_g"][0]:PV["norm_mix_g"][1]]

        with ExitStack() as inner:
            sbi = lambda n, s, d=F32: inner.enter_context(nc.sbuf_tensor(n, s, d))
            xt = sbi("xt_a", [P, 2, D])
            junk = sbi("junk_a", [P, D])
            xn = sbi("xn_a", [P, 2, D])
            xg = sbi("xg_a", [P, 2, DK, P])
            ss = sbi("ss_a", [P, 2, 1])
            rs = sbi("rs_a", [P, 2, 1])
            eps = sbi("eps_a", [P, 1])
            const_in, x_in0, x_in1 = sem("const_in_a"), sem("x_in0_a"), sem("x_in1_a")
            x_in = [x_in0, x_in1]
            sumsq_done, rms_done, rstd_done = sem("sumsq_a"), sem("rms_a"), sem("rstd_a")
            xn_done, transposed, scaled, hi_done, lo_done = (
                sem("xn_a"), sem("tr_a"), sem("scaled_a"), sem("hi_a"), sem("lo_a"))
            eps_done = sem("eps_done_a")
            with nc.Block() as block:
                @block.sync
                def _(sp):
                    sp.dma_start(par[:, :], params).then_inc(const_in, 16)
                    sp.dma_start(ident[:, :], consts[:, CC["ident"][0]:CC["ident"][1]]).then_inc(const_in, 16)
                    with sp.Fori(0, TILES // 2) as it:
                        for s in range(2):
                            sp.wait_ge(xn_done, 2 * it + s + 1)
                            sp.dma_start(xt[:, s, :], x[bass.ds(it * (2 * P) + s * P, P), :]).then_inc(x_in[s], 16)

                @block.scalar
                def _(act):
                    act.wait_ge(eps_done, 1)
                    with act.Fori(0, TILES // 2) as it:
                        for s in range(2):
                            act.wait_ge(x_in[s], 16 * (it + 1))
                            act.wait_ge(rstd_done, 2 * it + s + 1)
                            nc.scalar.activation(junk[:, :], xt[:, s, :], ACT.Square,
                                                 accum_out=ss[:, s, :]).then_inc(sumsq_done, 1)
                            act.wait_ge(sumsq_done, 2 * it + s + 1)
                            nc.scalar.activation(rs[:, s, :], ss[:, s, :], ACT.Sqrt, scale=1.0 / D,
                                                 bias=eps[:, 0:1]).then_inc(rms_done, 1)
                            act.wait_ge(scaled, 2 * it + s + 3)
                            nc.scalar.activation(hT_hi[:, :, bass.ds(it * (2 * P) + s * P, P)], xg[:, s, :, :],
                                                 ACT.Copy).then_inc(hi_done, 1)

                @block.vector
                def _(dve):
                    nc.vector.memset(eps[:, :], NORM_EPS).then_inc(eps_done, 1)
                    for free in (xn_done, scaled, rstd_done):
                        dve.sem_inc(free, 2)
                    dve.wait_ge(const_in, 32)
                    with dve.Fori(0, TILES // 2) as it:
                        for s in range(2):
                            n = 2 * it + s
                            dve.wait_ge(rms_done, n + 1)
                            nc.vector.reciprocal(rs[:, s, :], rs[:, s, :]).then_inc(rstd_done, 1)
                            dve.wait_ge(rstd_done, n + 3)
                            dve.wait_ge(transposed, n + 1)
                            nc.vector.tensor_scalar(xn[:, s, :], xt[:, s, :], rs[:, s, :], None,
                                                    ALU.mult).then_inc(xn_done, 1)
                            dve.wait_ge(transposed, n + 3)
                            nc.vector.tensor_tensor(
                                xg[:, s, :, :], ps[:, 2 * s:2 * s + 2, :].rearrange("p b (k t) -> p (b k) t", t=P),
                                g.unsqueeze(2).broadcast_to([P, DK, P]), ALU.mult).then_inc(scaled, 1)
                            dve.wait_ge(hi_done, n + 1)
                            cols = bass.ds(it * (2 * P) + s * P, P)
                            nc.vector.tensor_tensor(hT_lo[:, :, cols], xg[:, s, :, :],
                                                    hT_hi[:, :, cols].bitcast(F32), ALU.subtract).then_inc(lo_done, 1)

                @block.tensor
                def _(pe):
                    pe.sem_inc(transposed, 2)
                    pe.wait_ge(const_in, 32)
                    with pe.Fori(0, TILES // 2) as it:
                        for s in range(2):
                            n = 2 * it + s
                            pe.wait_ge(xn_done, n + 3)
                            pe.wait_ge(scaled, n + 1)
                            for k in range(DK):
                                last = nc.tensor.transpose(ps[:, 2 * s + k // 4, (k % 4) * P:(k % 4 + 1) * P],
                                                           xn[:, s, k * P:(k + 1) * P], ident[:, :])
                            last.then_inc(transposed, 1)

        with ExitStack() as inner:
            sbi = lambda n, s, d=F32: inner.enter_context(nc.sbuf_tensor(n, s, d))
            raw = sbi("wraw_a", [P, 2, DK, FC * P])
            w_hi = sbi("whi_a", [P, 2, DK, FC * P], F32R)
            w_lo = sbi("wlo_a", [P, 2, DK, FC * P], F32R)
            zo = sbi("zo_a", [P, 2, SEQ])
            zero = sbi("zero_a", [P, PADC])
            raw_in = [sem("raw_in0_a"), sem("raw_in1_a")]
            passed = sem("passed_a")
            w_hi_done, w_lo_done, w_used = sem("w_hi_a"), sem("w_lo_a"), sem("w_used_a")
            z_full, z_out, stored, pad_done, zero_done = (
                sem("z_full_a"), sem("z_out_a"), [sem("zst0_a"), sem("zst1_a")], sem("pad_a"), sem("zero_done_a"))
            with nc.Block() as block:
                @block.sync
                def _(sp):
                    sp.wait_ge(zero_done, 1)
                    sp.dma_start(zT[:, :, 0:PADC].rearrange("f p t -> p f t"),
                                 zero[:, :].unsqueeze(1).broadcast_to([P, ZT, PADC])).then_inc(pad_done, 16)
                    with sp.Fori(0, CHUNKS // 2) as it:
                        for s in range(2):
                            sp.wait_ge(w_lo_done, 2 * it + s + 1)
                            sp.sem_inc(passed, 1)
                            sp.dma_start(raw[:, s, :, :], w_in[bass.ds(2 * it + s, 1)].rearrange(
                                "n p k f -> p (n k) f")).then_inc(raw_in[s], 16)
                    sp.wait_ge(pad_done, 16)

                @block.gpsimd
                def _(pool):
                    nc.gpsimd.memset(zero[:, :], 0.0).then_inc(zero_done, 1)
                    pool.sem_inc(w_lo_done, 2)
                    with pool.Fori(0, CHUNKS // 2) as it:
                        for s in range(2):
                            n = 2 * it + s
                            pool.wait_ge(raw_in[s], 16 * (it + 1))
                            pool.wait_ge(w_used, n + 1)
                            pool.sem_inc(passed, 1)
                            nc.gpsimd.tensor_scalar(w_hi[:, s, :, :], raw[:, s, :, :], 1.0, None,
                                                    ALU.mult).then_inc(w_hi_done, 1)
                            pool.wait_ge(w_hi_done, n + 1)
                            nc.gpsimd.tensor_tensor(w_lo[:, s, :, :], raw[:, s, :, :],
                                                    w_hi[:, s, :, :].bitcast(F32), ALU.subtract).then_inc(w_lo_done, 1)

                @block.tensor
                def _(pe):
                    pe.sem_inc(w_used, 1)
                    with pe.Fori(0, CHUNKS // 2) as it:
                        for s in range(2):
                            n = 2 * it + s
                            pe.wait_ge(w_lo_done, n + 3)
                            for f in range(FC):
                                for tb in range(NTB):
                                    bank = f * NTB + tb
                                    pe.wait_ge(z_out, 8 * n + bank + 1)
                                    tok = slice(tb * TB, (tb + 1) * TB)
                                    feat = slice(f * P, (f + 1) * P)
                                    for k in range(DK):
                                        mm = nc.tensor.matmul(ps[:, bank, :], w_hi[:, s, k, feat], hT_hi[:, k, tok],
                                                              start=(k == 0), stop=False)
                                        if bank == 0 and k == 0:
                                            mm.then_inc(w_used, 1)
                                        nc.tensor.matmul(ps[:, bank, :], w_hi[:, s, k, feat], hT_lo[:, k, tok],
                                                         start=False, stop=False)
                                        mm = nc.tensor.matmul(ps[:, bank, :], w_lo[:, s, k, feat], hT_hi[:, k, tok],
                                                              start=False, stop=(k == DK - 1))
                                    mm.then_inc(z_full, 1)

                @block.scalar
                def _(act):
                    act.sem_inc(z_out, 8)
                    for f in range(FC):
                        act.sem_inc(stored[f], 16)
                    with act.Fori(0, CHUNKS // 2) as it:
                        for s in range(2):
                            n = 2 * it + s
                            for f in range(FC):
                                act.wait_ge(stored[f], 32 * it + (16 * s + 16))
                                for tb in range(NTB):
                                    bank = f * NTB + tb
                                    act.wait_ge(z_full, 8 * n + bank + 1)
                                    nc.scalar.activation(zo[:, f, tb * TB:(tb + 1) * TB], ps[:, bank, :],
                                                         ACT.Copy).then_inc(z_out, 1)
                                act.wait_ge(z_out, 8 * n + f * NTB + NTB + 8)
                                act.dma_start(zT[bass.ds(it * (2 * FC) + s * FC + f, 1), :, PADC:].rearrange(
                                    "n p t -> p (n t)"), zo[:, f, :]).then_inc(stored[f], 16)
                    for f in range(FC):
                        act.wait_ge(stored[f], 16 * CHUNKS + 16)


BACK = {"A": 0, "B": 1, "C": 2}
PE_STEPS = {
    "A": ["v_keys", "score_a", "score_b", "lora_w", "lora_a", "kk_norm", "norm_rows", "probs_t_a", "probs_t_b", "pv_a",
          "bonus", "pv_b", "gate", "t_beta", "t_alpha", "t_kappa", "t_v"] + [f"rw_score{h}" for h in range(HEADS)],
    "B": ([f"first_t{q}" for q in range(2)]
          + [f"{s}{l}_{q}" for l in range(1, LEVELS - 1) for s in ("ax", "xax") for q in range(2)]
          + [f"ax{LEVELS - 1}_0", f"ax{LEVELS - 1}_1", "av", f"xax{LEVELS - 1}_0", f"xax{LEVELS - 1}_1", "u", "w_t", "sa0", "grow0", "sa1", "grow1", "y"]),
    "C": ["out_t"]}
DVE_STEPS = {
    "A": ["logit_a", "logit_b", "rowmax_a", "max_a", "negmax_a", "sink_gap_a", "rowmax_b", "max_b", "negmax_b",
          "sink_gap_b", "cum", "norm_floor", "norm_inv", "a_scale", "kk", "alpha", "denom_a", "inv_a",
          "probs_a", "beta", "denom_b", "inv_b", "probs_b", "kappa", "rho"]
         + [f"masked{h}" for h in range(HEADS)] + ["p_ends"],
    "B": (["a_first0", "x_first0", "a_first1", "x_first1"]
          + [f"{s}{l}_{q}" for l in range(1, LEVELS) for s in ("ax_masked", "x_next") for q in range(2)]
          + ["sa_add0", "grow_add0", "state0", "sa_add1", "grow_add1", "state1", "y_sum", "y_mean", "y_center"]),
    "C": ["y_sqsum", "y_inv", "y_norm"]}
ACT_STEPS = {
    "A": ["v_copy", "tanh_w", "sig_g", "sig_w", "sig_a", "kk_sq", "norm_sqrt", "p_inc", "p_inv", "exp_a",
          "exp_sink_a", "p_exc", "exp_b", "exp_sink_b", "pt_copy_a", "pt_copy_b", "bonus_copy", "att_copy", "gate_copy",
          "alpha_t", "beta_t", "kappa_t", "v_t", "rho_copy"],
    "B": ["av_copy", "gate_keep", "u_copy", "w_copy"],
    "C": ["y_rms", "out_copy"]}
POOL_STEPS = {
    "A": ["diff_low", "diff_mu_low", "zs_low", "diff", "diff_mu", "zs", "kk_raw", "cum_before", "kmod", "kk_a", "rk", "rk_rk"],
    "B": ["xt_mask0", "xt_first0", "xt_mask1", "xt_first1", "bonus_v"],
    "C": ["y_sq", "y_gain", "y_bias", "y_bonus", "y_gate"]}


def progress(stages, sems):
    stage_of = {label: st for st, steps in stages.items() for label in steps}
    at = {st: 0 for st in stages}

    def value(slot, st, steps_done):
        per = len(stages[st])
        tiles = slot[1] - BACK[st]
        if slot[0] is None:
            return min(tiles, TILES) * per + steps_done + 1
        return slot[0] * per + (tiles * per + steps_done + 1)

    def mark(label):
        st = stage_of[label]
        assert stages[st][at[st]] == label, (stages[st][at[st]], label)
        at[st] = (at[st] + 1) % len(stages[st])
        return sems[st]

    def done(slot, label):
        st = stage_of[label]
        return sems[st], value(slot, st, stages[st].index(label) + 1)

    def before(slot):
        return [(sems[st], value(slot, st, 0)) for st in stages if slot[0] is not None or slot[1] > BACK[st]]

    return mark, done, before


def mix_tokens(nc, zT, mixT, params, consts, hrows, onehot, rel_bias, sinks, w_up, a_up, g_up, lnx_g, lnx_b, skew):
    with ExitStack() as ctx:
        sb = lambda n, s, d=F32: ctx.enter_context(nc.sbuf_tensor(n, s, d))
        sem = lambda n: ctx.enter_context(nc.semaphore(n))
        ps = ctx.enter_context(nc.psum_tensor("ps_m", [P, 8, 512], F32))
        par, con = sb("par_m", [P, NPV]), sb("con_m", [P, NCC])
        hsel = sb("hsel_m", [HEADS, RW])
        oneh, relb = sb("oneh_m", [BUCKETS + 1, EXT]), sb("relb_m", [BUCKETS + 1, HEADS])
        ext = sb("ext_m", [P, 2, EXT])
        bias = sb("bias_m", [P, HEADS, 2 * P])
        sink = sb("sink_m", [P, HEADS])
        lora = sb("lora_m", [P, RW])
        gup = sb("gup_m", [P, RW])
        lng, lnb = sb("lng_m", [P, RW]), sb("lnb_m", [P, RW])
        one_minus_ka = sb("omka_m", [P, PAIRS])
        lnx_eps = sb("lnxeps_m", [P, 1])

        zr = sb("zr_m", [P, RWT, P + 1])
        zd, zs = sb("zd_m", [P, RWT, P]), sb("zs_m", [P, RWT, P])
        qT, kvT = sb("qT_m", [P, PAIRS, P]), sb("kvT_m", [P, 2, 2 * P])
        f4 = lambda n: sb(n, [P, PAIRS, P])
        kk_raw, kk_sq, sw, av, cum, cumx = f4("kkraw_m"), f4("kksq_m"), f4("sw_m"), f4("av_m"), f4("cum_m"), f4("cumx_m")
        p_inc, p_exc, p_inv = f4("pinc_m"), f4("pexc_m"), f4("pinv_m")
        ascale, kmod, kk, kka, betaT, kappaT, rk = (
            f4("ascale_m"), f4("kmod_m"), f4("kk_m"), f4("kka_m"), f4("betaT_m"), f4("kappaT_m"), f4("rk_m"))
        ar = sb("ar_m", [P, PAIRS, 2, P])
        th = sb("th_m", [HD, P])
        sg = sb("sg_m", [P, P])
        gate_new, gate = sb("gatenew_m", [P, RW]), sb("gate_m", [P, RW])
        rho = f4("rho_m")
        ends = sb("ends_m", [P, PAIRS, 2])
        nrm = sb("nrm_m", [HEADS, P])
        vk = sb("vk_m", [P, 2, P])
        bon = sb("bon_m", [P, HEADS])
        logit, pt = sb("logit_m", [P, HEADS, 2 * P]), sb("pt_m", [P, 2, 2, PAIRS, P])
        small = lambda n: sb(n, [P, HEADS])
        rowmax, negmax, gap, den, esink = small("rowmax_m"), small("negmax_m"), small("gap_m"), small("den_m"), small("esink_m")
        attT = sb("attT_m", [P, PAIRS, P])
        t4 = lambda n: sb(n, [P, RW])
        beta_t, kappa_t, alpha_t, v_t = t4("betat_m"), t4("kappat_m"), t4("alphat_m"), t4("vt_m")
        bm = sb("bm_m", [P, HEADS, 4, P])
        x_m, xt_m, ax = sb("x_m", [P, HEADS, P]), sb("xt_m", [P, HEADS, P]), sb("ax_m", [P, HEADS, P])
        avt, u_t, wT, sa = t4("avt_m"), t4("ut_m"), f4("wT_m"), t4("sa_m")
        state = sb("state_m", [P, 2, PAIRS, HD])
        grow = sb("grow_m", [P, PAIRS, HD])
        y, ysq, yb = t4("y_m"), t4("ysq_m"), t4("yb_m")
        ysum, yss = small("ysum_m"), small("yss_m")
        rwT = f4("rwT_m")

        col = lambda n: par[:, PV[n][0]:PV[n][1]]
        cst = lambda n: con[:, CC[n][0]:CC[n][1]]
        ident = cst("ident")
        score_mask = cst("score_mask").rearrange("p (a t) -> p a t", a=4)
        level_mask = cst("level_mask").rearrange("p (l t) -> p l t", l=LEVELS)
        head_of = cst("head_of").rearrange("p (f h) -> p f h", f=PAIRS)
        bank = lambda b: ps[:, b, :]
        over = lambda a, n: a.unsqueeze(2).broadcast_to([a.shape[0], a.shape[1], n])
        by_parity = lambda a: a.rearrange("p (f a v) -> p a f v", a=2, v=HD)
        four = lambda m: m.unsqueeze(1).broadcast_to([P, 4, P])

        c_in, b_ps, b_sb, b_st, b_rd, ready = sem("c_in_m"), sem("b_ps_m"), sem("b_sb_m"), sem("b_st_m"), sem("b_rd_m"), sem("ready_m")
        CIN = 13
        with nc.Block() as block:
            @block.sync
            def _(sp):
                for dst, src in ((par[:, :], params), (con[:, :], consts), (hsel[:, :], hrows), (oneh[:, :], onehot),
                                 (relb[0:BUCKETS, :], rel_bias), (sink[:, :], sinks.broadcast_to([P, HEADS])),
                                 (lora[0:HD, :], w_up), (lora[HD:P, :], a_up), (gup[:, :], g_up),
                                 (lng[:, :], lnx_g.broadcast_to([P, RW])), (lnb[:, :], lnx_b.broadcast_to([P, RW]))):
                    sp.dma_start(dst, src).then_inc(c_in, 16)
                for h in range(HEADS):
                    sp.wait_ge(b_sb, h + 1)
                    sp.dma_start(bass.AP(skew, h * P * EXT, [[EXT, P], [1, EXT]]), ext[:, h % 2, :]).then_inc(b_st, 16)
                sp.wait_ge(b_st, 16 * HEADS)
                sp.dma_start(bias[:, :, :], bass.AP(skew, P - 1, [[EXT - 1, P], [P * EXT, HEADS], [1, 2 * P]])).then_inc(b_rd, 16)
                sp.wait_ge(b_rd, 16)

            @block.vector
            def _(dve):
                nc.vector.memset(relb[BUCKETS:BUCKETS + 1, :], 1.0).then_inc(ready, 1)
                nc.vector.memset(lnx_eps[:, :], LNX_EPS)
                nc.vector.memset(state[:, :, :, :], 0.0)
                dve.wait_ge(c_in, 16 * 11)
                nc.vector.tensor_scalar(one_minus_ka[:, :], col("k_a"), -1.0, 1.0, ALU.mult, ALU.add)
                for h in range(HEADS):
                    dve.wait_ge(b_ps, h + 1)
                    if h >= 2:
                        dve.wait_ge(b_st, 16 * h)
                    nc.vector.tensor_copy(ext[:, h % 2, :], ps[:, h, 0:EXT]).then_inc(b_sb, 1)

            @block.tensor
            def _(pe):
                pe.wait_ge(c_in, 16 * 11)
                pe.wait_ge(ready, 1)
                for h in range(HEADS):
                    nc.tensor.matmul(ps[:, h, 0:EXT], relb[:, h:h + 1].broadcast_to([BUCKETS + 1, P]), oneh[:, :],
                                     start=True, stop=True).then_inc(b_ps, 1)

        counts = lambda eng, stages: {st: sem(f"{eng}_{st}_done_m") for st in stages}
        pe_counts, dve_counts, act_counts, pool_counts = (
            counts("pe", PE_STEPS), counts("dve", DVE_STEPS), counts("act", ACT_STEPS), counts("pool", POOL_STEPS))
        rw_in, qkv_in, rw_stored, att_stored = sem("rw_in_m"), sem("qkv_in_m"), sem("rwst_m"), sem("attst_m")
        first_logit = sem("first_logit_m")
        pmark, pdone, pbefore = progress(PE_STEPS, pe_counts)
        vmark, vdone, vbefore = progress(DVE_STEPS, dve_counts)
        amark, adone, abefore = progress(ACT_STEPS, act_counts)
        gmark, gdone, gbefore = progress(POOL_STEPS, pool_counts)
        groups = {"a": 0, "b": 1}
        score_banks = (0, 1, 3, 2)
        passed = sem("passed_m")

        def start(eng, counts_):
            for count in counts_.values():
                eng.sem_inc(count, 1)

        def slot_start(eng, s):
            for before in (pbefore, vbefore, abefore, gbefore):
                for count, value in before(s):
                    eng.wait_ge(count, value)
            eng.sem_inc(passed, 1)

        def tile(s, stage):
            return s[1] - BACK[stage] if s[0] is None else s[0] + (s[1] - BACK[stage])

        def all_slots(eng, slot):
            slot((None, 0), "A")
            slot((None, 1), "AB")
            with eng.Fori(0, TILES - 2) as it:
                slot((it, 2), "ABC")
            slot((None, TILES), "BC")
            slot((None, TILES + 1), "C")

        with nc.Block() as block:
            @block.sync
            def _(sp):
                def load_rw(i):
                    sp.dma_start(zr[:, :, :], zT[0:RWT, :, bass.ds(i * P + (PADC - 1), P + 1)].rearrange(
                        "f p t -> p f t")).then_inc(rw_in, 16)

                def load_qkv(i):
                    sp.dma_start(qT[:, :, :], zT[RWT:RWT + PAIRS, :, bass.ds(i * P + PADC, P)].rearrange(
                        "f p t -> p f t")).then_inc(qkv_in, 16)
                    sp.dma_start(kvT[:, :, :], zT[RWT + PAIRS:ZT, :, bass.ds(i * P, 2 * P)].rearrange(
                        "f p t -> p f t")).then_inc(qkv_in, 16)

                def slot(s, stages, last=False):
                    if "A" in stages and not last:
                        sp.wait_ge(*pdone(s, "score_b"))
                        sp.sem_inc(passed, 1)
                        load_qkv(tile(s, "A") + 1)
                        sp.wait_ge(*gdone(s, "zs"))
                        sp.sem_inc(passed, 1)
                        load_rw(tile(s, "A") + 1)
                    if "C" in stages:
                        sp.wait_ge(*adone(s, "out_copy"))
                        sp.sem_inc(passed, 1)
                        sp.dma_start(mixT[0:PAIRS, :, bass.ds(tile(s, "C") * P, P)].rearrange("f p t -> p f t"),
                                     rwT[:, :, :]).then_inc(rw_stored, 16)
                    if "A" in stages:
                        sp.wait_ge(*adone(s, "att_copy"))
                        sp.sem_inc(passed, 1)
                        sp.dma_start(mixT[PAIRS:, :, bass.ds(tile(s, "A") * P, P)].rearrange("f p t -> p f t"),
                                     attT[:, :, :]).then_inc(att_stored, 16)

                load_rw(0)
                load_qkv(0)
                slot((None, 0), "A")
                slot((None, 1), "AB")
                with sp.Fori(0, TILES - 3) as it:
                    slot((it, 2), "ABC")
                slot((None, TILES - 1), "ABC", last=True)
                slot((None, TILES), "BC")
                slot((None, TILES + 1), "C")
                sp.wait_ge(rw_stored, 16 * TILES + 16)
                sp.wait_ge(att_stored, 16 * TILES + 16)

            @block.tensor
            def _(pe):
                T = nc.tensor
                start(pe, pe_counts)
                head = lambda a, h: a[:, h * HD:(h + 1) * HD]

                def slot(s, stages):
                    A, B, C = (st in stages for st in "ABC")
                    after = lambda done, label: pe.wait_ge(*done(s, label))

                    def first_transposes():
                        before = (s[0], s[1] - 1)
                        for q in range(2):
                            pe.wait_ge(*vdone(before, f"masked{4 * q + 3}"))
                            if C and q:
                                pe.wait_ge(*vdone(before, "y_center"))
                            pe.sem_inc(passed, 1)
                            for j in range(4):
                                mm = T.transpose(ps[:, 4 + 2 * q, j * P:(j + 1) * P], bm[:, 4 * q + j, 0, :], ident)
                            mm.then_inc(pmark(f"first_t{q}"), 1)

                    def attention_scores():
                        pe.wait_ge(qkv_in, 32 * (tile(s, "A") + 1))
                        for b in range(2):
                            mm = T.transpose(ps[:, 0, b * P:(b + 1) * P], kvT[:, 1, b * P:(b + 1) * P], ident)
                        mm.then_inc(pmark("v_keys"), 1)
                        for g, kv in groups.items():
                            if g == "b":
                                after(adone, "v_copy")
                            rows = slice(kv * HD, (kv + 1) * HD)
                            for j in range(PAIRS):
                                mm = T.matmul(ps[:, 2 - 2 * kv + j // 2, (j % 2) * 2 * P:(j % 2 + 1) * 2 * P],
                                              qT[rows, j, :], kvT[rows, 0, :], start=True, stop=True)
                            mm.then_inc(pmark("score_" + g), 1)

                    def low_rank():
                        after(adone, "tanh_w")
                        after(vdone, "logit_a")
                        for f in range(PAIRS):
                            mm = T.matmul(ps[:, 2, f * P:(f + 1) * P], lora[0:HD, f * P:(f + 1) * P], th[:, :],
                                          start=True, stop=True)
                        mm.then_inc(pmark("lora_w"), 1)
                        for f in range(PAIRS):
                            mm = T.matmul(ps[:, 3, f * P:(f + 1) * P], lora[HD:P, f * P:(f + 1) * P], zs[HD:P, 12, :],
                                          start=True, stop=True)
                        mm.then_inc(pmark("lora_a"), 1)

                    def key_norms():
                        after(adone, "kk_sq")
                        after(vdone, "logit_b")
                        for f in range(PAIRS):
                            mm = T.matmul(ps[0:HEADS, 1, 0:P], head_of[:, f, :], kk_sq[:, f, :],
                                          start=(f == 0), stop=(f == PAIRS - 1))
                        mm.then_inc(pmark("kk_norm"), 1)

                    def norm_rows():
                        after(vdone, "norm_inv")
                        for f in range(PAIRS):
                            mm = T.matmul(ps[:, 1, f * P:(f + 1) * P], hsel[:, f * P:(f + 1) * P], nrm[:, :],
                                          start=True, stop=True)
                        mm.then_inc(pmark("norm_rows"), 1)

                    def turn_probs(g, kv):
                        after(vdone, "probs_" + g)
                        after(*((adone, "sig_a") if g == "a" else (vdone, "kk")))
                        for b in range(2):
                            for j in range(PAIRS):
                                mm = T.transpose(ps[:, 2 - 2 * kv + b, j * P:(j + 1) * P],
                                                 logit[:, 4 * kv + j, b * P:(b + 1) * P], ident)
                        mm.then_inc(pmark("probs_t_" + g), 1)

                    def probs_by_values(g, kv):
                        after(adone, "pt_copy_" + g)
                        for b in range(2):
                            mm = T.matmul(ps[kv * HD:(kv + 1) * HD, 2, :], vk[:, b, kv * HD:(kv + 1) * HD],
                                          pt[:, kv, b, :, :], start=(b == 0), stop=(b == 1))
                        mm.then_inc(pmark("pv_" + g), 1)

                    def tokens_major(name, bank_, src, made):
                        after(*made)
                        if name == "v":
                            after(adone, "att_copy")
                        if name == "alpha":
                            after(adone, "bonus_copy")
                        for f in range(PAIRS):
                            mm = T.transpose(ps[:, bank_, f * P:(f + 1) * P], src[:, f, :], ident)
                        mm.then_inc(pmark("t_" + name), 1)

                    def delta_scores():
                        after(vdone, "rho")
                        for h in range(HEADS):
                            rows, f, b = slice((h % 2) * HD, (h % 2 + 1) * HD), h // 2, score_banks[h % 4]
                            after(*((vdone, f"masked{h - 4}") if h >= 4 else
                                    (adone, ("beta_t", "kappa_t", "alpha_t", "v_t")[h])))
                            rhs = ar[rows, f, :, :]
                            T.matmul(ps[:, b, 0:2 * P], betaT[rows, f, :], rhs, start=True, stop=True)
                            T.matmul(ps[:, b, 2 * P:], kappaT[rows, f, :], rhs, start=True, stop=True).then_inc(
                                pmark(f"rw_score{h}"), 1)

                    def bonus():
                        after(gdone, "rk_rk")
                        for f in range(PAIRS):
                            mm = T.matmul(ps[:, 3, 2 * f:2 * f + 2], rk[:, f, :], cst("pair_sel"), start=True, stop=True)
                        mm.then_inc(pmark("bonus"), 1)

                    def output_gate():
                        after(adone, "sig_g")
                        T.matmul(bank(7), sg[:, :], gup[:, :], start=True, stop=True).then_inc(pmark("gate"), 1)

                    def level_ax(l):
                        for q in range(2):
                            after(vdone, f"x_first{q}" if l == 1 else f"x_next{l - 1}_{q}")
                            for j in range(4):
                                h = 4 * q + j
                                mm = T.matmul(ps[:, 4 + 2 * q, j * P:(j + 1) * P], bm[:, h, 0, :], x_m[:, h, :],
                                              start=True, stop=True)
                            mm.then_inc(pmark(f"ax{l}_{q}"), 1)

                    def level_xax(l):
                        for q in range(2):
                            after(vdone, f"ax_masked{l}_{q}")
                            if l == 1:
                                after(gdone, f"xt_first{q}")
                            for j in range(4):
                                h = 4 * q + j
                                if l < LEVELS - 1:
                                    T.matmul(ps[:, 5 + 2 * q, j * P:(j + 1) * P], xt_m[:, h, :], ax[:, h, :],
                                             start=True, stop=True)
                                mm = T.matmul(ps[:, 4 + 2 * q, j * P:(j + 1) * P], ax[:, h, :], xt_m[:, h, :],
                                              start=True, stop=True)
                            mm.then_inc(pmark(f"xax{l}_{q}"), 1)

                    def a_by_v():
                        for h in range(HEADS):
                            mm = T.matmul(head(bank(5), h), bm[:, h, 2, :], head(v_t, h), start=True, stop=True)
                        mm.then_inc(pmark("av"), 1)

                    def u_and_w():
                        after(adone, "av_copy")
                        after(vdone, f"x_next{LEVELS - 1}_1")
                        if C:
                            after(adone, "out_copy")
                        for h in range(HEADS):
                            mm = T.matmul(head(bank(7), h), xt_m[:, h, :], head(avt, h), start=True, stop=True)
                        mm.then_inc(pmark("u"), 1)
                        for h in range(HEADS):
                            rows, f = slice((h % 2) * HD, (h % 2 + 1) * HD), h // 2
                            mm = T.matmul(ps[rows, 4, f * P:(f + 1) * P], head(alpha_t, h), xt_m[:, h, :],
                                          start=True, stop=True)
                        mm.then_inc(pmark("w_t"), 1)

                    def state_apply(c):
                        tok = slice(c * CH, (c + 1) * CH)
                        after(*((adone, "w_copy") if c == 0 else (vdone, "state0")))
                        pe.sem_inc(passed, 1)
                        for h in range(HEADS):
                            rows, f = slice((h % 2) * HD, (h % 2 + 1) * HD), h // 2
                            mm = T.matmul(ps[tok, 5 + h % 2, f * HD:(f + 1) * HD], wT[rows, f, tok], state[rows, c, f, :],
                                          start=True, stop=True)
                        mm.then_inc(pmark(f"sa{c}"), 1)

                    def state_grow(c):
                        tok = slice(c * CH, (c + 1) * CH)
                        after(vdone, f"sa_add{c}")
                        pe.sem_inc(passed, 1)
                        for h in range(HEADS):
                            rows, f = slice((h % 2) * HD, (h % 2 + 1) * HD), h // 2
                            dst = ps[rows, (7, 4)[c], f * HD:(f + 1) * HD]
                            T.matmul(dst, head(kappa_t[tok, :], h), head(v_t[tok, :], h), start=True, stop=False)
                            mm = T.matmul(dst, head(beta_t[tok, :], h), head(sa[tok, :], h), start=False, stop=True)
                        mm.then_inc(pmark(f"grow{c}"), 1)

                    def outputs():
                        for h in range(HEADS):
                            rows, f = slice((h % 2) * HD, (h % 2 + 1) * HD), h // 2
                            dst = ps[:, 5 + h % 2, f * HD:(f + 1) * HD]
                            T.matmul(dst, bm[:, h, 3, :], head(v_t, h), start=(h < 2), stop=False)
                            T.matmul(dst, bm[:, h, 1, :], head(sa, h), start=False, stop=False)
                        for h in range(HEADS):
                            rows, f = slice((h % 2) * HD, (h % 2 + 1) * HD), h // 2
                            for c in range(2):
                                tok = slice(c * CH, (c + 1) * CH)
                                mm = T.matmul(ps[tok, 5 + h % 2, f * HD:(f + 1) * HD], rho[rows, f, tok], state[rows, c, f, :],
                                              start=False, stop=(f == PAIRS - 1))
                        mm.then_inc(pmark("y"), 1)

                    def turn_out():
                        after(gdone, "y_gate")
                        if B:
                            after(vdone, f"x_next{LEVELS - 2}_1")
                        for f in range(PAIRS):
                            mm = T.transpose(ps[:, 7, f * P:(f + 1) * P], y[:, f * P:(f + 1) * P], ident)
                        mm.then_inc(pmark("out_t"), 1)

                    if B: first_transposes()
                    slot_start(pe, s)
                    if A: attention_scores()
                    if B: level_ax(1); level_xax(1)
                    if A: low_rank()
                    if B: level_ax(2); level_xax(2)
                    if A: key_norms()
                    if B: level_ax(3); level_xax(3)
                    if A: norm_rows()
                    if B: level_ax(4); level_xax(4); level_ax(5); a_by_v(); level_xax(5)
                    if A: turn_probs("a", 0)
                    if C: turn_out()
                    if B: u_and_w()
                    if A: turn_probs("b", 1)
                    if B: state_apply(0)
                    if A: probs_by_values("a", 0)
                    if B: state_grow(0)
                    if A: bonus()
                    if B: state_apply(1)
                    if A: probs_by_values("b", 1)
                    if B: state_grow(1)
                    if A:
                        output_gate()
                        tokens_major("beta", 0, betaT[:, :, :], (vdone, "beta"))
                        tokens_major("alpha", 3, ar[:, :, 0, :], (vdone, "alpha"))
                        tokens_major("kappa", 1, kappaT[:, :, :], (vdone, "kappa"))
                    if B: outputs()
                    if A:
                        tokens_major("v", 2, zs[:, 8:12, :], (gdone, "zs"))
                        delta_scores()

                all_slots(pe, slot)

            @block.vector
            def _(dve):
                V = nc.vector
                start(dve, dve_counts)

                def slot(s, stages):
                    A, B, C = (st in stages for st in "ABC")
                    after = lambda done, label: dve.wait_ge(*done(s, label))
                    own = lambda label: after(vdone, label)
                    r = zs[:, 0:4, :]
                    heads = lambda q: slice(4 * q, 4 * q + 4)
                    in_bank = lambda b: bank(b).rearrange("p (h t) -> p h t", h=4)

                    def first_inverse(q):
                        hs = heads(q)
                        after(pdone, f"first_t{q}")
                        V.tensor_tensor(x_m[:, hs, :], in_bank(4 + 2 * q), four(level_mask[:, 0, :]),
                                        ALU.mult).then_inc(vmark(f"a_first{q}"), 1)
                        own(f"a_first{q}")
                        V.tensor_tensor(x_m[:, hs, :], x_m[:, hs, :], four(ident), ALU.add).then_inc(vmark(f"x_first{q}"), 1)

                    def mask_ax(l):
                        for q in range(2):
                            after(pdone, f"ax{l}_{q}")
                            V.tensor_tensor(ax[:, heads(q), :], in_bank(4 + 2 * q), four(level_mask[:, l, :]),
                                            ALU.mult).then_inc(vmark(f"ax_masked{l}_{q}"), 1)

                    def next_inverse(l):
                        for q in range(2):
                            hs = heads(q)
                            after(pdone, f"xax{l}_{q}")
                            if l < LEVELS - 1:
                                V.tensor_tensor(x_m[:, hs, :], in_bank(5 + 2 * q), x_m[:, hs, :], ALU.add)
                            V.tensor_tensor(xt_m[:, hs, :], in_bank(4 + 2 * q), xt_m[:, hs, :],
                                            ALU.add).then_inc(vmark(f"x_next{l}_{q}"), 1)

                    def logits(g, kv):
                        hs = heads(kv)
                        after(pdone, "score_" + g)
                        o = V.scalar_tensor_tensor(logit[:, hs, :].rearrange("p h t -> p (h t)"),
                                                   ps[:, 2 - 2 * kv:4 - 2 * kv, :].rearrange("p b t -> p (b t)"), HD ** -0.5,
                                                   bias[:, hs, :].rearrange("p h t -> p (h t)"), ALU.mult, ALU.add)
                        if s[0] is None and s[1] == 0:
                            o.then_inc(first_logit, 1)
                            dve.wait_ge(first_logit, kv + 1)
                            o = V.tensor_scalar(logit[:, hs, 0:P], logit[:, hs, 0:P], NEG, None, ALU.add)
                        o.then_inc(vmark("logit_" + g), 1)

                    def maxima(g, kv):
                        hs = heads(kv)
                        own("logit_" + g)
                        V.tensor_reduce(rowmax[:, hs], logit[:, hs, :], AX.X, ALU.max).then_inc(vmark("rowmax_" + g), 1)
                        own("rowmax_" + g)
                        V.tensor_tensor(rowmax[:, hs], rowmax[:, hs], sink[:, hs], ALU.max).then_inc(vmark("max_" + g), 1)
                        own("max_" + g)
                        V.tensor_scalar(negmax[:, hs], rowmax[:, hs], -1.0, None, ALU.mult).then_inc(vmark("negmax_" + g), 1)
                        V.tensor_tensor(gap[:, hs], sink[:, hs], rowmax[:, hs], ALU.subtract).then_inc(vmark("sink_gap_" + g), 1)

                    def probabilities(g, kv):
                        hs = heads(kv)
                        after(adone, "exp_sink_" + g)
                        V.tensor_tensor(den[:, hs], den[:, hs], esink[:, hs], ALU.add).then_inc(vmark("denom_" + g), 1)
                        own("denom_" + g)
                        V.reciprocal(den[:, hs], den[:, hs]).then_inc(vmark("inv_" + g), 1)
                        own("inv_" + g)
                        V.tensor_tensor(logit[:, hs, :], logit[:, hs, :], over(den[:, hs], 2 * P), ALU.mult).then_inc(vmark("probs_" + g), 1)

                    def decay_sums():
                        after(adone, "sig_w")
                        V.tensor_tensor_scan(cum[:, :, :].rearrange("p f t -> p (f t)"), cst("chunk_start"),
                                             sw[:, :, :].rearrange("p f t -> p (f t)"), 0.0, ALU.mult, ALU.add).then_inc(vmark("cum"), 1)
                        after(adone, "norm_sqrt")
                        V.tensor_scalar(nrm[:, :], nrm[:, :], 1e-12, None, ALU.max).then_inc(vmark("norm_floor"), 1)
                        own("norm_floor")
                        V.reciprocal(nrm[:, :], nrm[:, :]).then_inc(vmark("norm_inv"), 1)

                    def key_scales():
                        after(adone, "sig_a")
                        for f in range(PAIRS):
                            o = V.tensor_scalar(ascale[:, f, :], av[:, f, :], col("k_a")[:, f:f + 1], one_minus_ka[:, f:f + 1],
                                                ALU.mult, ALU.add)
                        o.then_inc(vmark("a_scale"), 1)

                    def normal_keys():
                        after(pdone, "norm_rows")
                        V.tensor_tensor(kk[:, :, :], bank(1).rearrange("p (f t) -> p f t", t=P), kk_raw[:, :, :],
                                        ALU.mult).then_inc(vmark("kk"), 1)
                        own("kk")
                        after(adone, "p_exc")
                        V.scalar_tensor_tensor(ar[:, :, 0, :], kk[:, :, :], -1.0, p_exc[:, :, :], ALU.mult, ALU.mult).then_inc(vmark("alpha"), 1)

                    def beta():
                        after(gdone, "kk_a")
                        V.tensor_tensor(betaT[:, :, :], kka[:, :, :], p_inv[:, :, :], ALU.mult).then_inc(vmark("beta"), 1)

                    def kappa_rho():
                        after(gdone, "kmod")
                        V.tensor_tensor(kappaT[:, :, :], kmod[:, :, :], p_inv[:, :, :], ALU.mult).then_inc(vmark("kappa"), 1)
                        V.tensor_tensor(ar[:, :, 1, :], r, p_inc[:, :, :], ALU.mult).then_inc(vmark("rho"), 1)

                    def masks(hs):
                        for h in hs:
                            after(pdone, f"rw_score{h}")
                            V.tensor_tensor(bm[:, h, :, :], ps[:, score_banks[h % 4], :].rearrange("p (a t) -> p a t", a=4),
                                            score_mask, ALU.mult).then_inc(vmark(f"masked{h}"), 1)

                    def chunk(c):
                        tok = slice(c * CH, (c + 1) * CH)
                        after(pdone, f"sa{c}")
                        V.tensor_tensor(by_parity(sa[tok, :]), ps[tok, 5:7, 0:PAIRS * HD].rearrange("p a (f v) -> p a f v", f=PAIRS),
                                        by_parity(u_t[tok, :]), ALU.add).then_inc(vmark(f"sa_add{c}"), 1)
                        after(pdone, f"grow{c}")
                        V.tensor_tensor(grow[:, :, :], ps[:, (7, 4)[c], 0:PAIRS * HD].rearrange("p (f v) -> p f v", f=PAIRS),
                                        state[:, c, :, :], ALU.add).then_inc(vmark(f"grow_add{c}"), 1)
                        own(f"grow_add{c}")
                        if c == 1:
                            after(pdone, "y")
                        V.tensor_tensor(state[:, 1 - c, :, :], grow[:, :, :],
                                        ends[:, :, c:c + 1].broadcast_to([P, PAIRS, HD]), ALU.mult).then_inc(vmark(f"state{c}"), 1)

                    y_ps = ps[:, 5:7, 0:PAIRS * HD].rearrange("p a (f v) -> p f a v", f=PAIRS)
                    y3 = lambda a: a[:, :].rearrange("p (h v) -> p h v", h=HEADS)

                    def means():
                        V.tensor_reduce(ysum[:, :].rearrange("p (f a) -> p f a", a=2), y_ps, AX.X, ALU.add).then_inc(vmark("y_sum"), 1)
                        own("y_sum")
                        V.tensor_scalar(ysum[:, :], ysum[:, :], 1.0 / HD, None, ALU.mult).then_inc(vmark("y_mean"), 1)

                    def center():
                        own("y_mean")
                        if C:
                            after(pdone, "out_t")
                        V.tensor_tensor(y[:, :].rearrange("p (f a v) -> p f a v", a=2, v=HD), y_ps,
                                        ysum[:, :].rearrange("p (f a) -> p f a", a=2).unsqueeze(3).broadcast_to([P, PAIRS, 2, HD]),
                                        ALU.subtract).then_inc(vmark("y_center"), 1)

                    def variances():
                        after(gdone, "y_sq")
                        V.tensor_reduce(yss[:, :], y3(ysq), AX.X, ALU.add).then_inc(vmark("y_sqsum"), 1)

                    def normalise():
                        after(adone, "y_rms")
                        V.reciprocal(yss[:, :], yss[:, :]).then_inc(vmark("y_inv"), 1)
                        own("y_inv")
                        V.tensor_tensor(y3(y), y3(y), over(yss[:, :], HD), ALU.mult).then_inc(vmark("y_norm"), 1)

                    slot_start(dve, s)
                    if B: first_inverse(0); first_inverse(1)
                    if A: logits("a", 0)
                    if B: mask_ax(1)
                    if A: logits("b", 1)
                    if B: next_inverse(1)
                    if A: maxima("a", 0)
                    if B: mask_ax(2)
                    if C: variances()
                    if B: next_inverse(2)
                    if A: maxima("b", 1)
                    if B: mask_ax(3)
                    if A: decay_sums()
                    if B: next_inverse(3)
                    if C: normalise()
                    if B: mask_ax(4)
                    if A: key_scales()
                    if B: next_inverse(4)
                    if A: normal_keys()
                    if B: mask_ax(5)
                    if A: probabilities("a", 0)
                    if B: next_inverse(5)
                    if A: beta(); probabilities("b", 1); kappa_rho()
                    if B: chunk(0); chunk(1); means()
                    if A: masks(range(2))
                    if B: center()
                    if A:
                        masks(range(2, HEADS))
                        V.tensor_copy(ends[:, :, :], p_inc[:, :, :].rearrange("p f (c t) -> p f c t", c=2)[:, :, :, CH - 1]).then_inc(
                            vmark("p_ends"), 1)

                all_slots(dve, slot)

            @block.gpsimd
            def _(pool):
                G = nc.gpsimd
                start(pool, pool_counts)

                def slot(s, stages):
                    after = lambda done, label: pool.wait_ge(*done(s, label))
                    slot_start(pool, s)
                    A, B, C = (st in stages for st in "ABC")
                    own = lambda label: after(gdone, label)
                    r, k = zs[:, 0:4, :], zs[:, 4:8, :]

                    def shift(tiles, suffix):
                        now, d = zr[:, tiles, 1:P + 1], zd[:, tiles, :]
                        G.tensor_tensor(d, zr[:, tiles, 0:P], now, ALU.subtract).then_inc(gmark("diff" + suffix), 1)
                        own("diff" + suffix)
                        G.tensor_tensor(d, d, over(col("mu")[:, tiles], P), ALU.mult).then_inc(gmark("diff_mu" + suffix), 1)
                        own("diff_mu" + suffix)
                        G.tensor_tensor(zs[:, tiles, :], d, now, ALU.add).then_inc(gmark("zs" + suffix), 1)

                    def first_transposed_inverse(q):
                        hs = slice(4 * q, 4 * q + 4)
                        G.tensor_tensor(xt_m[:, hs, :], bm[:, hs, 0, :], four(cst("first_mask_t")), ALU.mult).then_inc(gmark(f"xt_mask{q}"), 1)
                        own(f"xt_mask{q}")
                        G.tensor_tensor(xt_m[:, hs, :], xt_m[:, hs, :], four(ident), ALU.add).then_inc(gmark(f"xt_first{q}"), 1)

                    if B: first_transposed_inverse(0)
                    if A:
                        pool.wait_ge(rw_in, 16 * (tile(s, "A") + 1))
                        pool.sem_inc(passed, 1)
                        shift(slice(12, 14), "_low")
                    if B: first_transposed_inverse(1)
                    if C: G.tensor_tensor(ysq[:, :], y[:, :], y[:, :], ALU.mult).then_inc(gmark("y_sq"), 1)
                    if A:
                        shift(slice(0, 12), "")
                        own("zs")
                        G.tensor_tensor(kk_raw[:, :, :], k, over(col("k_k"), P), ALU.mult).then_inc(gmark("kk_raw"), 1)
                        after(vdone, "cum")
                        G.tensor_tensor(cumx[:, :, :], cum[:, :, :], sw[:, :, :], ALU.subtract).then_inc(gmark("cum_before"), 1)
                    if C:
                        after(vdone, "y_norm")
                        G.tensor_tensor(y[:, :], y[:, :], lng[:, :], ALU.mult).then_inc(gmark("y_gain"), 1)
                    if A:
                        after(vdone, "a_scale")
                        G.tensor_tensor(kmod[:, :, :], k, ascale[:, :, :], ALU.mult).then_inc(gmark("kmod"), 1)
                    if C:
                        own("y_gain")
                        G.tensor_tensor(y[:, :], y[:, :], lnb[:, :], ALU.add).then_inc(gmark("y_bias"), 1)
                        own("y_bias")
                        G.tensor_tensor(y[:, :], y[:, :], yb[:, :], ALU.add).then_inc(gmark("y_bonus"), 1)
                    if A:
                        after(vdone, "kk")
                        G.tensor_tensor(kka[:, :, :], kk[:, :, :], av[:, :, :], ALU.mult).then_inc(gmark("kk_a"), 1)
                    if C:
                        own("y_bonus")
                        G.tensor_tensor(y[:, :], y[:, :], gate[:, :], ALU.mult).then_inc(gmark("y_gate"), 1)
                    if A:
                        own("kmod")
                        G.tensor_tensor(rk[:, :, :], r, kmod[:, :, :], ALU.mult).then_inc(gmark("rk"), 1)
                        own("rk")
                        G.tensor_tensor(rk[:, :, :], rk[:, :, :], over(col("r_k"), P), ALU.mult).then_inc(gmark("rk_rk"), 1)
                    if B:
                        G.tensor_tensor(yb[:, :].rearrange("p (h v) -> p h v", h=HEADS), v_t[:, :].rearrange("p (h v) -> p h v", h=HEADS),
                                        over(bon[:, :], HD), ALU.mult).then_inc(gmark("bonus_v"), 1)

                all_slots(pool, slot)

            @block.scalar
            def _(act):
                S = nc.scalar
                start(act, act_counts)
                for count in (att_stored, rw_stored):
                    act.sem_inc(count, 16)

                def slot(s, stages):
                    A, B, C = (st in stages for st in "ABC")
                    after = lambda done, label: act.wait_ge(*done(s, label))

                    def activations():
                        after(pdone, "v_keys")
                        S.activation(vk[:, :, :], ps[:, 0, 0:2 * P].rearrange("p (b t) -> p b t", b=2), ACT.Copy).then_inc(amark("v_copy"), 1)
                        after(gdone, "zs_low")
                        S.activation(th[:, :], zs[0:HD, 12, :], ACT.Tanh).then_inc(amark("tanh_w"), 1)
                        S.activation(sg[:, :], zs[:, 13, :], ACT.Sigmoid).then_inc(amark("sig_g"), 1)
                        for label, made, dst, bank_, base in (("sig_w", "lora_w", sw, 2, "w0"), ("sig_a", "lora_a", av, 3, "a0")):
                            after(pdone, made)
                            for f in range(PAIRS):
                                o = S.activation(dst[:, f, :], ps[:, bank_, f * P:(f + 1) * P], ACT.Sigmoid, bias=col(base)[:, f:f + 1])
                            o.then_inc(amark(label), 1)
                        after(gdone, "kk_raw")
                        S.activation(kk_sq[:, :, :], kk_raw[:, :, :], ACT.Square).then_inc(amark("kk_sq"), 1)

                    def roots():
                        if C:
                            after(vdone, "y_sqsum")
                            S.activation(yss[:, :], yss[:, :], ACT.Sqrt, scale=1.0 / HD, bias=lnx_eps[:, 0:1]).then_inc(amark("y_rms"), 1)
                        if A:
                            after(pdone, "kk_norm")
                            S.activation(nrm[:, :], ps[0:HEADS, 1, 0:P], ACT.Sqrt).then_inc(amark("norm_sqrt"), 1)

                    def exponentials():
                        after(vdone, "cum")
                        S.activation(p_inc[:, :, :], cum[:, :, :], ACT.Exp, scale=-DECAY).then_inc(amark("p_inc"), 1)
                        S.activation(p_inv[:, :, :], cum[:, :, :], ACT.Exp, scale=DECAY).then_inc(amark("p_inv"), 1)
                        for g, kv in groups.items():
                            if g == "b":
                                after(gdone, "cum_before")
                                S.activation(p_exc[:, :, :], cumx[:, :, :], ACT.Exp, scale=-DECAY).then_inc(amark("p_exc"), 1)
                            hs = slice(4 * kv, 4 * kv + 4)
                            after(vdone, "sink_gap_" + g)
                            for h in range(4 * kv, 4 * kv + 4):
                                o = S.activation(logit[:, h, :], logit[:, h, :], ACT.Exp, bias=negmax[:, h:h + 1],
                                                 accum_out=den[:, h:h + 1])
                            o.then_inc(amark("exp_" + g), 1)
                            S.activation(esink[:, hs], gap[:, hs], ACT.Exp).then_inc(amark("exp_sink_" + g), 1)

                    def copy_probs(g, kv):
                        after(pdone, "probs_t_" + g)
                        S.activation(pt[:, kv, :, :, :].rearrange("p b j t -> p (b j t)"),
                                     ps[:, 2 - 2 * kv:4 - 2 * kv, :].rearrange("p b t -> p (b t)"), ACT.Copy).then_inc(amark("pt_copy_" + g), 1)

                    def copy_attention():
                        after(pdone, "pv_b")
                        act.wait_ge(att_stored, 16 * tile(s, "A") + 16)
                        S.activation(attT[:, :, :], bank(2).rearrange("p (j t) -> p j t", j=PAIRS), ACT.Copy).then_inc(amark("att_copy"), 1)

                    def copy_tokens_major():
                        for name, dst, bank_, used in (("alpha", alpha_t, 3, "w_t"), ("beta", beta_t, 0, "grow1"),
                                                       ("kappa", kappa_t, 1, "grow1"), ("v", v_t, 2, "y")):
                            after(pdone, "t_" + name)
                            if B:
                                act.sem_inc(passed, 1)
                                after(pdone, used)
                                if name == "v":
                                    after(gdone, "bonus_v")
                            S.activation(dst[:, :], bank(bank_), ACT.Copy).then_inc(amark(name + "_t"), 1)
                        after(vdone, "rho")
                        S.activation(rho[:, :, :], ar[:, :, 1, :], ACT.Copy).then_inc(amark("rho_copy"), 1)

                    def copy_out():
                        after(pdone, "out_t")
                        act.wait_ge(rw_stored, 16 * tile(s, "C") + 16)
                        S.activation(rwT[:, :, :], bank(7).rearrange("p (f t) -> p f t", f=PAIRS), ACT.Copy).then_inc(amark("out_copy"), 1)

                    def keep_gate():
                        if C:
                            after(gdone, "y_gate")
                        S.activation(gate[:, :], gate_new[:, :], ACT.Copy).then_inc(amark("gate_keep"), 1)

                    def copy(label, made, dst, src):
                        after(pdone, made)
                        S.activation(dst, src, ACT.Copy).then_inc(amark(label), 1)

                    slot_start(act, s)
                    if A: activations()
                    roots()
                    if A: exponentials()
                    if B: copy("av_copy", "av", avt[:, :], bank(5))
                    if A: copy_probs("a", 0)
                    if C: copy_out()
                    if B:
                        keep_gate()
                        copy("u_copy", "u", u_t[:, :], bank(7))
                        copy("w_copy", "w_t", wT[:, :, :], bank(4).rearrange("p (f t) -> p f t", f=PAIRS))
                    if A:
                        copy_probs("b", 1)
                        if B:
                            after(gdone, "bonus_v")
                        copy("bonus_copy", "bonus", bon[:, :], ps[:, 3, 0:HEADS])
                        copy_attention()
                        copy("gate_copy", "gate", gate_new[:, :], bank(7))
                        copy_tokens_major()

                all_slots(act, slot)


HG, HGD = 4, FF // 4
TBK = 512
BLOCKS = SEQ // TBK
NJ = [(n, j) for n in range(2) for j in range(4)]
each = lambda s, ns=(0, 1): [f"{s}{n}_{j}" for n in ns for j in range(4)]
ks_of = lambda s, ks: [f"{s}{k}" for k in ks]
PE_L = (each("out") + ["pt0", "pt1"] + ks_of("ut", range(DK)), each("up") + each("down"),
        each("ple", [0]) + ks_of("xt", range(4)) + each("ple", [1]) + ks_of("xt", range(4, DK)) + each("gate"))
ACT_L = (["p_hi0", "p_hi1"] + [f"{s}{j}" for j in range(4) for s in ("ss", "rms")] + ks_of("u_hi", range(DK)),
         [f"{s}{n}_{j}" for n, j in NJ for s in ("relu", "h_hi")],
         each("e_copy", [0]) + ks_of("x2_hi", range(4)) + each("e_copy", [1]) + ks_of("x2_hi", range(4, DK))
         + [f"{s}{j}" for s in ("ess", "erms") for j in range(4)] + each("sig") + ["mix_hi0", "mix_hi1"]
         + [f"{s}{j}" for s in ("fss", "frms") for j in range(4)])
DVE_L = (each("out_add") + ["p_lo0", "p_lo1"] + [f"{s}{j}" for j in range(4) for s in ("inv", "xn")]
         + ks_of("u_lo", range(DK)),
         [f"{s}{n}_{j}" for n, j in NJ for s in ("square", "h_lo")] + each("down_add"),
         ks_of("x2_lo", range(DK)) + [f"{s}{j}" for j in range(4) for s in ("einv", "e_norm")]
         + [f"{s}{n}_{j}" for n, j in NJ for s in ("gmul", "x_add")] + ["mix_lo0", "mix_lo1"]
         + [f"{s}{j}" for j in range(4) for s in ("finv", "fout")])


def nested_progress(parts, sem):
    pre, mid, post = parts
    total, seen = len(pre) + HG * len(mid) + len(post), []

    def mark(label):
        assert (pre + mid + post)[len(seen)] == label, ((pre + mid + post)[len(seen)], label)
        seen.append(label)
        return sem

    def done(b, g, label, blocks_back=0):
        base = total * (1 - blocks_back)
        if label in pre:
            return sem, b * total + (base + pre.index(label) + 1)
        if label in mid:
            return sem, b * total + g * len(mid) + (base + len(pre) + mid.index(label) + 1)
        return sem, b * total + (base + len(pre) + HG * len(mid) + post.index(label) + 1)

    return mark, done, total


def finish_layer(nc, x, p, mixT, out, params, consts, ple_g, final_g, w_out, w_up, w_down, w_ple, w_gate):
    PRE, MID, POST = 4, 8, 6
    PER = PRE + HG * MID + POST
    with ExitStack() as ctx:
        sb = lambda n, s, d=F32: ctx.enter_context(nc.sbuf_tensor(n, s, d))
        sem = lambda n: ctx.enter_context(nc.semaphore(n))
        ps = ctx.enter_context(nc.psum_tensor("ps_f", [P, 8, 512], F32))
        par, ident = sb("par_f", [P, NPV]), sb("ident_f", [P, P])
        pleg, fing = sb("pleg_f", [P, D]), sb("fing_f", [P, D])
        eps = sb("eps_f", [P, 1])
        raw = sb("wraw_f", [P, 2, 4, 512])
        w_hi, w_lo = sb("whi_f", [P, 2, 4, 512], F32R), sb("wlo_f", [P, 2, 4, 512], F32R)
        xr = sb("x_f", [P, 4, D])
        stage = sb("stage_f", [P, 4, D])
        act_hi, act_lo = sb("acthi_f", [P, DK, TBK], F32R), sb("actlo_f", [P, DK, TBK], F32R)
        h_hi, h_lo = sb("hhi_f", [P, 8, TBK], F32R), sb("hlo_f", [P, 8, TBK], F32R)
        tmp, sq = sb("tmp_f", [P, 2, 512]), sb("sq_f", [P, 2, 512])
        pin = sb("p_f", [P, 4, PLE])
        pT_hi, pT_lo = sb("pthi_f", [P, 2, TBK], F32R), sb("ptlo_f", [P, 2, TBK], F32R)
        e = sb("e_f", [P, 4, D])
        stat = sb("stat_f", [P, 3, 4])
        junk = sb("junk_f", [P, D])
        gain = par[:, PV["norm_mlp_g"][0]:PV["norm_mlp_g"][1]]
        stage_half = lambda h: stage[:, 2 * h:2 * h + 2, :].rearrange("p j d -> p (j d)")
        act_half = lambda a, h: a[:, 4 * h:4 * h + 4, :].rearrange("p k t -> p (k t)")

        const_in, gains_in, eps_done, passed = sem("const_in_f"), sem("gains_in_f"), sem("eps_f_done"), sem("passed_f")
        raw_in = [sem("raw_in0_f"), sem("raw_in1_f")]
        w_hi_done, w_lo_done, w_used = sem("w_hi_f_done"), sem("w_lo_f_done"), sem("w_used_f")
        x_in, mix_in, p_in, stored = sem("x_in_f"), sem("mix_in_f"), sem("p_in_f"), sem("stored_f")
        pe_done, dve_done, act_done = sem("pe_done_f"), sem("dve_done_f"), sem("act_done_f")
        first_hi = sem("first_hi_f")
        pmark, pdone, PT = nested_progress(PE_L, pe_done)
        vmark, vdone, VT = nested_progress(DVE_L, dve_done)
        amark, adone, AT = nested_progress(ACT_L, act_done)

        with nc.Block() as block:
            @block.sync
            def _(sp):
                for dst, src in ((par[:, :], params), (ident[:, :], consts[:, CC["ident"][0]:CC["ident"][1]])):
                    sp.dma_start(dst, src).then_inc(const_in, 16)

                def load(n, s, src, k=4):
                    sp.wait_ge(w_lo_done, n + 1)
                    sp.sem_inc(passed, 1)
                    sp.dma_start(raw[:, s, 0:k, :], src).then_inc(raw_in[s], 16)

                for c in range(2):
                    load(c, c, w_out[c])
                for dst, src in ((pleg[:, :], ple_g.broadcast_to([P, D])), (fing[:, :], final_g.broadcast_to([P, D]))):
                    sp.dma_start(dst, src).then_inc(gains_in, 16)
                with sp.Fori(0, BLOCKS) as b:
                    for c in range(2, PRE):
                        load(b * PER + c, c % 2, w_out[c])
                    with sp.Fori(0, HG) as g:
                        for c in range(MID):
                            src = w_up if c < 4 else w_down
                            load(b * PER + g * MID + (PRE + c), c % 2,
                                 src[bass.ds(g * 4 + c % 4, 1)].rearrange("n p k f -> p (n k) f"))
                    for c in range(POST):
                        src = w_ple[c] if c < 2 else w_gate[c - 2]
                        load(b * PER + (PRE + HG * MID + c), c % 2, src, 2 if c < 2 else 4)
                    for c in range(2):
                        load(b * PER + (PER + c), c % 2, w_out[c])

            @block.gpsimd
            def _(pool):
                pool.sem_inc(w_lo_done, 2)
                pool.wait_ge(const_in, 32)

                def low_parts(first, chunks):
                    with pool.Fori(0, chunks // 2) as c:
                        for s in range(2):
                            pool.wait_ge(w_hi_done, first + 2 * c + (s + 1))
                            nc.gpsimd.tensor_tensor(w_lo[:, s, :, :], raw[:, s, :, :], w_hi[:, s, :, :].bitcast(F32),
                                                    ALU.subtract).then_inc(w_lo_done, 1)

                def load_mix(b):
                    pool.dma_start(stage[:, :, :].rearrange("p j d -> p (j d)").rearrange("p (k t) -> p k t", k=DK),
                                   mixT[:, :, bass.ds(b * TBK, TBK)].rearrange("k p t -> p k t")).then_inc(mix_in, 16)

                load_mix(0)
                with pool.Fori(0, BLOCKS - 1) as b:
                    low_parts(b * PER, PRE + 2)
                    pool.wait_ge(*pdone(b, 0, f"ut{DK - 1}"))
                    pool.sem_inc(passed, 1)
                    load_mix(b + 1)
                    low_parts(b * PER + (PRE + 2), PER - PRE - 2)
                low_parts((BLOCKS - 1) * PER, PRE + 2)
                pool.wait_ge(*pdone(BLOCKS - 1, 0, f"ut{DK - 1}"))
                load_mix(0)
                low_parts((BLOCKS - 1) * PER + (PRE + 2), PER - PRE)

            @block.tensor
            def _(pe):
                T = nc.tensor
                pe.sem_inc(w_used, 1)
                pe.sem_inc(pe_done, PT)
                pe.wait_ge(const_in, 32)

                def products(bank, s, k0, ks, weights_still, j, hi, lo, first, final, label):
                    for k in range(ks):
                        if weights_still:
                            wh, wl = (w[:, s, k, j * P:(j + 1) * P] for w in (w_hi, w_lo))
                            pairs = ((wh, hi[:, k0 + k, :]), (wh, lo[:, k0 + k, :]), (wl, hi[:, k0 + k, :]))
                        else:
                            ah, al = (a[:, k0 + k, j * P:(j + 1) * P] for a in (hi, lo))
                            pairs = ((ah, w_hi[:, s, k, :]), (ah, w_lo[:, s, k, :]), (al, w_hi[:, s, k, :]))
                        for t, (still, moving) in enumerate(pairs):
                            mm = T.matmul(ps[:, bank, :], still, moving, start=(first and k == 0 and t == 0),
                                          stop=(final and k == ks - 1 and t == 2))
                            if j == 0 and k == 0 and t == 0:
                                mm.then_inc(w_used, 1)
                    if final:
                        mm.then_inc(pmark(label), 1)

                def project(name, n, n_chunk, banks, weights_still, hi, lo, free, ready=None, chunks=2, ks=4):
                    for c in range(chunks):
                        pe.wait_ge(w_lo_done, n_chunk + (c + 3))
                        for j in range(4):
                            if c == 0 and free is not None:
                                pe.wait_ge(*free(j))
                            if ready is not None and j == 0:
                                pe.wait_ge(*ready(c))
                            products(banks + j, (c if chunks == 2 else n) % 2, c * ks, ks, weights_still, j, hi, lo,
                                     c == 0, c == chunks - 1, f"{name}{n}_{j}")

                def turn(label, bank, src, k):
                    for j in range(4):
                        mm = T.transpose(ps[:, bank, j * P:(j + 1) * P], src[:, j, k * P:(k + 1) * P], ident[:, :])
                    mm.then_inc(pmark(f"{label}{k}"), 1)

                with pe.Fori(0, BLOCKS) as b:
                    for n in range(2):
                        project("out", n, b * PER + 2 * n, 4 * n, False, act_hi, act_lo,
                                free=lambda j: adone(b, 0, f"sig{n}_{j}", 1),
                                ready=(lambda c: vdone(b, 0, f"mix_lo{c}", 1)) if n == 0 else None)
                    pe.wait_ge(p_in, 16 * (b + 1))
                    for k in range(2):
                        pe.wait_ge(*vdone(b, 0, f"out_add0_{k}"))
                        turn("pt", k, pin, k)
                    pe.wait_ge(*vdone(b, 0, "xn3"))
                    for k in range(DK):
                        turn("ut", k, stage, k)
                    pe.wait_ge(*vdone(b, 0, "u_lo3"))
                    pe.sem_inc(passed, 1)
                    with pe.Fori(0, HG) as g:
                        for n in range(2):
                            ahead = b * VT + g * len(DVE_L[1]) + (VT + len(DVE_L[0]) - 7 + 4 * n)
                            project("up", n, b * PER + g * MID + (PRE + 2 * n), 4 * n, True, act_hi, act_lo,
                                    free=lambda j: (dve_done, ahead + j),
                                    ready=(lambda c: vdone(b, 0, "u_lo7") if c else (const_in, 32)) if n == 0 else None)
                        for n in range(2):
                            project("down", n, b * PER + g * MID + (PRE + 4 + 2 * n), 4 * n, False, h_hi, h_lo,
                                    free=lambda j: adone(b, g, f"relu{n}_{j}"),
                                    ready=(lambda c: vdone(b, g, f"h_lo{c}_3")) if n == 0 else None)
                    base = b * PER + (PRE + HG * MID)
                    pe.wait_ge(*vdone(b, 0, "p_lo1"))
                    project("ple", 0, base, 4, False, pT_hi, pT_lo,
                            free=lambda j: vdone(b, HG - 1, f"down_add1_{j}"), chunks=1, ks=2)
                    for k in range(4):
                        turn("xt", k, xr, k)
                    project("ple", 1, base + 1, 4, False, pT_hi, pT_lo,
                            free=lambda j: adone(b, 0, f"e_copy0_{j}"), chunks=1, ks=2)
                    for k in range(4, DK):
                        pe.wait_ge(*vdone(b, 0, f"x2_lo{k - 4}"))
                        turn("xt", k - 4, xr, k)
                    project("gate", 0, base + 2, 0, False, act_hi, act_lo,
                            free=lambda j: vdone(b, 0, f"x2_lo{4 + j}"))
                    project("gate", 1, base + 4, 4, False, act_hi, act_lo,
                            free=lambda j: adone(b, 0, f"e_copy1_{j}"))
                pe.wait_ge(*pdone(BLOCKS - 1, 0, "gate1_3"))
                pe.sem_inc(w_used, 1)

            @block.scalar
            def _(act):
                A = nc.scalar
                act.sem_inc(act_done, AT)
                act.sem_inc(stored, 16)
                act.wait_ge(eps_done, 1)
                tok = lambda a, b: a[bass.ds(b * TBK, TBK), :].rearrange("(j p) d -> p j d", p=P)

                def load_x(b):
                    act.dma_start(xr[:, :, :], tok(x, b)).then_inc(x_in, 16)

                def load_p(b):
                    act.dma_start(pin[:, :, :], tok(p, b)).then_inc(p_in, 16)

                def high_part(n, s, uses):
                    act.wait_ge(raw_in[s], 16 * uses)
                    act.wait_ge(w_used, n + 1)
                    A.activation(w_hi[:, s, :, :], raw[:, s, :, :], ACT.Copy).then_inc(w_hi_done, 1)

                def high(b, c, g=None):
                    n, uses = b * PER + c, b * (PER // 2) + (c // 2 + 1)
                    if g is not None:
                        n, uses = n + g * MID, uses + g * (MID // 2)
                    high_part(n, c % 2, uses)

                load_x(0)
                load_p(0)
                high_part(0, 0, 1)
                act.wait_ge(mix_in, 16)
                for h in range(2):
                    A.activation(act_half(act_hi, h), stage_half(h), ACT.Copy).then_inc(first_hi, 1)
                high_part(1, 1, 1)
                with act.Fori(0, BLOCKS) as b:
                    high(b, 2)
                    high(b, 3)
                    for k in range(2):
                        act.wait_ge(*pdone(b, 0, f"pt{k}"))
                        A.activation(pT_hi[:, k, :], ps[:, k, :], ACT.Copy).then_inc(amark(f"p_hi{k}"), 1)
                    high(b, 4)
                    for j in range(4):
                        act.wait_ge(*vdone(b, 0, f"out_add1_{j}"))
                        A.activation(junk[:, :], xr[:, j, :], ACT.Square, accum_out=stat[:, 0, j:j + 1]).then_inc(amark(f"ss{j}"), 1)
                        act.wait_ge(*adone(b, 0, f"ss{j}"))
                        A.activation(stat[:, 0, j:j + 1], stat[:, 0, j:j + 1], ACT.Sqrt, scale=1.0 / D,
                                     bias=eps[:, 0:1]).then_inc(amark(f"rms{j}"), 1)
                    for k in range(DK):
                        act.wait_ge(*pdone(b, 0, f"ut{k}"))
                        A.activation(act_hi[:, k, :], ps[:, k, :], ACT.Copy, scale=gain[:, k:k + 1]).then_inc(amark(f"u_hi{k}"), 1)
                    high(b, 5)
                    with act.Fori(0, HG) as g:
                        for n in range(2):
                            high(b, PRE + 2 + 2 * n, g)
                            for j in range(4):
                                act.wait_ge(*pdone(b, g, f"up{n}_{j}"))
                                A.activation(tmp[:, j % 2, :], ps[:, 4 * n + j, :], ACT.Relu).then_inc(amark(f"relu{n}_{j}"), 1)
                                act.wait_ge(*vdone(b, g, f"square{n}_{j}"))
                                A.activation(h_hi[:, 4 * n + j, :], sq[:, j % 2, :], ACT.Copy).then_inc(amark(f"h_hi{n}_{j}"), 1)
                            high(b, PRE + 3 + 2 * n, g)
                        for c in range(6, 10):
                            high(b, PRE + c, g)
                    at = PRE + HG * MID
                    act.wait_ge(stored, 64 * b + 16)
                    for n in range(2):
                        for j in range(4):
                            act.wait_ge(*pdone(b, 0, f"ple{n}_{j}"))
                            A.activation(e[:, j, n * 512:(n + 1) * 512], ps[:, 4 + j, :], ACT.Copy).then_inc(amark(f"e_copy{n}_{j}"), 1)
                        if n == 0:
                            high(b, at + 2)
                        for k in range(4 * n, 4 * n + 4):
                            act.wait_ge(*pdone(b, 0, f"xt{k}"))
                            A.activation(act_hi[:, k, :], ps[:, k % 4, :], ACT.Copy).then_inc(amark(f"x2_hi{k}"), 1)
                    high(b, at + 3)
                    for j in range(4):
                        act.wait_ge(*adone(b, 0, f"ess{j - 1}" if j else "x2_hi7"))
                        A.activation(junk[:, :], e[:, j, :], ACT.Square, accum_out=stat[:, 1, j:j + 1]).then_inc(amark(f"ess{j}"), 1)
                    for j in range(4):
                        act.wait_ge(*adone(b, 0, f"ess{j}"))
                        A.activation(stat[:, 1, j:j + 1], stat[:, 1, j:j + 1], ACT.Sqrt, scale=1.0 / D,
                                     bias=eps[:, 0:1]).then_inc(amark(f"erms{j}"), 1)
                    high(b, at + 4)
                    for n in range(2):
                        for j in range(4):
                            act.wait_ge(*pdone(b, 0, f"gate{n}_{j}"))
                            if n or j >= 2:
                                act.wait_ge(*vdone(b, 0, f"gmul{n if j >= 2 else n - 1}_{(j + 2) % 4}"))
                            A.activation(tmp[:, j % 2, :], ps[:, 4 * n + j, :], ACT.Sigmoid).then_inc(amark(f"sig{n}_{j}"), 1)
                        if n == 0:
                            high(b, at + 5)
                            high(b, at + 6)
                    act.wait_ge(mix_in, 16 * (b + 2))
                    for h in range(2):
                        A.activation(act_half(act_hi, h), stage_half(h), ACT.Copy).then_inc(amark(f"mix_hi{h}"), 1)
                    high(b, at + 7)
                    for j in range(4):
                        act.wait_ge(*vdone(b, 0, f"x_add1_{j}"))
                        act.wait_ge(*adone(b, 0, f"fss{j - 1}" if j else "mix_hi1"))
                        A.activation(junk[:, :], xr[:, j, :], ACT.Square, accum_out=stat[:, 2, j:j + 1]).then_inc(amark(f"fss{j}"), 1)
                    for j in range(4):
                        act.wait_ge(*adone(b, 0, f"fss{j}"))
                        A.activation(stat[:, 2, j:j + 1], stat[:, 2, j:j + 1], ACT.Sqrt, scale=1.0 / D,
                                     bias=eps[:, 0:1]).then_inc(amark(f"frms{j}"), 1)
                    for j in range(4):
                        act.wait_ge(*vdone(b, 0, f"fout{j}"))
                        act.dma_start(out[bass.ds(b * TBK + j * P, P), :], e[:, j, :]).then_inc(stored, 16)
                    load_x((b + 1) % BLOCKS)
                    load_p((b + 1) % BLOCKS)
                act.wait_ge(stored, 64 * BLOCKS + 16)
                act.wait_ge(x_in, 16 * (BLOCKS + 1))
                act.wait_ge(p_in, 16 * (BLOCKS + 1))

            @block.vector
            def _(dve):
                V = nc.vector
                tail = len(DVE_L[2]) - DVE_L[2].index("mix_lo0")
                dve.sem_inc(dve_done, VT - tail)
                V.memset(eps[:, :], NORM_EPS).then_inc(eps_done, 1)
                for h in range(2):
                    dve.wait_ge(first_hi, h + 1)
                    V.tensor_tensor(act_half(act_lo, h), stage_half(h), act_half(act_hi, h).bitcast(F32),
                                    ALU.subtract).then_inc(dve_done, 1)
                dve.wait_ge(const_in, 32)
                dve.wait_ge(gains_in, 32)
                dve.wait_ge(dve_done, VT - tail + 2)
                dve.sem_inc(dve_done, tail - 2)
                with dve.Fori(0, BLOCKS) as b:
                    dve.wait_ge(x_in, 16 * (b + 1))
                    for n, j in NJ:
                        dve.wait_ge(*pdone(b, 0, f"out{n}_{j}"))
                        V.tensor_tensor(xr[:, j, n * 512:(n + 1) * 512], ps[:, 4 * n + j, :], xr[:, j, n * 512:(n + 1) * 512],
                                        ALU.add).then_inc(vmark(f"out_add{n}_{j}"), 1)
                    for k in range(2):
                        dve.wait_ge(*adone(b, 0, f"p_hi{k}"))
                        V.tensor_tensor(pT_lo[:, k, :], ps[:, k, :], pT_hi[:, k, :].bitcast(F32), ALU.subtract).then_inc(vmark(f"p_lo{k}"), 1)
                    for j in range(4):
                        dve.wait_ge(*adone(b, 0, f"rms{j}"))
                        V.reciprocal(stat[:, 0, j:j + 1], stat[:, 0, j:j + 1]).then_inc(vmark(f"inv{j}"), 1)
                        dve.wait_ge(*vdone(b, 0, f"inv{j}"))
                        V.tensor_scalar(stage[:, j, :], xr[:, j, :], stat[:, 0, j:j + 1], None, ALU.mult).then_inc(vmark(f"xn{j}"), 1)
                    for k in range(DK):
                        dve.wait_ge(*adone(b, 0, f"u_hi{k}"))
                        V.scalar_tensor_tensor(act_lo[:, k, :], ps[:, k, :], gain[:, k:k + 1], act_hi[:, k, :].bitcast(F32),
                                               ALU.mult, ALU.subtract).then_inc(vmark(f"u_lo{k}"), 1)
                    with dve.Fori(0, HG) as g:
                        for n, j in NJ:
                            dve.wait_ge(*adone(b, g, f"relu{n}_{j}"))
                            V.tensor_tensor(sq[:, j % 2, :], tmp[:, j % 2, :], tmp[:, j % 2, :], ALU.mult).then_inc(vmark(f"square{n}_{j}"), 1)
                            dve.wait_ge(*adone(b, g, f"h_hi{n}_{j}"))
                            V.tensor_tensor(h_lo[:, 4 * n + j, :], sq[:, j % 2, :], h_hi[:, 4 * n + j, :].bitcast(F32),
                                            ALU.subtract).then_inc(vmark(f"h_lo{n}_{j}"), 1)
                        for n, j in NJ:
                            dve.wait_ge(*pdone(b, g, f"down{n}_{j}"))
                            V.tensor_tensor(xr[:, j, n * 512:(n + 1) * 512], ps[:, 4 * n + j, :], xr[:, j, n * 512:(n + 1) * 512],
                                            ALU.add).then_inc(vmark(f"down_add{n}_{j}"), 1)
                    for k in range(DK):
                        dve.wait_ge(*adone(b, 0, f"x2_hi{k}"))
                        V.tensor_tensor(act_lo[:, k, :], ps[:, k % 4, :], act_hi[:, k, :].bitcast(F32), ALU.subtract).then_inc(vmark(f"x2_lo{k}"), 1)
                    for j in range(4):
                        dve.wait_ge(*adone(b, 0, f"erms{j}"))
                        V.reciprocal(stat[:, 1, j:j + 1], stat[:, 1, j:j + 1]).then_inc(vmark(f"einv{j}"), 1)
                        dve.wait_ge(*vdone(b, 0, f"einv{j}"))
                        V.scalar_tensor_tensor(e[:, j, :], e[:, j, :], stat[:, 1, j:j + 1], pleg[:, :], ALU.mult,
                                               ALU.mult).then_inc(vmark(f"e_norm{j}"), 1)
                    for n, j in NJ:
                        cols = slice(n * 512, (n + 1) * 512)
                        dve.wait_ge(*adone(b, 0, f"sig{n}_{j}"))
                        dve.wait_ge(*vdone(b, 0, f"e_norm{j}"))
                        V.tensor_tensor(e[:, j, cols], tmp[:, j % 2, :], e[:, j, cols], ALU.mult).then_inc(vmark(f"gmul{n}_{j}"), 1)
                        dve.wait_ge(*vdone(b, 0, f"gmul{n}_{j}"))
                        V.tensor_tensor(xr[:, j, cols], e[:, j, cols], xr[:, j, cols], ALU.add).then_inc(vmark(f"x_add{n}_{j}"), 1)
                    for h in range(2):
                        dve.wait_ge(*adone(b, 0, f"mix_hi{h}"))
                        V.tensor_tensor(act_half(act_lo, h), stage_half(h), act_half(act_hi, h).bitcast(F32),
                                        ALU.subtract).then_inc(vmark(f"mix_lo{h}"), 1)
                    for j in range(4):
                        dve.wait_ge(*adone(b, 0, f"frms{j}"))
                        V.reciprocal(stat[:, 2, j:j + 1], stat[:, 2, j:j + 1]).then_inc(vmark(f"finv{j}"), 1)
                        dve.wait_ge(*vdone(b, 0, f"finv{j}"))
                        V.scalar_tensor_tensor(e[:, j, :], xr[:, j, :], stat[:, 2, j:j + 1], fing[:, :], ALU.mult,
                                               ALU.mult).then_inc(vmark(f"fout{j}"), 1)


def pack(inputs):
    f = lambda n: np.ascontiguousarray(inputs[n])
    per_feature = lambda a: np.asarray(a).reshape(-1, P).T
    q = np.arange(RW).reshape(2, PAIRS, HD).transpose(1, 0, 2).reshape(-1)
    cols = np.concatenate([np.arange(RWT * P), RWT * P + q, np.arange((RWT + PAIRS) * P, ZT * P)])
    rows = np.concatenate([np.arange(RW), RW + q])
    chunks = lambda w, n, c, k: np.asarray(w).reshape(c, k, P, n, -1).transpose(3, 0, 2, 1, 4).reshape(n * c, P, k, -1)
    up = f("w_ff_up")[0]
    down = f("w_ff_down")[0]
    a = {
        "x": f("x")[0], "p": f("p")[0, 0],
        "params": np.concatenate([per_feature(inputs[n]) for n in
                                  ("norm_mix_g", "norm_mlp_g", "mu_shift", "w0", "a0", "k_k", "k_a", "r_k")], 1),
        "consts": shape_constants(), "hrows": head_rows(), "onehot": bucket_onehot(),
        "rel_bias": f("rel_bias"), "sinks": f("sinks"),
        "w_lora": f("w_up")[0], "a_lora": f("a_up")[0], "g_lora": f("g_up")[0],
        "lnx_g": f("lnx_g"), "lnx_b": f("lnx_b"),
        "ple_g": f("ple_norm_g"), "final_g": f("final_norm_g").reshape(1, D),
        "w_in": chunks(f("w_in")[0][:, cols], ZT // 2, 1, DK),
        "w_out": chunks(f("w_out")[0][rows], 2, 2, 4),
        "w_ff_up": chunks(up, 2 * HG, 2, 4),
        "w_ff_down": np.concatenate([chunks(down[g * HGD:(g + 1) * HGD], 2, 2, 4) for g in range(HG)], 0),
        "w_ple": chunks(f("ple_proj")[0], 2, 1, 2),
        "w_gate": chunks(f("ple_gate")[0], 2, 2, 4),
    }
    return {k: np.ascontiguousarray(v) for k, v in a.items()}


def build(nc, t, out):
    zT = nc.dram_tensor("zT", [ZT, P, PADC + SEQ], F32, kind="Internal")
    mixT = nc.dram_tensor("mixT", [2 * PAIRS, P, SEQ], F32, kind="Internal")
    skew = nc.dram_tensor("skew", [HEADS * P * EXT + P], F32, kind="Internal")
    norm_and_project(nc, t["x"], t["w_in"], t["params"], t["consts"], zT)
    mix_tokens(nc, zT, mixT, t["params"], t["consts"], t["hrows"], t["onehot"], t["rel_bias"], t["sinks"],
               t["w_lora"], t["a_lora"], t["g_lora"], t["lnx_g"], t["lnx_b"], skew)
    finish_layer(nc, t["x"], t["p"], mixT, out, t["params"], t["consts"], t["ple_g"], t["final_g"],
                 t["w_out"], t["w_ff_up"], t["w_ff_down"], t["w_ple"], t["w_gate"])


def kernel(**inputs):
    import concourse.bacc as bacc
    from concourse.bass_utils import run_bass_kernel_spmd

    nc = bacc.Bacc("TRN2", target_bir_lowering=False, num_devices=1)
    arrays = {f"in_{k}": v for k, v in pack(inputs).items()}
    t = {k[3:]: nc.dram_tensor(k, v.shape, mybir.dt.from_np(v.dtype), kind="ExternalInput").ap() for k, v in arrays.items()}
    out = nc.dram_tensor("out_y", (SEQ, D), F32, kind="ExternalOutput").ap()
    build(nc, t, out)
    r = run_bass_kernel_spmd(nc, [arrays], core_ids=[0])
    return np.asarray(r.results[0]["out_y"]).reshape(1, SEQ, D)
```

```python
from contextlib import ExitStack

import numpy as np

import concourse.bass as bass
from concourse import mybir

F32 = mybir.dt.float32
F32R = mybir.dt.float32r
ALU = mybir.AluOpType
ACT = mybir.ActivationFunctionType
AX = mybir.AxisListType

P = 128
SEQ, D, PLE, FF = 2048, 1024, 256, 4096
DK = D // P
TILES = SEQ // P
HEADS, HD = 8, 64
RW = HEADS * HD
PAIRS = RW // P
RWT = 14
ZT = 20
CH = 64
BUCKETS = 32
PADC = P
DECAY = float(np.exp(-0.5))
NEG = -1e30
NORM_EPS, LNX_EPS = 1e-6, 64e-5
EXT = 3 * P

PV = {}
_at = 0
for _n, _w in (("norm_mix_g", DK), ("norm_mlp_g", DK), ("mu", RWT), ("w0", PAIRS), ("a0", PAIRS),
               ("k_k", PAIRS), ("k_a", PAIRS), ("r_k", PAIRS)):
    PV[_n] = (_at, _at + _w)
    _at += _w
NPV = _at

LEVELS = 6
CC = {}
_at = 0
for _n, _w in (("ident", P), ("score_mask", 4 * P), ("level_mask", LEVELS * P), ("first_mask_t", P),
               ("chunk_start", PAIRS * P), ("head_of", PAIRS * HEADS), ("pair_sel", 2)):
    CC[_n] = (_at, _at + _w)
    _at += _w
NCC = _at


def shape_constants():
    c = np.zeros((P, NCC), np.float32)
    r, t = np.arange(P)[:, None], np.arange(P)[None, :]
    c[:, CC["ident"][0]:CC["ident"][1]] = r == t
    same = r // CH == t // CH
    strict, incl = same & (r < t), same & (r <= t)
    c[:, CC["score_mask"][0]:CC["score_mask"][1]] = np.concatenate([strict, incl, strict, incl], 1)
    lv = []
    for l in range(LEVELS):
        b = 1 << l
        lv.append((r // (2 * b) == t // (2 * b)) & ((r // b) % 2 == 1) & ((t // b) % 2 == 0))
    c[:, CC["level_mask"][0]:CC["level_mask"][1]] = np.concatenate(lv, 1)
    c[:, CC["first_mask_t"][0]:CC["first_mask_t"][1]] = lv[0].T
    c[:, CC["chunk_start"][0]:CC["chunk_start"][1]] = np.tile(np.arange(P) % CH != 0, PAIRS)[None]
    ho = np.zeros((P, PAIRS, HEADS), np.float32)
    for f in range(PAIRS):
        for h in range(2):
            ho[h * HD:(h + 1) * HD, f, 2 * f + h] = 1
    c[:, CC["head_of"][0]:CC["head_of"][1]] = ho.reshape(P, -1)
    c[:, CC["pair_sel"][0]:CC["pair_sel"][1]] = ho[:, 0, 0:2]
    return c


def head_rows():
    return np.repeat(np.eye(HEADS, dtype=np.float32), HD, axis=1)


def bucket_onehot():
    o = np.zeros((BUCKETS + 1, EXT), np.float32)
    for m in range(EXT):
        d = 2 * P - 1 - m
        if not 0 <= d < P:
            o[BUCKETS, m] = NEG
            continue
        half = BUCKETS // 2
        if d < half:
            b = d
        else:
            b = half + int(np.float32(np.log(np.float32(d) / np.float32(half))) / np.float32(np.log(P / half))
                           * np.float32(BUCKETS - half))
        o[min(b, BUCKETS - 1), m] = 1
    return o


def norm_and_project(nc, x, w_in, params, consts, zT, onehot, rel_bias, skew):
    FC = 2
    CHUNKS = ZT // FC
    TB = 512
    NTB = SEQ // TB
    with ExitStack() as ctx:
        sb = lambda n, s, d=F32: ctx.enter_context(nc.sbuf_tensor(n, s, d))
        sem = lambda n: ctx.enter_context(nc.semaphore(n))
        hT_hi = sb("hT_hi", [P, DK, SEQ], F32R)
        hT_lo = sb("hT_lo", [P, DK, SEQ], F32R)
        par = sb("par_a", [P, NPV])
        ident = sb("ident_a", [P, P])
        ps = ctx.enter_context(nc.psum_tensor("ps_a", [P, 8, 512], F32))
        g = par[:, PV["norm_mix_g"][0]:PV["norm_mix_g"][1]]
        raw = sb("wraw_a", [P, 2, DK, FC * P])
        w_hi = sb("whi_a", [P, 2, DK, FC * P], F32R)
        w_lo = sb("wlo_a", [P, 2, DK, FC * P], F32R)
        raw_in = [sem("raw_in0_a"), sem("raw_in1_a")]
        w_hi_done, w_lo_done = sem("w_hi_a"), sem("w_lo_a")

        def split_chunk(pool, s, count):
            nc.gpsimd.tensor_scalar(w_hi[:, s, :, :], raw[:, s, :, :], 1.0, None, ALU.mult).then_inc(w_hi_done, 1)
            pool.wait_ge(w_hi_done, count)
            nc.gpsimd.tensor_tensor(w_lo[:, s, :, :], raw[:, s, :, :], w_hi[:, s, :, :].bitcast(F32),
                                    ALU.subtract).then_inc(w_lo_done, 1)

        with ExitStack() as inner:
            sbi = lambda n, s, d=F32: inner.enter_context(nc.sbuf_tensor(n, s, d))
            xt = sbi("xt_a", [P, 2, D])
            junk = sbi("junk_a", [P, D])
            xn = sbi("xn_a", [P, 2, D])
            xg = sbi("xg_a", [P, 2, DK, P])
            ss = sbi("ss_a", [P, 2, 1])
            rs = sbi("rs_a", [P, 2, 1])
            eps = sbi("eps_a", [P, 1])
            oneh, relb = sbi("oneh_a", [BUCKETS + 1, EXT]), sbi("relb_a", [BUCKETS + 1, HEADS])
            ext = sbi("ext_a", [HEADS, EXT])
            b_in, b_one, b_ps, b_sb, b_st = sem("b_in_a"), sem("b_one_a"), sem("b_ps_a"), sem("b_sb_a"), sem("b_st_a")
            const_in, x_in0, x_in1 = sem("const_in_a"), sem("x_in0_a"), sem("x_in1_a")
            x_in = [x_in0, x_in1]
            sumsq_done, rms_done, rstd_done = sem("sumsq_a"), sem("rms_a"), sem("rstd_a")
            xn_done, transposed, scaled, hi_done, lo_done = (
                sem("xn_a"), sem("tr_a"), sem("scaled_a"), sem("hi_a"), sem("lo_a"))
            eps_done = sem("eps_done_a")
            with nc.Block() as block:
                count = lambda it, k: k if it is None else 2 * it + k
                cols = lambda it, k: bass.ds(k * P if it is None else it * (2 * P) + k * P, P)

                @block.sync
                def _(sp):
                    with sp.Fori(0, TILES // 2) as it:
                        for s in range(2):
                            sp.wait_ge(xn_done, 2 * it + s + 1)
                            sp.dma_start(xt[:, s, :], x[bass.ds(it * (2 * P) + s * P, P), :]).then_inc(x_in[s], 16)

                @block.gpsimd
                def _(pool):
                    nc.gpsimd.memset(relb[BUCKETS:BUCKETS + 1, :], 1.0).then_inc(b_one, 1)
                    pool.wait_ge(b_one, 1)
                    for s in range(2):
                        pool.wait_ge(raw_in[s], 16)
                        split_chunk(pool, s, s + 1)

                @block.scalar
                def _(act):
                    act.dma_start(par[:, :], params).then_inc(const_in, 16)
                    act.dma_start(ident[:, :], consts[:, CC["ident"][0]:CC["ident"][1]]).then_inc(const_in, 16)
                    for dst, src in ((oneh[:, :], onehot), (relb[0:BUCKETS, :], rel_bias)):
                        act.dma_start(dst, src).then_inc(b_in, 16)
                    for s in range(2):
                        act.dma_start(raw[:, s, :, :], w_in[s]).then_inc(raw_in[s], 16)
                    act.wait_ge(eps_done, 1)

                    def root_mean_square(it, k):
                        s = k % 2
                        act.wait_ge(x_in[s], 16 * (k // 2 + 1) if it is None else 16 * it + 16 * (k // 2 + 1))
                        act.wait_ge(rstd_done, count(it, k + 1))
                        nc.scalar.activation(junk[:, :], xt[:, s, :], ACT.Square, accum_out=ss[:, s, :]).then_inc(sumsq_done, 1)
                        act.wait_ge(sumsq_done, count(it, k + 1))
                        nc.scalar.activation(rs[:, s, :], ss[:, s, :], ACT.Sqrt, scale=1.0 / D,
                                             bias=eps[:, 0:1]).then_inc(rms_done, 1)

                    def high(it, k):
                        act.wait_ge(scaled, count(it, k + 3))
                        nc.scalar.activation(hT_hi[:, :, cols(it, k)], xg[:, k % 2, :, :], ACT.Copy).then_inc(hi_done, 1)

                    root_mean_square(None, 0)
                    root_mean_square(None, 1)
                    act.wait_ge(b_ps, 1)
                    nc.scalar.activation(ext[:, :], ps[0:HEADS, 7, 0:EXT], ACT.Copy).then_inc(b_sb, 1)
                    act.wait_ge(b_sb, 1)
                    act.dma_start(bass.AP(skew, 0, [[P * EXT, HEADS], [EXT, P], [1, EXT]]),
                                  ext[:, :].unsqueeze(1).broadcast_to([HEADS, P, EXT])).then_inc(b_st, 16)
                    with act.Fori(0, TILES // 2 - 1) as it:
                        for k in range(2):
                            root_mean_square(it, k + 2)
                            high(it, k)
                    high(None, TILES - 2)
                    high(None, TILES - 1)
                    act.wait_ge(b_st, 16)

                @block.vector
                def _(dve):
                    nc.vector.memset(eps[:, :], NORM_EPS).then_inc(eps_done, 1)
                    for free in (xn_done, scaled, rstd_done, lo_done):
                        dve.sem_inc(free, 2)
                    dve.wait_ge(const_in, 32)

                    def normalise(it, k):
                        s = k % 2
                        dve.wait_ge(rms_done, count(it, k + 1))
                        nc.vector.reciprocal(rs[:, s, :], rs[:, s, :]).then_inc(rstd_done, 1)
                        dve.wait_ge(rstd_done, count(it, k + 3))
                        dve.wait_ge(transposed, count(it, k + 1))
                        nc.vector.tensor_scalar(xn[:, s, :], xt[:, s, :], rs[:, s, :], None, ALU.mult).then_inc(xn_done, 1)

                    def gain(it, k):
                        s = k % 2
                        dve.wait_ge(lo_done, count(it, k + 1))
                        dve.wait_ge(transposed, count(it, k + 3))
                        nc.vector.tensor_tensor(
                            xg[:, s, :, :], ps[:, 2 * s:2 * s + 2, :].rearrange("p b (k t) -> p (b k) t", t=P),
                            g.unsqueeze(2).broadcast_to([P, DK, P]), ALU.mult).then_inc(scaled, 1)

                    def low(it, k):
                        dve.wait_ge(hi_done, count(it, k + 1))
                        nc.vector.tensor_tensor(hT_lo[:, :, cols(it, k)], xg[:, k % 2, :, :],
                                                hT_hi[:, :, cols(it, k)].bitcast(F32), ALU.subtract).then_inc(lo_done, 1)

                    normalise(None, 0)
                    normalise(None, 1)
                    gain(None, 0)
                    with dve.Fori(0, TILES // 2 - 1) as it:
                        for k in range(1, 3):
                            normalise(it, k + 1)
                            gain(it, k)
                            low(it, k - 1)
                    gain(None, TILES - 1)
                    low(None, TILES - 2)
                    low(None, TILES - 1)

                @block.tensor
                def _(pe):
                    pe.sem_inc(transposed, 2)
                    pe.wait_ge(b_in, 32)
                    pe.wait_ge(b_one, 1)
                    nc.tensor.matmul(ps[0:HEADS, 7, 0:EXT], relb[:, :], oneh[:, :], start=True, stop=True).then_inc(b_ps, 1)
                    pe.wait_ge(const_in, 32)
                    with pe.Fori(0, TILES // 2) as it:
                        for s in range(2):
                            n = 2 * it + s
                            pe.wait_ge(xn_done, n + 3)
                            pe.wait_ge(scaled, n + 1)
                            for k in range(DK):
                                last = nc.tensor.transpose(ps[:, 2 * s + k // 4, (k % 4) * P:(k % 4 + 1) * P],
                                                           xn[:, s, k * P:(k + 1) * P], ident[:, :])
                            last.then_inc(transposed, 1)

        with ExitStack() as inner:
            sbi = lambda n, s, d=F32: inner.enter_context(nc.sbuf_tensor(n, s, d))
            zo = sbi("zo_a", [P, 2, SEQ])
            zero = sbi("zero_a", [P, PADC])
            passed = sem("passed_a")
            w_used = sem("w_used_a")
            z_full, z_out, stored, pad_done, zero_done = (
                sem("z_full_a"), sem("z_out_a"), [sem("zst0_a"), sem("zst1_a")], sem("pad_a"), sem("zero_done_a"))
            with nc.Block() as block:
                @block.sync
                def _(sp):
                    sp.wait_ge(zero_done, 1)
                    sp.dma_start(zT[:, :, 0:PADC].rearrange("f p t -> p f t"),
                                 zero[:, :].unsqueeze(1).broadcast_to([P, ZT, PADC])).then_inc(pad_done, 16)
                    with sp.Fori(0, CHUNKS // 2 - 1) as it:
                        for s in range(2):
                            sp.wait_ge(w_lo_done, 2 * it + s + 1)
                            sp.sem_inc(passed, 1)
                            sp.dma_start(raw[:, s, :, :], w_in[bass.ds(2 * it + (s + 2), 1)].rearrange(
                                "n p k f -> p (n k) f")).then_inc(raw_in[s], 16)
                    sp.wait_ge(pad_done, 16)

                @block.gpsimd
                def _(pool):
                    nc.gpsimd.memset(zero[:, :], 0.0).then_inc(zero_done, 1)
                    with pool.Fori(0, CHUNKS // 2 - 1) as it:
                        for s in range(2):
                            n = 2 * it + (s + 2)
                            pool.wait_ge(raw_in[s], 16 * it + 32)
                            pool.wait_ge(w_used, n + 1)
                            pool.sem_inc(passed, 1)
                            split_chunk(pool, s, n + 1)

                @block.tensor
                def _(pe):
                    pe.sem_inc(w_used, 1)
                    with pe.Fori(0, CHUNKS // 2) as it:
                        for s in range(2):
                            n = 2 * it + s
                            pe.wait_ge(w_lo_done, n + 1)
                            for f in range(FC):
                                for tb in range(NTB):
                                    bank = f * NTB + tb
                                    pe.wait_ge(z_out, 8 * n + bank + 1)
                                    tok = slice(tb * TB, (tb + 1) * TB)
                                    feat = slice(f * P, (f + 1) * P)
                                    for k in range(DK):
                                        mm = nc.tensor.matmul(ps[:, bank, :], w_hi[:, s, k, feat], hT_hi[:, k, tok],
                                                              start=(k == 0), stop=False)
                                        if bank == 0 and k == 0:
                                            mm.then_inc(w_used, 1)
                                        nc.tensor.matmul(ps[:, bank, :], w_hi[:, s, k, feat], hT_lo[:, k, tok],
                                                         start=False, stop=False)
                                        mm = nc.tensor.matmul(ps[:, bank, :], w_lo[:, s, k, feat], hT_hi[:, k, tok],
                                                              start=False, stop=(k == DK - 1))
                                    mm.then_inc(z_full, 1)

                @block.scalar
                def _(act):
                    act.sem_inc(z_out, 8)
                    for f in range(FC):
                        act.sem_inc(stored[f], 16)
                    with act.Fori(0, CHUNKS // 2) as it:
                        for s in range(2):
                            n = 2 * it + s
                            for f in range(FC):
                                act.wait_ge(stored[f], 32 * it + (16 * s + 16))
                                for tb in range(NTB):
                                    bank = f * NTB + tb
                                    act.wait_ge(z_full, 8 * n + bank + 1)
                                    nc.scalar.activation(zo[:, f, tb * TB:(tb + 1) * TB], ps[:, bank, :],
                                                         ACT.Copy).then_inc(z_out, 1)
                                act.wait_ge(z_out, 8 * n + f * NTB + NTB + 8)
                                act.dma_start(zT[bass.ds(it * (2 * FC) + s * FC + f, 1), :, PADC:].rearrange(
                                    "n p t -> p (n t)"), zo[:, f, :]).then_inc(stored[f], 16)
                    for f in range(FC):
                        act.wait_ge(stored[f], 16 * CHUNKS + 16)


BACK = {"A": 0, "B": 1, "C": 2}
PE_STEPS = {
    "A": ["v_keys", "score_a", "score_b", "lora_w", "lora_a", "kk_norm", "norm_rows", "probs_t_a", "probs_t_b", "pv_a",
          "bonus", "pv_b", "gate", "t_beta", "t_alpha", "t_kappa", "t_v"] + [f"rw_score{h}" for h in range(HEADS)],
    "B": ([f"first_t{q}" for q in range(2)]
          + [f"{s}{l}_{q}" for l in range(1, LEVELS - 1) for s in ("ax", "xax") for q in range(2)]
          + [f"ax{LEVELS - 1}_0", f"ax{LEVELS - 1}_1", "av", f"xax{LEVELS - 1}_0", f"xax{LEVELS - 1}_1", "u", "w_t", "sa0", "grow0", "sa1", "grow1", "y"]),
    "C": ["out_t"]}
DVE_STEPS = {
    "A": ["logit_a", "logit_b", "rowmax_a", "max_a", "negmax_a", "sink_gap_a", "rowmax_b", "max_b", "negmax_b",
          "sink_gap_b", "cum", "norm_floor", "norm_inv", "kk", "alpha", "denom_a", "inv_a",
          "probs_a", "a_scale", "denom_b", "inv_b", "probs_b", "beta", "kappa", "rho"]
         + [f"masked{h}" for h in range(HEADS)] + ["p_ends"],
    "B": (["a_first0", "x_first0", "a_first1", "x_first1"]
          + [f"{s}{l}_{q}" for l in range(1, LEVELS) for s in ("ax_masked", "x_next") for q in range(2)]
          + ["sa_add0", "grow_add0", "state0", "sa_add1", "grow_add1", "state1", "y_sum", "y_mean", "y_center"]),
    "C": ["y_sqsum", "y_inv", "y_norm"]}
ACT_STEPS = {
    "A": ["v_copy", "tanh_w", "sig_g", "sig_w", "sig_a", "kk_sq", "norm_sqrt", "p_inc", "p_inv", "exp_a",
          "exp_sink_a", "p_exc", "exp_b", "exp_sink_b", "pt_copy_a", "pt_copy_b", "bonus_copy", "att_copy", "gate_copy",
          "alpha_t", "beta_t", "kappa_t", "v_t", "rho_copy"],
    "B": ["av_copy", "u_copy", "w_copy", "gate_keep"],
    "C": ["y_rms", "out_copy"]}
POOL_STEPS = {
    "A": ["diff_low", "diff_mu_low", "zs_low", "diff_k", "diff_mu_k", "zs_k", "kk_raw", "diff", "diff_mu", "zs", "cum_before", "kk_a", "kmod", "rk", "rk_rk"],
    "B": ["xt_mask0", "xt_first0", "xt_mask1", "xt_first1", "bonus_v"],
    "C": ["y_sq", "y_gain", "y_bias", "y_bonus", "y_gate"]}


def progress(stages, sems):
    stage_of = {label: st for st, steps in stages.items() for label in steps}
    at = {st: 0 for st in stages}

    def value(slot, st, steps_done):
        per = len(stages[st])
        tiles = slot[1] - BACK[st]
        if slot[0] is None:
            return min(tiles, TILES) * per + steps_done + 1
        return slot[0] * per + (tiles * per + steps_done + 1)

    def mark(label):
        st = stage_of[label]
        assert stages[st][at[st]] == label, (stages[st][at[st]], label)
        at[st] = (at[st] + 1) % len(stages[st])
        return sems[st]

    def done(slot, label):
        st = stage_of[label]
        return sems[st], value(slot, st, stages[st].index(label) + 1)

    def before(slot):
        return [(sems[st], value(slot, st, 0)) for st in stages if slot[0] is not None or slot[1] > BACK[st]]

    return mark, done, before


def mix_tokens(nc, zT, mixT, params, consts, hrows, sinks, w_up, a_up, g_up, lnx_g, lnx_b, skew,
               w_out, first_block):
    raw_f, stage_f, raw_in_f, first_mix_in = first_block
    with ExitStack() as ctx:
        sb = lambda n, s, d=F32: ctx.enter_context(nc.sbuf_tensor(n, s, d))
        sem = lambda n: ctx.enter_context(nc.semaphore(n))
        ps = ctx.enter_context(nc.psum_tensor("ps_m", [P, 8, 512], F32))
        par, con = sb("par_m", [P, NPV]), sb("con_m", [P, NCC])
        hsel = sb("hsel_m", [HEADS, RW])
        bias = sb("bias_m", [P, HEADS, 2 * P])
        sink = sb("sink_m", [P, HEADS])
        lora = sb("lora_m", [P, RW])
        gup = sb("gup_m", [P, RW])
        lng, lnb = sb("lng_m", [P, RW]), sb("lnb_m", [P, RW])
        one_minus_ka = sb("omka_m", [P, PAIRS])
        lnx_eps = sb("lnxeps_m", [P, 1])

        zr = sb("zr_m", [P, RWT, P + 1])
        zs = sb("zs_m", [P, RWT, P])
        qT, kvT = sb("qT_m", [P, PAIRS, P]), sb("kvT_m", [P, 2, 2 * P])
        f4 = lambda n: sb(n, [P, PAIRS, P])
        kk_raw, kk_sq, sw, av, cum, cumx = f4("kkraw_m"), f4("kksq_m"), f4("sw_m"), f4("av_m"), f4("cum_m"), f4("cumx_m")
        p_inc, p_exc, p_inv = f4("pinc_m"), f4("pexc_m"), f4("pinv_m")
        ascale, kmod, kk, kka, betaT, kappaT, rk = (
            f4("ascale_m"), f4("kmod_m"), f4("kk_m"), f4("kka_m"), f4("betaT_m"), f4("kappaT_m"), f4("rk_m"))
        ar = sb("ar_m", [P, PAIRS, 2, P])
        th = sb("th_m", [HD, P])
        sg = sb("sg_m", [P, P])
        gate_new, gate = sb("gatenew_m", [P, RW]), sb("gate_m", [P, RW])
        rho = f4("rho_m")
        ends = sb("ends_m", [P, PAIRS, 2])
        nrm = sb("nrm_m", [HEADS, P])
        vk = sb("vk_m", [P, 2, P])
        bon = sb("bon_m", [P, HEADS])
        logit, pt = sb("logit_m", [P, HEADS, 2 * P]), sb("pt_m", [P, 2, 2, PAIRS, P])
        small = lambda n: sb(n, [P, HEADS])
        rowmax, negmax, gap, den, esink = small("rowmax_m"), small("negmax_m"), small("gap_m"), small("den_m"), small("esink_m")
        attT = sb("attT_m", [P, PAIRS, P])
        t4 = lambda n: sb(n, [P, RW])
        beta_t, kappa_t, alpha_t, v_t = t4("betat_m"), t4("kappat_m"), t4("alphat_m"), t4("vt_m")
        bm = sb("bm_m", [P, HEADS, 4, P])
        x_m, xt_m, ax = sb("x_m", [P, HEADS, P]), sb("xt_m", [P, HEADS, P]), sb("ax_m", [P, HEADS, P])
        avt, u_t, wT, sa = t4("avt_m"), t4("ut_m"), f4("wT_m"), t4("sa_m")
        state = sb("state_m", [P, 2, PAIRS, HD])
        grow = sb("grow_m", [P, PAIRS, HD])
        y, ysq, yb = t4("y_m"), t4("ysq_m"), t4("yb_m")
        ysum, yss = small("ysum_m"), small("yss_m")
        rwT = f4("rwT_m")

        col = lambda n: par[:, PV[n][0]:PV[n][1]]
        cst = lambda n: con[:, CC[n][0]:CC[n][1]]
        ident = cst("ident")
        score_mask = cst("score_mask").rearrange("p (a t) -> p a t", a=4)
        level_mask = cst("level_mask").rearrange("p (l t) -> p l t", l=LEVELS)
        head_of = cst("head_of").rearrange("p (f h) -> p f h", f=PAIRS)
        bank = lambda b: ps[:, b, :]
        over = lambda a, n: a.unsqueeze(2).broadcast_to([a.shape[0], a.shape[1], n])
        by_parity = lambda a: a.rearrange("p (f a v) -> p a f v", a=2, v=HD)
        four = lambda m: m.unsqueeze(1).broadcast_to([P, 4, P])

        c_in, con_in, par_in, b_rd, set_up = sem("c_in_m"), sem("con_in_m"), sem("par_in_m"), sem("b_rd_m"), sem("set_up_m")
        CONSTS = 7
        rw_in, qkv_in = sem("rw_in_m"), sem("qkv_in_m")

        def load_rw(sp, i):
            sp.dma_start(zr[:, :, :], zT[0:RWT, :, bass.ds(i * P + (PADC - 1), P + 1)].rearrange(
                "f p t -> p f t")).then_inc(rw_in, 16)

        def load_qkv(sp, i):
            sp.dma_start(qT[:, :, :], zT[RWT:RWT + PAIRS, :, bass.ds(i * P + PADC, P)].rearrange(
                "f p t -> p f t")).then_inc(qkv_in, 16)
            sp.dma_start(kvT[:, :, :], zT[RWT + PAIRS:ZT, :, bass.ds(i * P, 2 * P)].rearrange(
                "f p t -> p f t")).then_inc(qkv_in, 16)

        counts = lambda eng, stages: {st: sem(f"{eng}_{st}_done_m") for st in stages}
        pe_counts, dve_counts, act_counts, pool_counts = (
            counts("pe", PE_STEPS), counts("dve", DVE_STEPS), counts("act", ACT_STEPS), counts("pool", POOL_STEPS))
        rw_stored, att_stored = sem("rwst_m"), sem("attst_m")
        first_logit = sem("first_logit_m")
        pmark, pdone, pbefore = progress(PE_STEPS, pe_counts)
        vmark, vdone, vbefore = progress(DVE_STEPS, dve_counts)
        amark, adone, abefore = progress(ACT_STEPS, act_counts)
        gmark, gdone, gbefore = progress(POOL_STEPS, pool_counts)
        groups = {"a": 0, "b": 1}
        score_banks = (0, 1, 3, 2)
        passed = sem("passed_m")

        def start(eng, counts_):
            for count in counts_.values():
                eng.sem_inc(count, 1)

        def slot_start(eng, s):
            for before in (pbefore, vbefore, abefore, gbefore):
                for count, value in before(s):
                    eng.wait_ge(count, value)
            eng.sem_inc(passed, 1)

        def tile(s, stage):
            return s[1] - BACK[stage] if s[0] is None else s[0] + (s[1] - BACK[stage])

        def all_slots(eng, slot):
            slot((None, 0), "A")
            slot((None, 1), "AB")
            with eng.Fori(0, TILES - 2) as it:
                slot((it, 2), "ABC")
            slot((None, TILES), "BC")
            slot((None, TILES + 1), "C")

        with nc.Block() as block:
            @block.sync
            def _(sp):
                consts_ = ((hsel[:, :], hrows), (sink[:, :], sinks.broadcast_to([P, HEADS])),
                           (lora[0:HD, :], w_up), (lora[HD:P, :], a_up), (gup[:, :], g_up),
                           (lng[:, :], lnx_g.broadcast_to([P, RW])), (lnb[:, :], lnx_b.broadcast_to([P, RW])))
                load_qkv(sp, 0)
                sp.dma_start(con[:, :], consts).then_inc(con_in, 16)
                load_rw(sp, 0)
                sp.dma_start(par[:, :], params).then_inc(par_in, 16)
                sp.dma_start(bias[:, :, :], bass.AP(skew, P - 1, [[EXT - 1, P], [P * EXT, HEADS], [1, 2 * P]])).then_inc(b_rd, 16)
                for dst, src in consts_:
                    sp.dma_start(dst, src).then_inc(c_in, 16)

                def slot(s, stages, last=False):
                    if "A" in stages and not last:
                        sp.wait_ge(*pdone(s, "score_b"))
                        sp.sem_inc(passed, 1)
                        load_qkv(sp, tile(s, "A") + 1)
                        sp.wait_ge(*gdone(s, "zs"))
                        sp.sem_inc(passed, 1)
                        load_rw(sp, tile(s, "A") + 1)
                    if "C" in stages:
                        sp.wait_ge(*adone(s, "out_copy"))
                        sp.sem_inc(passed, 1)
                        sp.dma_start(mixT[0:PAIRS, :, bass.ds(tile(s, "C") * P, P)].rearrange("f p t -> p f t"),
                                     rwT[:, :, :]).then_inc(rw_stored, 16)
                    if "A" in stages:
                        sp.wait_ge(*adone(s, "att_copy"))
                        sp.sem_inc(passed, 1)
                        sp.dma_start(mixT[PAIRS:, :, bass.ds(tile(s, "A") * P, P)].rearrange("f p t -> p f t"),
                                     attT[:, :, :]).then_inc(att_stored, 16)

                slot((None, 0), "A")
                slot((None, 1), "AB")
                with sp.Fori(0, TILES - 3) as it:
                    slot((it, 2), "ABC")
                slot((None, TILES - 1), "ABC", last=True)
                for c in range(2):
                    sp.dma_start(raw_f[:, c, :, :], w_out[c]).then_inc(raw_in_f[c], 16)
                sp.wait_ge(rw_stored, 16 * (TILES - 2) + 16)
                sp.wait_ge(att_stored, 16 * TILES + 16)
                sp.dma_start(stage_f[:, :, :].rearrange("p j d -> p (j d)").rearrange("p (k t) -> p k t", k=DK),
                             mixT[:, :, 0:TBK].rearrange("k p t -> p k t")).then_inc(first_mix_in, 16)
                slot((None, TILES), "BC")
                slot((None, TILES + 1), "C")
                sp.wait_ge(rw_stored, 16 * TILES + 16)
                sp.wait_ge(att_stored, 16 * TILES + 16)
                sp.wait_ge(c_in, 16 * CONSTS)

            @block.tensor
            def _(pe):
                T = nc.tensor
                start(pe, pe_counts)
                pe.wait_ge(con_in, 16)
                head = lambda a, h: a[:, h * HD:(h + 1) * HD]

                def slot(s, stages):
                    A, B, C = (st in stages for st in "ABC")
                    after = lambda done, label: pe.wait_ge(*done(s, label))

                    def first_transposes():
                        before = (s[0], s[1] - 1)
                        for q in range(2):
                            pe.wait_ge(*vdone(before, f"masked{4 * q + 3}"))
                            if C and q:
                                pe.wait_ge(*vdone(before, "y_center"))
                            pe.sem_inc(passed, 1)
                            for j in range(4):
                                mm = T.transpose(ps[:, 4 + 2 * q, j * P:(j + 1) * P], bm[:, 4 * q + j, 0, :], ident)
                            mm.then_inc(pmark(f"first_t{q}"), 1)

                    def attention_scores():
                        pe.wait_ge(qkv_in, 32 * (tile(s, "A") + 1))
                        for b in range(2):
                            mm = T.transpose(ps[:, 0, b * P:(b + 1) * P], kvT[:, 1, b * P:(b + 1) * P], ident)
                        mm.then_inc(pmark("v_keys"), 1)
                        for g, kv in groups.items():
                            if g == "b":
                                after(adone, "v_copy")
                            rows = slice(kv * HD, (kv + 1) * HD)
                            for j in range(PAIRS):
                                mm = T.matmul(ps[:, 2 - 2 * kv + j // 2, (j % 2) * 2 * P:(j % 2 + 1) * 2 * P],
                                              qT[rows, j, :], kvT[rows, 0, :], start=True, stop=True)
                            mm.then_inc(pmark("score_" + g), 1)

                    def low_rank():
                        pe.wait_ge(c_in, 16 * CONSTS)
                        after(adone, "tanh_w")
                        after(vdone, "logit_a")
                        for f in range(PAIRS):
                            mm = T.matmul(ps[:, 2, f * P:(f + 1) * P], lora[0:HD, f * P:(f + 1) * P], th[:, :],
                                          start=True, stop=True)
                        mm.then_inc(pmark("lora_w"), 1)
                        for f in range(PAIRS):
                            mm = T.matmul(ps[:, 3, f * P:(f + 1) * P], lora[HD:P, f * P:(f + 1) * P], zs[HD:P, 12, :],
                                          start=True, stop=True)
                        mm.then_inc(pmark("lora_a"), 1)

                    def key_norms():
                        after(adone, "kk_sq")
                        after(vdone, "logit_b")
                        for f in range(PAIRS):
                            mm = T.matmul(ps[0:HEADS, 1, 0:P], head_of[:, f, :], kk_sq[:, f, :],
                                          start=(f == 0), stop=(f == PAIRS - 1))
                        mm.then_inc(pmark("kk_norm"), 1)

                    def norm_rows():
                        after(vdone, "norm_inv")
                        for f in range(PAIRS):
                            mm = T.matmul(ps[:, 1, f * P:(f + 1) * P], hsel[:, f * P:(f + 1) * P], nrm[:, :],
                                          start=True, stop=True)
                        mm.then_inc(pmark("norm_rows"), 1)

                    def turn_probs(g, kv):
                        after(vdone, "probs_" + g)
                        after(*((adone, "sig_a") if g == "a" else (vdone, "kk")))
                        if C and g == "b":
                            after(adone, "out_copy")
                        for b in range(2):
                            for j in range(PAIRS):
                                mm = T.transpose(ps[:, 2 - 2 * kv + b, j * P:(j + 1) * P],
                                                 logit[:, 4 * kv + j, b * P:(b + 1) * P], ident)
                        mm.then_inc(pmark("probs_t_" + g), 1)

                    def probs_by_values(g, kv):
                        after(adone, "pt_copy_" + g)
                        for b in range(2):
                            mm = T.matmul(ps[kv * HD:(kv + 1) * HD, 2, :], vk[:, b, kv * HD:(kv + 1) * HD],
                                          pt[:, kv, b, :, :], start=(b == 0), stop=(b == 1))
                        mm.then_inc(pmark("pv_" + g), 1)

                    def tokens_major(name, bank_, src, made):
                        after(*made)
                        if name == "v":
                            after(adone, "att_copy")
                        if name == "alpha":
                            after(adone, "bonus_copy")
                        for f in range(PAIRS):
                            mm = T.transpose(ps[:, bank_, f * P:(f + 1) * P], src[:, f, :], ident)
                        mm.then_inc(pmark("t_" + name), 1)

                    def delta_scores():
                        after(vdone, "rho")
                        for h in range(HEADS):
                            rows, f, b = slice((h % 2) * HD, (h % 2 + 1) * HD), h // 2, score_banks[h % 4]
                            after(*((vdone, f"masked{h - 4}") if h >= 4 else
                                    (adone, ("beta_t", "kappa_t", "alpha_t", "v_t")[h])))
                            rhs = ar[rows, f, :, :]
                            T.matmul(ps[:, b, 0:2 * P], betaT[rows, f, :], rhs, start=True, stop=True)
                            T.matmul(ps[:, b, 2 * P:], kappaT[rows, f, :], rhs, start=True, stop=True).then_inc(
                                pmark(f"rw_score{h}"), 1)

                    def bonus():
                        after(gdone, "rk_rk")
                        for f in range(PAIRS):
                            mm = T.matmul(ps[:, 3, 2 * f:2 * f + 2], rk[:, f, :], cst("pair_sel"), start=True, stop=True)
                        mm.then_inc(pmark("bonus"), 1)

                    def output_gate():
                        after(adone, "sig_g")
                        T.matmul(bank(7), sg[:, :], gup[:, :], start=True, stop=True).then_inc(pmark("gate"), 1)

                    def level_ax(l):
                        for q in range(2):
                            after(vdone, f"x_first{q}" if l == 1 else f"x_next{l - 1}_{q}")
                            for j in range(4):
                                h = 4 * q + j
                                mm = T.matmul(ps[:, 4 + 2 * q, j * P:(j + 1) * P], bm[:, h, 0, :], x_m[:, h, :],
                                              start=True, stop=True)
                            mm.then_inc(pmark(f"ax{l}_{q}"), 1)

                    def level_xax(l):
                        for q in range(2):
                            after(vdone, f"ax_masked{l}_{q}")
                            if l == 1:
                                after(gdone, f"xt_first{q}")
                            for j in range(4):
                                h = 4 * q + j
                                if l < LEVELS - 1:
                                    T.matmul(ps[:, 5 + 2 * q, j * P:(j + 1) * P], xt_m[:, h, :], ax[:, h, :],
                                             start=True, stop=True)
                                mm = T.matmul(ps[:, 4 + 2 * q, j * P:(j + 1) * P], ax[:, h, :], xt_m[:, h, :],
                                              start=True, stop=True)
                            mm.then_inc(pmark(f"xax{l}_{q}"), 1)

                    def a_by_v():
                        for h in range(HEADS):
                            mm = T.matmul(head(bank(5), h), bm[:, h, 2, :], head(v_t, h), start=True, stop=True)
                        mm.then_inc(pmark("av"), 1)

                    def u_and_w():
                        after(adone, "av_copy")
                        after(vdone, f"x_next{LEVELS - 1}_1")
                        for h in range(HEADS):
                            mm = T.matmul(head(bank(7), h), xt_m[:, h, :], head(avt, h), start=True, stop=True)
                        mm.then_inc(pmark("u"), 1)
                        for h in range(HEADS):
                            rows, f = slice((h % 2) * HD, (h % 2 + 1) * HD), h // 2
                            mm = T.matmul(ps[rows, 4, f * P:(f + 1) * P], head(alpha_t, h), xt_m[:, h, :],
                                          start=True, stop=True)
                        mm.then_inc(pmark("w_t"), 1)

                    def state_apply(c):
                        tok = slice(c * CH, (c + 1) * CH)
                        after(*((adone, "w_copy") if c == 0 else (vdone, "state0")))
                        pe.sem_inc(passed, 1)
                        for h in range(HEADS):
                            rows, f = slice((h % 2) * HD, (h % 2 + 1) * HD), h // 2
                            mm = T.matmul(ps[tok, 5 + h % 2, f * HD:(f + 1) * HD], wT[rows, f, tok], state[rows, c, f, :],
                                          start=True, stop=True)
                        mm.then_inc(pmark(f"sa{c}"), 1)

                    def state_grow(c):
                        tok = slice(c * CH, (c + 1) * CH)
                        after(vdone, f"sa_add{c}")
                        pe.sem_inc(passed, 1)
                        for h in range(HEADS):
                            rows, f = slice((h % 2) * HD, (h % 2 + 1) * HD), h // 2
                            dst = ps[rows, (7, 4)[c], f * HD:(f + 1) * HD]
                            T.matmul(dst, head(kappa_t[tok, :], h), head(v_t[tok, :], h), start=True, stop=False)
                            mm = T.matmul(dst, head(beta_t[tok, :], h), head(sa[tok, :], h), start=False, stop=True)
                        mm.then_inc(pmark(f"grow{c}"), 1)

                    def outputs():
                        for h in range(HEADS):
                            rows, f = slice((h % 2) * HD, (h % 2 + 1) * HD), h // 2
                            dst = ps[:, 5 + h % 2, f * HD:(f + 1) * HD]
                            T.matmul(dst, bm[:, h, 3, :], head(v_t, h), start=(h < 2), stop=False)
                            T.matmul(dst, bm[:, h, 1, :], head(sa, h), start=False, stop=False)
                        for h in range(HEADS):
                            rows, f = slice((h % 2) * HD, (h % 2 + 1) * HD), h // 2
                            for c in range(2):
                                tok = slice(c * CH, (c + 1) * CH)
                                mm = T.matmul(ps[tok, 5 + h % 2, f * HD:(f + 1) * HD], rho[rows, f, tok], state[rows, c, f, :],
                                              start=False, stop=(f == PAIRS - 1))
                        mm.then_inc(pmark("y"), 1)

                    def turn_out():
                        after(gdone, "y_gate")
                        if A:
                            after(vdone, "logit_b")
                        for f in range(PAIRS):
                            mm = T.transpose(ps[:, 0, f * P:(f + 1) * P], y[:, f * P:(f + 1) * P], ident)
                        mm.then_inc(pmark("out_t"), 1)

                    if B: first_transposes()
                    if A: attention_scores()
                    slot_start(pe, s)
                    if B: level_ax(1); level_xax(1)
                    if A: low_rank()
                    if B: level_ax(2); level_xax(2); level_ax(3)
                    if A: key_norms()
                    if B: level_xax(3); level_ax(4); level_xax(4)
                    if A: norm_rows()
                    if B: level_ax(5); a_by_v(); level_xax(5)
                    if A: turn_probs("a", 0)
                    if B: u_and_w()
                    if C: turn_out()
                    if A: turn_probs("b", 1)
                    if B: state_apply(0)
                    if A: probs_by_values("a", 0)
                    if B: state_grow(0)
                    if A: bonus()
                    if B: state_apply(1)
                    if A: probs_by_values("b", 1)
                    if B: state_grow(1)
                    if A:
                        output_gate()
                        tokens_major("beta", 0, betaT[:, :, :], (vdone, "beta"))
                        tokens_major("alpha", 3, ar[:, :, 0, :], (vdone, "alpha"))
                        tokens_major("kappa", 1, kappaT[:, :, :], (vdone, "kappa"))
                    if B: outputs()
                    if A:
                        tokens_major("v", 2, zs[:, 8:12, :], (gdone, "zs"))
                        delta_scores()

                all_slots(pe, slot)

            @block.vector
            def _(dve):
                V = nc.vector
                start(dve, dve_counts)
                V.memset(lnx_eps[:, :], LNX_EPS).then_inc(set_up, 1)
                V.memset(state[:, :, :, :], 0.0).then_inc(set_up, 1)
                dve.wait_ge(par_in, 16)
                V.tensor_scalar(one_minus_ka[:, :], col("k_a"), -1.0, 1.0, ALU.mult, ALU.add).then_inc(set_up, 1)
                dve.wait_ge(set_up, 3)
                dve.wait_ge(con_in, 16)
                dve.wait_ge(c_in, 16 * CONSTS)
                dve.wait_ge(b_rd, 16)

                def slot(s, stages):
                    A, B, C = (st in stages for st in "ABC")
                    after = lambda done, label: dve.wait_ge(*done(s, label))
                    own = lambda label: after(vdone, label)
                    r = zs[:, 0:4, :]
                    heads = lambda q: slice(4 * q, 4 * q + 4)
                    in_bank = lambda b: bank(b).rearrange("p (h t) -> p h t", h=4)

                    def first_inverse(q):
                        hs = heads(q)
                        after(pdone, f"first_t{q}")
                        V.tensor_tensor(x_m[:, hs, :], in_bank(4 + 2 * q), four(level_mask[:, 0, :]),
                                        ALU.mult).then_inc(vmark(f"a_first{q}"), 1)
                        own(f"a_first{q}")
                        V.tensor_tensor(x_m[:, hs, :], x_m[:, hs, :], four(ident), ALU.add).then_inc(vmark(f"x_first{q}"), 1)

                    def mask_ax(l):
                        for q in range(2):
                            after(pdone, f"ax{l}_{q}")
                            V.tensor_tensor(ax[:, heads(q), :], in_bank(4 + 2 * q), four(level_mask[:, l, :]),
                                            ALU.mult).then_inc(vmark(f"ax_masked{l}_{q}"), 1)

                    def next_inverse(l):
                        for q in range(2):
                            hs = heads(q)
                            after(pdone, f"xax{l}_{q}")
                            if l < LEVELS - 1:
                                V.tensor_tensor(x_m[:, hs, :], in_bank(5 + 2 * q), x_m[:, hs, :], ALU.add)
                            V.tensor_tensor(xt_m[:, hs, :], in_bank(4 + 2 * q), xt_m[:, hs, :],
                                            ALU.add).then_inc(vmark(f"x_next{l}_{q}"), 1)

                    def logits(g, kv):
                        hs = heads(kv)
                        after(pdone, "score_" + g)
                        o = V.scalar_tensor_tensor(logit[:, hs, :].rearrange("p h t -> p (h t)"),
                                                   ps[:, 2 - 2 * kv:4 - 2 * kv, :].rearrange("p b t -> p (b t)"), HD ** -0.5,
                                                   bias[:, hs, :].rearrange("p h t -> p (h t)"), ALU.mult, ALU.add)
                        if s[0] is None and s[1] == 0:
                            o.then_inc(first_logit, 1)
                            dve.wait_ge(first_logit, kv + 1)
                            o = V.tensor_scalar(logit[:, hs, 0:P], logit[:, hs, 0:P], NEG, None, ALU.add)
                        o.then_inc(vmark("logit_" + g), 1)

                    def maxima(g, kv):
                        hs = heads(kv)
                        own("logit_" + g)
                        V.tensor_reduce(rowmax[:, hs], logit[:, hs, :], AX.X, ALU.max).then_inc(vmark("rowmax_" + g), 1)
                        own("rowmax_" + g)
                        V.tensor_tensor(rowmax[:, hs], rowmax[:, hs], sink[:, hs], ALU.max).then_inc(vmark("max_" + g), 1)
                        own("max_" + g)
                        V.tensor_scalar(negmax[:, hs], rowmax[:, hs], -1.0, None, ALU.mult).then_inc(vmark("negmax_" + g), 1)
                        V.tensor_tensor(gap[:, hs], sink[:, hs], rowmax[:, hs], ALU.subtract).then_inc(vmark("sink_gap_" + g), 1)

                    def probabilities(g, kv):
                        hs = heads(kv)
                        after(adone, "exp_sink_" + g)
                        V.tensor_tensor(den[:, hs], den[:, hs], esink[:, hs], ALU.add).then_inc(vmark("denom_" + g), 1)
                        own("denom_" + g)
                        V.reciprocal(den[:, hs], den[:, hs]).then_inc(vmark("inv_" + g), 1)
                        own("inv_" + g)
                        V.tensor_tensor(logit[:, hs, :], logit[:, hs, :], over(den[:, hs], 2 * P), ALU.mult).then_inc(vmark("probs_" + g), 1)

                    def decay_sums():
                        after(adone, "sig_w")
                        V.tensor_tensor_scan(cum[:, :, :].rearrange("p f t -> p (f t)"), cst("chunk_start"),
                                             sw[:, :, :].rearrange("p f t -> p (f t)"), 0.0, ALU.mult, ALU.add).then_inc(vmark("cum"), 1)

                    def inverse_norms():
                        after(adone, "norm_sqrt")
                        V.tensor_scalar(nrm[:, :], nrm[:, :], 1e-12, None, ALU.max).then_inc(vmark("norm_floor"), 1)
                        own("norm_floor")
                        V.reciprocal(nrm[:, :], nrm[:, :]).then_inc(vmark("norm_inv"), 1)

                    def key_scales():
                        after(adone, "sig_a")
                        for f in range(PAIRS):
                            o = V.tensor_scalar(ascale[:, f, :], av[:, f, :], col("k_a")[:, f:f + 1], one_minus_ka[:, f:f + 1],
                                                ALU.mult, ALU.add)
                        o.then_inc(vmark("a_scale"), 1)

                    def normal_keys():
                        after(pdone, "norm_rows")
                        V.tensor_tensor(kk[:, :, :], bank(1).rearrange("p (f t) -> p f t", t=P), kk_raw[:, :, :],
                                        ALU.mult).then_inc(vmark("kk"), 1)
                        own("kk")
                        after(adone, "p_exc")
                        V.scalar_tensor_tensor(ar[:, :, 0, :], kk[:, :, :], -1.0, p_exc[:, :, :], ALU.mult, ALU.mult).then_inc(vmark("alpha"), 1)

                    def beta():
                        after(gdone, "kk_a")
                        V.tensor_tensor(betaT[:, :, :], kka[:, :, :], p_inv[:, :, :], ALU.mult).then_inc(vmark("beta"), 1)

                    def kappa_rho():
                        after(gdone, "kmod")
                        V.tensor_tensor(kappaT[:, :, :], kmod[:, :, :], p_inv[:, :, :], ALU.mult).then_inc(vmark("kappa"), 1)
                        V.tensor_tensor(ar[:, :, 1, :], r, p_inc[:, :, :], ALU.mult).then_inc(vmark("rho"), 1)

                    def masks(hs):
                        for h in hs:
                            after(pdone, f"rw_score{h}")
                            V.tensor_tensor(bm[:, h, :, :], ps[:, score_banks[h % 4], :].rearrange("p (a t) -> p a t", a=4),
                                            score_mask, ALU.mult).then_inc(vmark(f"masked{h}"), 1)

                    def chunk(c):
                        tok = slice(c * CH, (c + 1) * CH)
                        after(pdone, f"sa{c}")
                        V.tensor_tensor(by_parity(sa[tok, :]), ps[tok, 5:7, 0:PAIRS * HD].rearrange("p a (f v) -> p a f v", f=PAIRS),
                                        by_parity(u_t[tok, :]), ALU.add).then_inc(vmark(f"sa_add{c}"), 1)
                        after(pdone, f"grow{c}")
                        V.tensor_tensor(grow[:, :, :], ps[:, (7, 4)[c], 0:PAIRS * HD].rearrange("p (f v) -> p f v", f=PAIRS),
                                        state[:, c, :, :], ALU.add).then_inc(vmark(f"grow_add{c}"), 1)
                        own(f"grow_add{c}")
                        if c == 1:
                            after(pdone, "y")
                        V.tensor_tensor(state[:, 1 - c, :, :], grow[:, :, :],
                                        ends[:, :, c:c + 1].broadcast_to([P, PAIRS, HD]), ALU.mult).then_inc(vmark(f"state{c}"), 1)

                    y_ps = ps[:, 5:7, 0:PAIRS * HD].rearrange("p a (f v) -> p f a v", f=PAIRS)
                    y3 = lambda a: a[:, :].rearrange("p (h v) -> p h v", h=HEADS)

                    def means():
                        V.tensor_reduce(ysum[:, :].rearrange("p (f a) -> p f a", a=2), y_ps, AX.X, ALU.add).then_inc(vmark("y_sum"), 1)
                        own("y_sum")
                        V.tensor_scalar(ysum[:, :], ysum[:, :], 1.0 / HD, None, ALU.mult).then_inc(vmark("y_mean"), 1)

                    def center():
                        own("y_mean")
                        if C:
                            after(pdone, "out_t")
                        V.tensor_tensor(y[:, :].rearrange("p (f a v) -> p f a v", a=2, v=HD), y_ps,
                                        ysum[:, :].rearrange("p (f a) -> p f a", a=2).unsqueeze(3).broadcast_to([P, PAIRS, 2, HD]),
                                        ALU.subtract).then_inc(vmark("y_center"), 1)

                    def variances():
                        after(gdone, "y_sq")
                        V.tensor_reduce(yss[:, :], y3(ysq), AX.X, ALU.add).then_inc(vmark("y_sqsum"), 1)

                    def normalise():
                        after(adone, "y_rms")
                        V.reciprocal(yss[:, :], yss[:, :]).then_inc(vmark("y_inv"), 1)
                        own("y_inv")
                        V.tensor_tensor(y3(y), y3(y), over(yss[:, :], HD), ALU.mult).then_inc(vmark("y_norm"), 1)

                    slot_start(dve, s)
                    if B: first_inverse(0); first_inverse(1)
                    if A: logits("a", 0)
                    if B: mask_ax(1)
                    if A: logits("b", 1)
                    if B: next_inverse(1)
                    if A: maxima("a", 0)
                    if B: mask_ax(2)
                    if A: maxima("b", 1)
                    if B: next_inverse(2)
                    if C: variances()
                    if B: mask_ax(3)
                    if A: decay_sums()
                    if B: next_inverse(3); mask_ax(4)
                    if A: inverse_norms()
                    if C: normalise()
                    if B: next_inverse(4)
                    if A: normal_keys()
                    if B: mask_ax(5)
                    if A: probabilities("a", 0)
                    if B: next_inverse(5)
                    if A: key_scales(); probabilities("b", 1); beta(); kappa_rho()
                    if B: chunk(0); chunk(1); means()
                    if A: masks(range(2))
                    if B: center()
                    if A:
                        masks(range(2, HEADS))
                        V.tensor_copy(ends[:, :, :], p_inc[:, :, :].rearrange("p f (c t) -> p f c t", c=2)[:, :, :, CH - 1]).then_inc(
                            vmark("p_ends"), 1)

                all_slots(dve, slot)

            @block.gpsimd
            def _(pool):
                G = nc.gpsimd
                start(pool, pool_counts)
                pool.wait_ge(par_in, 16)

                def slot(s, stages):
                    after = lambda done, label: pool.wait_ge(*done(s, label))
                    slot_start(pool, s)
                    A, B, C = (st in stages for st in "ABC")
                    own = lambda label: after(gdone, label)
                    r, k = zs[:, 0:4, :], zs[:, 4:8, :]

                    def shift(part, suffix):
                        now, d = part(zr[:, :, 1:P + 1]), part(zs[:, :, :])
                        G.tensor_tensor(d, part(zr[:, :, 0:P]), now, ALU.subtract).then_inc(gmark("diff" + suffix), 1)
                        own("diff" + suffix)
                        G.tensor_tensor(d, d, part(over(col("mu"), P)), ALU.mult).then_inc(gmark("diff_mu" + suffix), 1)
                        own("diff_mu" + suffix)
                        G.tensor_tensor(d, d, now, ALU.add).then_inc(gmark("zs" + suffix), 1)

                    def first_transposed_inverse(q):
                        hs = slice(4 * q, 4 * q + 4)
                        G.tensor_tensor(xt_m[:, hs, :], bm[:, hs, 0, :], four(cst("first_mask_t")), ALU.mult).then_inc(gmark(f"xt_mask{q}"), 1)
                        own(f"xt_mask{q}")
                        G.tensor_tensor(xt_m[:, hs, :], xt_m[:, hs, :], four(ident), ALU.add).then_inc(gmark(f"xt_first{q}"), 1)

                    if s[0] is None and s[1] == 1:
                        pool.wait_ge(con_in, 16)
                        pool.wait_ge(c_in, 16 * CONSTS)
                    if B: first_transposed_inverse(0)
                    if A:
                        pool.wait_ge(rw_in, 16 * (tile(s, "A") + 1))
                        pool.sem_inc(passed, 1)
                        shift(lambda a: a[:, 12:14, :], "_low")
                    if B: first_transposed_inverse(1)
                    if C: G.tensor_tensor(ysq[:, :], y[:, :], y[:, :], ALU.mult).then_inc(gmark("y_sq"), 1)
                    if A:
                        shift(lambda a: a[:, 4:8, :], "_k")
                        own("zs_k")
                        G.tensor_tensor(kk_raw[:, :, :], k, over(col("k_k"), P), ALU.mult).then_inc(gmark("kk_raw"), 1)
                        shift(lambda a: a[:, 0:12, :].rearrange("p (a f) t -> p a f t", f=PAIRS)[:, 0:3:2], "")
                        after(vdone, "cum")
                        G.tensor_tensor(cumx[:, :, :], cum[:, :, :], sw[:, :, :], ALU.subtract).then_inc(gmark("cum_before"), 1)
                    if C:
                        after(vdone, "y_norm")
                        G.tensor_tensor(y[:, :], y[:, :], lng[:, :], ALU.mult).then_inc(gmark("y_gain"), 1)
                    if C:
                        own("y_gain")
                        G.tensor_tensor(y[:, :], y[:, :], lnb[:, :], ALU.add).then_inc(gmark("y_bias"), 1)
                        own("y_bias")
                        G.tensor_tensor(y[:, :], y[:, :], yb[:, :], ALU.add).then_inc(gmark("y_bonus"), 1)
                    if A:
                        after(vdone, "kk")
                        G.tensor_tensor(kka[:, :, :], kk[:, :, :], av[:, :, :], ALU.mult).then_inc(gmark("kk_a"), 1)
                    if C:
                        own("y_bonus")
                        G.tensor_tensor(y[:, :], y[:, :], gate[:, :], ALU.mult).then_inc(gmark("y_gate"), 1)
                    if A:
                        after(vdone, "a_scale")
                        G.tensor_tensor(kmod[:, :, :], k, ascale[:, :, :], ALU.mult).then_inc(gmark("kmod"), 1)
                    if A:
                        own("kmod")
                        G.tensor_tensor(rk[:, :, :], r, kmod[:, :, :], ALU.mult).then_inc(gmark("rk"), 1)
                        own("rk")
                        G.tensor_tensor(rk[:, :, :], rk[:, :, :], over(col("r_k"), P), ALU.mult).then_inc(gmark("rk_rk"), 1)
                    if B:
                        G.tensor_tensor(yb[:, :].rearrange("p (h v) -> p h v", h=HEADS), v_t[:, :].rearrange("p (h v) -> p h v", h=HEADS),
                                        over(bon[:, :], HD), ALU.mult).then_inc(gmark("bonus_v"), 1)

                all_slots(pool, slot)

            @block.scalar
            def _(act):
                S = nc.scalar
                start(act, act_counts)
                for count in (att_stored, rw_stored):
                    act.sem_inc(count, 16)
                act.wait_ge(par_in, 16)
                act.wait_ge(set_up, 3)

                def slot(s, stages):
                    A, B, C = (st in stages for st in "ABC")
                    after = lambda done, label: act.wait_ge(*done(s, label))

                    def activations():
                        after(pdone, "v_keys")
                        S.activation(vk[:, :, :], ps[:, 0, 0:2 * P].rearrange("p (b t) -> p b t", b=2), ACT.Copy).then_inc(amark("v_copy"), 1)
                        after(gdone, "zs_low")
                        S.activation(th[:, :], zs[0:HD, 12, :], ACT.Tanh).then_inc(amark("tanh_w"), 1)
                        S.activation(sg[:, :], zs[:, 13, :], ACT.Sigmoid).then_inc(amark("sig_g"), 1)
                        for label, made, dst, bank_, base in (("sig_w", "lora_w", sw, 2, "w0"), ("sig_a", "lora_a", av, 3, "a0")):
                            after(pdone, made)
                            for f in range(PAIRS):
                                o = S.activation(dst[:, f, :], ps[:, bank_, f * P:(f + 1) * P], ACT.Sigmoid, bias=col(base)[:, f:f + 1])
                            o.then_inc(amark(label), 1)
                        after(gdone, "kk_raw")
                        S.activation(kk_sq[:, :, :], kk_raw[:, :, :], ACT.Square).then_inc(amark("kk_sq"), 1)

                    def roots():
                        if C:
                            after(vdone, "y_sqsum")
                            S.activation(yss[:, :], yss[:, :], ACT.Sqrt, scale=1.0 / HD, bias=lnx_eps[:, 0:1]).then_inc(amark("y_rms"), 1)
                        if A:
                            after(pdone, "kk_norm")
                            S.activation(nrm[:, :], ps[0:HEADS, 1, 0:P], ACT.Sqrt).then_inc(amark("norm_sqrt"), 1)

                    def exponentials():
                        after(vdone, "cum")
                        S.activation(p_inc[:, :, :], cum[:, :, :], ACT.Exp, scale=-DECAY).then_inc(amark("p_inc"), 1)
                        S.activation(p_inv[:, :, :], cum[:, :, :], ACT.Exp, scale=DECAY).then_inc(amark("p_inv"), 1)
                        for g, kv in groups.items():
                            if g == "b":
                                after(gdone, "cum_before")
                                S.activation(p_exc[:, :, :], cumx[:, :, :], ACT.Exp, scale=-DECAY).then_inc(amark("p_exc"), 1)
                            hs = slice(4 * kv, 4 * kv + 4)
                            after(vdone, "sink_gap_" + g)
                            for h in range(4 * kv, 4 * kv + 4):
                                o = S.activation(logit[:, h, :], logit[:, h, :], ACT.Exp, bias=negmax[:, h:h + 1],
                                                 accum_out=den[:, h:h + 1])
                            o.then_inc(amark("exp_" + g), 1)
                            S.activation(esink[:, hs], gap[:, hs], ACT.Exp).then_inc(amark("exp_sink_" + g), 1)

                    def copy_probs(g, kv):
                        after(pdone, "probs_t_" + g)
                        S.activation(pt[:, kv, :, :, :].rearrange("p b j t -> p (b j t)"),
                                     ps[:, 2 - 2 * kv:4 - 2 * kv, :].rearrange("p b t -> p (b t)"), ACT.Copy).then_inc(amark("pt_copy_" + g), 1)

                    def copy_attention():
                        after(pdone, "pv_b")
                        act.wait_ge(att_stored, 16 * tile(s, "A") + 16)
                        S.activation(attT[:, :, :], bank(2).rearrange("p (j t) -> p j t", j=PAIRS), ACT.Copy).then_inc(amark("att_copy"), 1)

                    def copy_tokens_major():
                        for name, dst, bank_, used in (("alpha", alpha_t, 3, "w_t"), ("beta", beta_t, 0, "grow1"),
                                                       ("kappa", kappa_t, 1, "grow1"), ("v", v_t, 2, "y")):
                            after(pdone, "t_" + name)
                            if B:
                                act.sem_inc(passed, 1)
                                after(pdone, used)
                                if name == "v":
                                    after(gdone, "bonus_v")
                            S.activation(dst[:, :], bank(bank_), ACT.Copy).then_inc(amark(name + "_t"), 1)
                        after(vdone, "rho")
                        S.activation(rho[:, :, :], ar[:, :, 1, :], ACT.Copy).then_inc(amark("rho_copy"), 1)

                    def copy_out():
                        after(pdone, "out_t")
                        act.wait_ge(rw_stored, 16 * tile(s, "C") + 16)
                        S.activation(rwT[:, :, :], bank(0).rearrange("p (f t) -> p f t", f=PAIRS), ACT.Copy).then_inc(amark("out_copy"), 1)

                    def keep_gate():
                        if C:
                            after(gdone, "y_gate")
                        S.activation(gate[:, :], gate_new[:, :], ACT.Copy).then_inc(amark("gate_keep"), 1)

                    def copy(label, made, dst, src):
                        after(pdone, made)
                        S.activation(dst, src, ACT.Copy).then_inc(amark(label), 1)

                    slot_start(act, s)
                    if A: activations()
                    roots()
                    if A: exponentials()
                    if B: copy("av_copy", "av", avt[:, :], bank(5))
                    if A: copy_probs("a", 0)
                    if B:
                        copy("u_copy", "u", u_t[:, :], bank(7))
                        copy("w_copy", "w_t", wT[:, :, :], bank(4).rearrange("p (f t) -> p f t", f=PAIRS))
                    if C: copy_out()
                    if B: keep_gate()
                    if A:
                        copy_probs("b", 1)
                        if B:
                            after(gdone, "bonus_v")
                        copy("bonus_copy", "bonus", bon[:, :], ps[:, 3, 0:HEADS])
                        copy_attention()
                        copy("gate_copy", "gate", gate_new[:, :], bank(7))
                        copy_tokens_major()

                all_slots(act, slot)


HG, HGD = 4, FF // 4
TBK = 512
BLOCKS = SEQ // TBK
NJ = [(n, j) for n in range(2) for j in range(4)]
each = lambda s, ns=(0, 1): [f"{s}{n}_{j}" for n in ns for j in range(4)]
ks_of = lambda s, ks: [f"{s}{k}" for k in ks]
PE_L = (each("out", [0]) + ["pt0", "pt1"] + each("out", [1]) + ks_of("ut", range(4)), each("up") + each("down"),
        each("ple", [0]) + ks_of("xt", range(4)) + each("ple", [1]) + ks_of("xt", range(4, DK)) + each("gate"))
ACT_L = (["p_hi0", "p_hi1"] + [f"{s}{j}" for j in range(4) for s in ("ss", "rms")] + ks_of("u_hi", range(DK)),
         [f"{s}{n}_{j}" for n, j in NJ for s in ("relu", "h_hi")],
         each("e_copy", [0]) + ks_of("x2_hi", range(4)) + each("e_copy", [1]) + ks_of("x2_hi", range(4, DK))
         + [f"{s}{j}" for s in ("ess", "erms") for j in range(4)] + ["mix_hi0", "mix_hi1"] + each("sig")
         + [f"{s}{j}" for s in ("fss", "frms") for j in range(4)])
DVE_L = (each("out_add", [0]) + ["p_lo0", "p_lo1", "out_add1_0", "out_add1_1", "inv0", "xn0", "out_add1_2", "inv1", "xn1",
                                 "out_add1_3", "inv2", "xn2", "inv3", "xn3"] + ks_of("u_lo", range(DK)),
         [f"{s}{n}_{j}" for n, j in NJ for s in ("square", "h_lo")] + each("down_add"),
         ks_of("x2_lo", range(DK)) + [f"{s}{j}" for j in range(4) for s in ("einv", "e_norm")]
         + ["mix_lo0", "mix_lo1"] + [f"{s}{n}_{j}" for n, j in NJ for s in ("gmul", "x_add")]
         + [f"{s}{j}" for j in range(4) for s in ("finv", "fout")])


def nested_progress(parts, sem):
    pre, mid, post = parts
    total, seen = len(pre) + HG * len(mid) + len(post), []

    def mark(label):
        steps = pre + mid + post
        expected = steps[len(seen) % len(steps)]
        assert expected == label, (expected, label)
        seen.append(label)
        return sem

    def done(b, g, label, blocks_back=0):
        base = total * (1 - blocks_back)
        if label in pre:
            return sem, b * total + (base + pre.index(label) + 1)
        if label in mid:
            return sem, b * total + g * len(mid) + (base + len(pre) + mid.index(label) + 1)
        return sem, b * total + (base + len(pre) + HG * len(mid) + post.index(label) + 1)

    return mark, done, total


def finish_layer(nc, x, p, mixT, out, params, consts, ple_g, final_g, w_out, w_up, w_down, w_ple, w_gate, first_block):
    raw, stage, raw_in, first_mix_in = first_block
    PRE, MID, POST = 4, 8, 6
    PER = PRE + HG * MID + POST
    with ExitStack() as ctx:
        sb = lambda n, s, d=F32: ctx.enter_context(nc.sbuf_tensor(n, s, d))
        sem = lambda n: ctx.enter_context(nc.semaphore(n))
        ps = ctx.enter_context(nc.psum_tensor("ps_f", [P, 8, 512], F32))
        par, ident = sb("par_f", [P, NPV]), sb("ident_f", [P, P])
        pleg, fing = sb("pleg_f", [P, D]), sb("fing_f", [P, D])
        eps = sb("eps_f", [P, 1])
        w_hi, w_lo = sb("whi_f", [P, 2, 4, 512], F32R), sb("wlo_f", [P, 2, 4, 512], F32R)
        xr = sb("x_f", [P, 4, D])
        act_hi, act_lo = sb("acthi_f", [P, DK, TBK], F32R), sb("actlo_f", [P, DK, TBK], F32R)
        h_hi, h_lo = sb("hhi_f", [P, 8, TBK], F32R), sb("hlo_f", [P, 8, TBK], F32R)
        tmp, sq = sb("tmp_f", [P, 2, 512]), sb("sq_f", [P, 2, 512])
        pin = sb("p_f", [P, 4, PLE])
        pT_hi, pT_lo = sb("pthi_f", [P, 2, TBK], F32R), sb("ptlo_f", [P, 2, TBK], F32R)
        e = sb("e_f", [P, 4, D])
        stat = sb("stat_f", [P, 3, 4])
        junk = sb("junk_f", [P, D])
        gain = par[:, PV["norm_mlp_g"][0]:PV["norm_mlp_g"][1]]
        stage_half = lambda h: stage[:, 2 * h:2 * h + 2, :].rearrange("p j d -> p (j d)")
        act_half = lambda a, h: a[:, 4 * h:4 * h + 4, :].rearrange("p k t -> p (k t)")

        const_in, gains_in, eps_done, passed = sem("const_in_f"), sem("gains_in_f"), sem("eps_f_done"), sem("passed_f")
        w_hi_done, w_lo_done, w_used = sem("w_hi_f_done"), sem("w_lo_f_done"), sem("w_used_f")
        x_in, mix_in, p_in, stored = sem("x_in_f"), sem("mix_in_f"), sem("p_in_f"), sem("stored_f")
        pe_done, dve_done, act_done = sem("pe_done_f"), sem("dve_done_f"), sem("act_done_f")
        first_hi = sem("first_hi_f")
        pmark, pdone, PT = nested_progress(PE_L, pe_done)
        vmark, vdone, VT = nested_progress(DVE_L, dve_done)
        amark, adone, AT = nested_progress(ACT_L, act_done)

        with nc.Block() as block:
            @block.sync
            def _(sp):
                for dst, src in ((par[:, :], params), (ident[:, :], consts[:, CC["ident"][0]:CC["ident"][1]])):
                    sp.dma_start(dst, src).then_inc(const_in, 16)

                def load(n, s, src, k=4):
                    sp.wait_ge(w_lo_done, n + 1)
                    sp.sem_inc(passed, 1)
                    sp.dma_start(raw[:, s, 0:k, :], src).then_inc(raw_in[s], 16)

                for dst, src in ((pleg[:, :], ple_g.broadcast_to([P, D])), (fing[:, :], final_g.broadcast_to([P, D]))):
                    sp.dma_start(dst, src).then_inc(gains_in, 16)
                with sp.Fori(0, BLOCKS) as b:
                    for c in range(2, PRE):
                        load(b * PER + c, c % 2, w_out[c])
                    with sp.Fori(0, HG) as g:
                        for c in range(MID):
                            src = w_up if c < 4 else w_down
                            load(b * PER + g * MID + (PRE + c), c % 2,
                                 src[bass.ds(g * 4 + c % 4, 1)].rearrange("n p k f -> p (n k) f"))
                    for c in range(POST):
                        src = w_ple[c] if c < 2 else w_gate[c - 2]
                        load(b * PER + (PRE + HG * MID + c), c % 2, src, 2 if c < 2 else 4)
                    for c in range(2):
                        load(b * PER + (PER + c), c % 2, w_out[c])

            @block.gpsimd
            def _(pool):
                pool.sem_inc(w_lo_done, 2)

                def low_parts(first, chunks):
                    with pool.Fori(0, chunks // 2) as c:
                        for s in range(2):
                            pool.wait_ge(w_hi_done, first + 2 * c + (s + 1))
                            nc.gpsimd.tensor_tensor(w_lo[:, s, :, :], raw[:, s, :, :], w_hi[:, s, :, :].bitcast(F32),
                                                    ALU.subtract).then_inc(w_lo_done, 1)

                def load_mix(b):
                    pool.dma_start(stage[:, :, :].rearrange("p j d -> p (j d)").rearrange("p (k t) -> p k t", k=DK),
                                   mixT[:, :, bass.ds(b * TBK, TBK)].rearrange("k p t -> p k t")).then_inc(mix_in, 16)

                with pool.Fori(0, BLOCKS - 1) as b:
                    low_parts(b * PER, PRE + 2)
                    pool.wait_ge(*pdone(b, 0, "ut3"))
                    pool.sem_inc(passed, 1)
                    load_mix(b + 1)
                    low_parts(b * PER + (PRE + 2), PER - PRE - 2)
                low_parts((BLOCKS - 1) * PER, PRE + 2)
                pool.wait_ge(*pdone(BLOCKS - 1, 0, "ut3"))
                load_mix(0)
                low_parts((BLOCKS - 1) * PER + (PRE + 2), PER - PRE)

            @block.tensor
            def _(pe):
                T = nc.tensor
                pe.sem_inc(w_used, 1)
                pe.sem_inc(pe_done, PT)
                pe.wait_ge(const_in, 32)

                def products(bank, s, k0, ks, weights_still, j, hi, lo, first, final, label, ready_k=None):
                    for k in range(ks):
                        if ready_k is not None and k:
                            pe.wait_ge(*ready_k(k))
                        if weights_still:
                            wh, wl = (w[:, s, k, j * P:(j + 1) * P] for w in (w_hi, w_lo))
                            pairs = ((wh, hi[:, k0 + k, :]), (wh, lo[:, k0 + k, :]), (wl, hi[:, k0 + k, :]))
                        else:
                            ah, al = (a[:, k0 + k, j * P:(j + 1) * P] for a in (hi, lo))
                            pairs = ((ah, w_hi[:, s, k, :]), (ah, w_lo[:, s, k, :]), (al, w_hi[:, s, k, :]))
                        for t, (still, moving) in enumerate(pairs):
                            mm = T.matmul(ps[:, bank, :], still, moving, start=(first and k == 0 and t == 0),
                                          stop=(final and k == ks - 1 and t == 2))
                            if j == 0 and k == 0 and t == 0:
                                mm.then_inc(w_used, 1)
                    if final:
                        mm.then_inc(pmark(label), 1)

                def project(name, n, n_chunk, banks, weights_still, hi, lo, free, ready=None, ready_k=None, chunks=2, ks=4):
                    for c in range(chunks):
                        pe.wait_ge(w_lo_done, n_chunk + (c + 3))
                        for j in range(4):
                            if c == 0 and free is not None:
                                pe.wait_ge(*free(j))
                            if ready is not None and j == 0:
                                pe.wait_ge(*ready(c))
                            products(banks + j, (c if chunks == 2 else n) % 2, c * ks, ks, weights_still, j, hi, lo,
                                     c == 0, c == chunks - 1, f"{name}{n}_{j}", ready_k if c == j == 0 else None)

                def turn(label, bank, src, k):
                    for j in range(4):
                        mm = T.transpose(ps[:, bank, j * P:(j + 1) * P], src[:, j, k * P:(k + 1) * P], ident[:, :])
                    mm.then_inc(pmark(f"{label}{k}"), 1)

                with pe.Fori(0, BLOCKS) as b:
                    project("out", 0, b * PER, 0, False, h_hi, h_lo, free=lambda j: adone(b, 0, f"sig0_{j}", 1),
                            ready=lambda c: vdone(b, 0, f"mix_lo{c}", 1))
                    pe.wait_ge(p_in, 16 * (b + 1))
                    for k in range(2):
                        pe.wait_ge(*adone(b, 0, f"sig1_{k + 2}", 1))
                        turn("pt", 6 + k, pin, k)
                    project("out", 1, b * PER + 2, 4, False, h_hi, h_lo,
                            free=lambda j: adone(b, 0, f"sig1_{j}", 1) if j < 2 else vdone(b, 0, f"p_lo{j - 2}"))
                    for j in range(4):
                        pe.wait_ge(*vdone(b, 0, f"xn{j}"))
                        if j == 0:
                            pe.sem_inc(passed, 1)
                            pe.wait_ge(*vdone(b, 0, "out_add1_3"))
                        for k in range(DK):
                            mm = T.transpose(ps[:, k, j * P:(j + 1) * P], stage[:, j, k * P:(k + 1) * P], ident[:, :])
                        mm.then_inc(pmark(f"ut{j}"), 1)
                    with pe.Fori(0, HG) as g:
                        for n in range(2):
                            ahead = b * VT + g * len(DVE_L[1]) + (VT + len(DVE_L[0]) - 7 + 4 * n)
                            project("up", n, b * PER + g * MID + (PRE + 2 * n), 4 * n, True, act_hi, act_lo,
                                    free=lambda j: (dve_done, ahead + j),
                                    ready=(lambda c: vdone(b, 0, "u_lo7" if c else "u_lo0")) if n == 0 else None,
                                    ready_k=(lambda k: vdone(b, 0, f"u_lo{k}")) if n == 0 else None)
                        for n in range(2):
                            project("down", n, b * PER + g * MID + (PRE + 4 + 2 * n), 4 * n, False, h_hi, h_lo,
                                    free=lambda j: adone(b, g, f"relu{n}_{j}"),
                                    ready=(lambda c: vdone(b, g, f"h_lo{c}_3")) if n == 0 else None)
                    base = b * PER + (PRE + HG * MID)
                    pe.wait_ge(*vdone(b, 0, "p_lo1"))
                    project("ple", 0, base, 4, False, pT_hi, pT_lo,
                            free=lambda j: vdone(b, HG - 1, f"down_add1_{j}"), chunks=1, ks=2)
                    for k in range(4):
                        turn("xt", k, xr, k)
                    project("ple", 1, base + 1, 4, False, pT_hi, pT_lo,
                            free=lambda j: adone(b, 0, f"e_copy0_{j}"), chunks=1, ks=2)
                    for k in range(4, DK):
                        pe.wait_ge(*vdone(b, 0, f"x2_lo{k - 4}"))
                        turn("xt", k - 4, xr, k)
                    project("gate", 0, base + 2, 0, False, act_hi, act_lo,
                            free=lambda j: vdone(b, 0, f"x2_lo{4 + j}"))
                    project("gate", 1, base + 4, 4, False, act_hi, act_lo,
                            free=lambda j: adone(b, 0, f"e_copy1_{j}"))
                pe.wait_ge(*pdone(BLOCKS - 1, 0, "gate1_3"))
                pe.sem_inc(w_used, 1)

            @block.scalar
            def _(act):
                A = nc.scalar
                act.sem_inc(act_done, AT)
                act.sem_inc(stored, 16)
                act.wait_ge(eps_done, 1)
                tok = lambda a, b: a[bass.ds(b * TBK, TBK), :].rearrange("(j p) d -> p j d", p=P)

                def load_x(b):
                    act.dma_start(xr[:, :, :], tok(x, b)).then_inc(x_in, 16)

                def load_p(b):
                    act.dma_start(pin[:, :, :], tok(p, b)).then_inc(p_in, 16)

                def high_part(n, s, uses):
                    act.wait_ge(raw_in[s], 16 * uses)
                    act.wait_ge(w_used, n + 1)
                    A.activation(w_hi[:, s, :, :], raw[:, s, :, :], ACT.Copy).then_inc(w_hi_done, 1)

                def high(b, c, g=None):
                    n, uses = b * PER + c, b * (PER // 2) + (c // 2 + 1)
                    if g is not None:
                        n, uses = n + g * MID, uses + g * (MID // 2)
                    high_part(n, c % 2, uses)

                high_part(0, 0, 1)
                load_x(0)
                load_p(0)
                act.wait_ge(first_mix_in, 16)
                for h in range(2):
                    A.activation(act_half(h_hi, h), stage_half(h), ACT.Copy).then_inc(first_hi, 1)
                high_part(1, 1, 1)

                def block_of_tokens(b, last):
                    high(b, 2)
                    for k in range(2):
                        act.wait_ge(*pdone(b, 0, f"pt{k}"))
                        A.activation(pT_hi[:, k, :], ps[:, 6 + k, :], ACT.Copy).then_inc(amark(f"p_hi{k}"), 1)
                    if not last:
                        load_p(b + 1)
                    high(b, 3)
                    high(b, 4)
                    for j in range(4):
                        act.wait_ge(*vdone(b, 0, f"out_add1_{j}"))
                        A.activation(junk[:, :], xr[:, j, :], ACT.Square, accum_out=stat[:, 0, j:j + 1]).then_inc(amark(f"ss{j}"), 1)
                        act.wait_ge(*adone(b, 0, f"ss{j}"))
                        A.activation(stat[:, 0, j:j + 1], stat[:, 0, j:j + 1], ACT.Sqrt, scale=1.0 / D,
                                     bias=eps[:, 0:1]).then_inc(amark(f"rms{j}"), 1)
                    for k in range(DK):
                        act.wait_ge(*pdone(b, 0, "ut3"))
                        A.activation(act_hi[:, k, :], ps[:, k, :], ACT.Copy, scale=gain[:, k:k + 1]).then_inc(amark(f"u_hi{k}"), 1)
                    high(b, 5)
                    with act.Fori(0, HG) as g:
                        for n in range(2):
                            high(b, PRE + 2 + 2 * n, g)
                            for j in range(4):
                                act.wait_ge(*pdone(b, g, f"up{n}_{j}"))
                                A.activation(tmp[:, j % 2, :], ps[:, 4 * n + j, :], ACT.Relu).then_inc(amark(f"relu{n}_{j}"), 1)
                                act.wait_ge(*vdone(b, g, f"square{n}_{j}"))
                                A.activation(h_hi[:, 4 * n + j, :], sq[:, j % 2, :], ACT.Copy).then_inc(amark(f"h_hi{n}_{j}"), 1)
                            high(b, PRE + 3 + 2 * n, g)
                        for c in range(6, 10):
                            high(b, PRE + c, g)
                    at = PRE + HG * MID
                    act.wait_ge(stored, 64 * b + 16)
                    for n in range(2):
                        for j in range(4):
                            act.wait_ge(*pdone(b, 0, f"ple{n}_{j}"))
                            A.activation(e[:, j, n * 512:(n + 1) * 512], ps[:, 4 + j, :], ACT.Copy).then_inc(amark(f"e_copy{n}_{j}"), 1)
                        if n == 0:
                            high(b, at + 2)
                        for k in range(4 * n, 4 * n + 4):
                            act.wait_ge(*pdone(b, 0, f"xt{k}"))
                            A.activation(act_hi[:, k, :], ps[:, k % 4, :], ACT.Copy).then_inc(amark(f"x2_hi{k}"), 1)
                    high(b, at + 3)
                    for j in range(4):
                        act.wait_ge(*adone(b, 0, f"ess{j - 1}" if j else "x2_hi7"))
                        A.activation(junk[:, :], e[:, j, :], ACT.Square, accum_out=stat[:, 1, j:j + 1]).then_inc(amark(f"ess{j}"), 1)
                    for j in range(4):
                        act.wait_ge(*adone(b, 0, f"ess{j}"))
                        A.activation(stat[:, 1, j:j + 1], stat[:, 1, j:j + 1], ACT.Sqrt, scale=1.0 / D,
                                     bias=eps[:, 0:1]).then_inc(amark(f"erms{j}"), 1)
                    high(b, at + 4)
                    act.wait_ge(mix_in, 16 * (b + 1))
                    for h in range(2):
                        A.activation(act_half(h_hi, h), stage_half(h), ACT.Copy).then_inc(amark(f"mix_hi{h}"), 1)
                    for n in range(2):
                        for j in range(4):
                            act.wait_ge(*pdone(b, 0, f"gate{n}_{j}"))
                            if n or j >= 2:
                                act.wait_ge(*vdone(b, 0, f"gmul{n if j >= 2 else n - 1}_{(j + 2) % 4}"))
                            A.activation(tmp[:, j % 2, :], ps[:, 4 * n + j, :], ACT.Sigmoid).then_inc(amark(f"sig{n}_{j}"), 1)
                        if n == 0:
                            high(b, at + 5)
                            high(b, at + 6)
                    high(b, at + 7)
                    for j in range(4):
                        act.wait_ge(*vdone(b, 0, f"x_add1_{j}"))
                        act.wait_ge(*adone(b, 0, f"fss{j - 1}" if j else "ess3"))
                        A.activation(junk[:, :], xr[:, j, :], ACT.Square, accum_out=stat[:, 2, j:j + 1]).then_inc(amark(f"fss{j}"), 1)
                    for j in range(4):
                        act.wait_ge(*adone(b, 0, f"fss{j}"))
                        A.activation(stat[:, 2, j:j + 1], stat[:, 2, j:j + 1], ACT.Sqrt, scale=1.0 / D,
                                     bias=eps[:, 0:1]).then_inc(amark(f"frms{j}"), 1)
                    for j in range(4):
                        act.wait_ge(*vdone(b, 0, f"fout{j}"))
                        act.dma_start(out[bass.ds(b * TBK + j * P, P), :], e[:, j, :]).then_inc(stored, 16)
                    if not last:
                        load_x(b + 1)

                with act.Fori(0, BLOCKS - 1) as b:
                    block_of_tokens(b, last=False)
                block_of_tokens(BLOCKS - 1, last=True)
                act.wait_ge(stored, 64 * BLOCKS + 16)

            @block.vector
            def _(dve):
                V = nc.vector
                tail = len(DVE_L[2]) - DVE_L[2].index("mix_lo0")
                dve.sem_inc(dve_done, VT - tail)
                V.memset(eps[:, :], NORM_EPS).then_inc(eps_done, 1)
                for h in range(2):
                    dve.wait_ge(first_hi, h + 1)
                    V.tensor_tensor(act_half(h_lo, h), stage_half(h), act_half(h_hi, h).bitcast(F32),
                                    ALU.subtract).then_inc(dve_done, 1)
                dve.wait_ge(const_in, 32)
                dve.wait_ge(gains_in, 32)
                dve.wait_ge(dve_done, VT - tail + 2)
                dve.sem_inc(dve_done, tail - 2)
                with dve.Fori(0, BLOCKS) as b:
                    dve.wait_ge(x_in, 16 * (b + 1))
                    def add_out(n, j):
                        cols = slice(n * 512, (n + 1) * 512)
                        dve.wait_ge(*pdone(b, 0, f"out{n}_{j}"))
                        V.tensor_tensor(xr[:, j, cols], ps[:, 4 * n + j, :], xr[:, j, cols], ALU.add).then_inc(vmark(f"out_add{n}_{j}"), 1)

                    def normalise(j):
                        dve.wait_ge(*adone(b, 0, f"rms{j}"))
                        V.reciprocal(stat[:, 0, j:j + 1], stat[:, 0, j:j + 1]).then_inc(vmark(f"inv{j}"), 1)
                        dve.wait_ge(*vdone(b, 0, f"inv{j}"))
                        V.tensor_scalar(stage[:, j, :], xr[:, j, :], stat[:, 0, j:j + 1], None, ALU.mult).then_inc(vmark(f"xn{j}"), 1)

                    for j in range(4):
                        add_out(0, j)
                    for k in range(2):
                        dve.wait_ge(*adone(b, 0, f"p_hi{k}"))
                        V.tensor_tensor(pT_lo[:, k, :], ps[:, 6 + k, :], pT_hi[:, k, :].bitcast(F32), ALU.subtract).then_inc(vmark(f"p_lo{k}"), 1)
                    add_out(1, 0)
                    for j in range(1, 4):
                        add_out(1, j)
                        normalise(j - 1)
                    normalise(3)
                    for k in range(DK):
                        dve.wait_ge(*adone(b, 0, f"u_hi{k}"))
                        V.scalar_tensor_tensor(act_lo[:, k, :], ps[:, k, :], gain[:, k:k + 1], act_hi[:, k, :].bitcast(F32),
                                               ALU.mult, ALU.subtract).then_inc(vmark(f"u_lo{k}"), 1)
                    with dve.Fori(0, HG) as g:
                        for n, j in NJ:
                            dve.wait_ge(*adone(b, g, f"relu{n}_{j}"))
                            V.tensor_tensor(sq[:, j % 2, :], tmp[:, j % 2, :], tmp[:, j % 2, :], ALU.mult).then_inc(vmark(f"square{n}_{j}"), 1)
                            dve.wait_ge(*adone(b, g, f"h_hi{n}_{j}"))
                            V.tensor_tensor(h_lo[:, 4 * n + j, :], sq[:, j % 2, :], h_hi[:, 4 * n + j, :].bitcast(F32),
                                            ALU.subtract).then_inc(vmark(f"h_lo{n}_{j}"), 1)
                        for n, j in NJ:
                            dve.wait_ge(*pdone(b, g, f"down{n}_{j}"))
                            V.tensor_tensor(xr[:, j, n * 512:(n + 1) * 512], ps[:, 4 * n + j, :], xr[:, j, n * 512:(n + 1) * 512],
                                            ALU.add).then_inc(vmark(f"down_add{n}_{j}"), 1)
                    for k in range(DK):
                        dve.wait_ge(*adone(b, 0, f"x2_hi{k}"))
                        V.tensor_tensor(act_lo[:, k, :], ps[:, k % 4, :], act_hi[:, k, :].bitcast(F32), ALU.subtract).then_inc(vmark(f"x2_lo{k}"), 1)
                    for j in range(4):
                        dve.wait_ge(*adone(b, 0, f"erms{j}"))
                        V.reciprocal(stat[:, 1, j:j + 1], stat[:, 1, j:j + 1]).then_inc(vmark(f"einv{j}"), 1)
                        dve.wait_ge(*vdone(b, 0, f"einv{j}"))
                        V.scalar_tensor_tensor(e[:, j, :], e[:, j, :], stat[:, 1, j:j + 1], pleg[:, :], ALU.mult,
                                               ALU.mult).then_inc(vmark(f"e_norm{j}"), 1)
                    for h in range(2):
                        dve.wait_ge(*adone(b, 0, f"mix_hi{h}"))
                        V.tensor_tensor(act_half(h_lo, h), stage_half(h), act_half(h_hi, h).bitcast(F32),
                                        ALU.subtract).then_inc(vmark(f"mix_lo{h}"), 1)
                    for n, j in NJ:
                        cols = slice(n * 512, (n + 1) * 512)
                        dve.wait_ge(*adone(b, 0, f"sig{n}_{j}"))
                        dve.wait_ge(*vdone(b, 0, f"e_norm{j}"))
                        V.tensor_tensor(e[:, j, cols], tmp[:, j % 2, :], e[:, j, cols], ALU.mult).then_inc(vmark(f"gmul{n}_{j}"), 1)
                        dve.wait_ge(*vdone(b, 0, f"gmul{n}_{j}"))
                        V.tensor_tensor(xr[:, j, cols], e[:, j, cols], xr[:, j, cols], ALU.add).then_inc(vmark(f"x_add{n}_{j}"), 1)
                    for j in range(4):
                        dve.wait_ge(*adone(b, 0, f"frms{j}"))
                        V.reciprocal(stat[:, 2, j:j + 1], stat[:, 2, j:j + 1]).then_inc(vmark(f"finv{j}"), 1)
                        dve.wait_ge(*vdone(b, 0, f"finv{j}"))
                        V.scalar_tensor_tensor(e[:, j, :], xr[:, j, :], stat[:, 2, j:j + 1], fing[:, :], ALU.mult,
                                               ALU.mult).then_inc(vmark(f"fout{j}"), 1)


def pack(inputs):
    f = lambda n: np.ascontiguousarray(inputs[n])
    per_feature = lambda a: np.asarray(a).reshape(-1, P).T
    q = np.arange(RW).reshape(2, PAIRS, HD).transpose(1, 0, 2).reshape(-1)
    cols = np.concatenate([np.arange(RWT * P), RWT * P + q, np.arange((RWT + PAIRS) * P, ZT * P)])
    rows = np.concatenate([np.arange(RW), RW + q])
    chunks = lambda w, n, c, k: np.asarray(w).reshape(c, k, P, n, -1).transpose(3, 0, 2, 1, 4).reshape(n * c, P, k, -1)
    up = f("w_ff_up")[0]
    down = f("w_ff_down")[0]
    a = {
        "x": f("x")[0], "p": f("p")[0, 0],
        "params": np.concatenate([per_feature(inputs[n]) for n in
                                  ("norm_mix_g", "norm_mlp_g", "mu_shift", "w0", "a0", "k_k", "k_a", "r_k")], 1),
        "consts": shape_constants(), "hrows": head_rows(), "onehot": bucket_onehot(),
        "rel_bias": f("rel_bias"), "sinks": f("sinks"),
        "w_lora": f("w_up")[0], "a_lora": f("a_up")[0], "g_lora": f("g_up")[0],
        "lnx_g": f("lnx_g"), "lnx_b": f("lnx_b"),
        "ple_g": f("ple_norm_g"), "final_g": f("final_norm_g").reshape(1, D),
        "w_in": chunks(f("w_in")[0][:, cols], ZT // 2, 1, DK),
        "w_out": chunks(f("w_out")[0][rows], 2, 2, 4),
        "w_ff_up": chunks(up, 2 * HG, 2, 4),
        "w_ff_down": np.concatenate([chunks(down[g * HGD:(g + 1) * HGD], 2, 2, 4) for g in range(HG)], 0),
        "w_ple": chunks(f("ple_proj")[0], 2, 1, 2),
        "w_gate": chunks(f("ple_gate")[0], 2, 2, 4),
    }
    return {k: np.ascontiguousarray(v) for k, v in a.items()}


def build(nc, t, out):
    zT = nc.dram_tensor("zT", [ZT, P, PADC + SEQ], F32, kind="Internal")
    mixT = nc.dram_tensor("mixT", [2 * PAIRS, P, SEQ], F32, kind="Internal")
    skew = nc.dram_tensor("skew", [HEADS * P * EXT + P], F32, kind="Internal")
    norm_and_project(nc, t["x"], t["w_in"], t["params"], t["consts"], zT, t["onehot"], t["rel_bias"], skew)
    with ExitStack() as ctx:
        first_block = (ctx.enter_context(nc.sbuf_tensor("wraw_f", [P, 2, 4, 512], F32)),
                       ctx.enter_context(nc.sbuf_tensor("stage_f", [P, 4, D], F32)),
                       [ctx.enter_context(nc.semaphore(f"raw_in{s}_f")) for s in range(2)],
                       ctx.enter_context(nc.semaphore("first_mix_in_f")))
        mix_tokens(nc, zT, mixT, t["params"], t["consts"], t["hrows"], t["sinks"],
                   t["w_lora"], t["a_lora"], t["g_lora"], t["lnx_g"], t["lnx_b"], skew, t["w_out"], first_block)
        finish_layer(nc, t["x"], t["p"], mixT, out, t["params"], t["consts"], t["ple_g"], t["final_g"],
                     t["w_out"], t["w_ff_up"], t["w_ff_down"], t["w_ple"], t["w_gate"], first_block)


def kernel(**inputs):
    import concourse.bacc as bacc
    from concourse.bass_utils import run_bass_kernel_spmd

    nc = bacc.Bacc("TRN2", target_bir_lowering=False, num_devices=1)
    arrays = {f"in_{k}": v for k, v in pack(inputs).items()}
    t = {k[3:]: nc.dram_tensor(k, v.shape, mybir.dt.from_np(v.dtype), kind="ExternalInput").ap() for k, v in arrays.items()}
    out = nc.dram_tensor("out_y", (SEQ, D), F32, kind="ExternalOutput").ap()
    build(nc, t, out)
    r = run_bass_kernel_spmd(nc, [arrays], core_ids=[0])
    return np.asarray(r.results[0]["out_y"]).reshape(1, SEQ, D)
```
